# Optimizing a Trainium2 kernel written in Bass

```python
import jax, jax.numpy as jnp
from jax import lax
import numpy as np
import math
import jax
import jax.numpy as jnp

D_MODEL = 2048
BATCH = 1
SEQ = 256
DEPTH = 2

GRID_W = 64
CTX_LEN = 256
D_MIX = D_MODEL
SGU_WIDTH = D_MIX // 2
SGU_GROUPS = 8
SGU_GROUP_DIM = SGU_WIDTH // SGU_GROUPS
CHUNK = 128
ATTN_WIDTH = D_MIX - SGU_WIDTH
HEAD_DIM = 128
N_Q_HEADS = ATTN_WIDTH // HEAD_DIM
N_KV_HEADS = 2
KV_WIDTH = N_KV_HEADS * HEAD_DIM
Q_BLOCK = 128
ROPE_THETA = 10000.0
EPS = 1e-6
SPLIT_POINTS = (
    SGU_WIDTH,
    2 * SGU_WIDTH,
    3 * SGU_WIDTH,
    3 * SGU_WIDTH + ATTN_WIDTH,
    3 * SGU_WIDTH + ATTN_WIDTH + KV_WIDTH,
    3 * SGU_WIDTH + ATTN_WIDTH + 2 * KV_WIDTH,
)
KV_START = SPLIT_POINTS[3]
KV_END = SPLIT_POINTS[5]
D_IN = SPLIT_POINTS[5] + ATTN_WIDTH


def rms_norm(x, w):
    xf = x.astype(jnp.float32)
    y = xf * lax.rsqrt(jnp.mean(xf * xf, axis=-1, keepdims=True) + EPS)
    return (y * w.astype(jnp.float32)).astype(x.dtype)

def modulation(cond, w_mod, b_mod):
    m = jax.nn.silu(cond) @ w_mod + b_mod
    m = m.reshape(-1, 1, 3 * D_MODEL)
    return jnp.split(m, 3, axis=-1)

def axial_rope_tables(n_tokens, dtype):
    rows = n_tokens // GRID_W
    row_id = jnp.broadcast_to(jnp.arange(rows)[:, None], (rows, GRID_W)).reshape(-1)
    col_id = jnp.broadcast_to(jnp.arange(GRID_W)[None, :], (rows, GRID_W)).reshape(-1)
    axis_dim = HEAD_DIM // 2
    inv_freq = ROPE_THETA ** (-jnp.arange(0, axis_dim, 2, dtype=jnp.float32) / axis_dim)
    ang_r = row_id.astype(jnp.float32)[:, None] * inv_freq[None, :]
    ang_c = col_id.astype(jnp.float32)[:, None] * inv_freq[None, :]
    ang = jnp.concatenate([ang_r, ang_r, ang_c, ang_c], axis=-1)
    return jnp.cos(ang).astype(dtype), jnp.sin(ang).astype(dtype)

def _rotate_half(t):
    t1, t2 = jnp.split(t, 2, axis=-1)
    return jnp.concatenate([-t2, t1], axis=-1)

def apply_axial_rope(x, cos, sin):
    x_r, x_c = jnp.split(x, 2, axis=-1)
    rot = jnp.concatenate([_rotate_half(x_r), _rotate_half(x_c)], axis=-1)
    return x * cos + rot * sin

def split_heads(t, n_heads):
    b, n, _ = t.shape
    return t.reshape(b, n, n_heads, HEAD_DIM).transpose(0, 2, 1, 3)

def merge_heads(t):
    b, h, n, d = t.shape
    return t.transpose(0, 2, 1, 3).reshape(b, n, h * d)

def kv_heads(k, v, k_norm_w):
    return rms_norm(split_heads(k, N_KV_HEADS), k_norm_w), split_heads(v, N_KV_HEADS)

def blocked_gqa(q, k, v):
    b, hq, nq, d = q.shape
    rep = hq // N_KV_HEADS
    qb = q.reshape(b, N_KV_HEADS, rep, nq // Q_BLOCK, Q_BLOCK, d)
    qb = jnp.moveaxis(qb, 3, 0)
    scale = HEAD_DIM ** -0.5

    def one_block(q_blk):
        s = jnp.einsum('bgrqd,bgkd->bgrqk', q_blk, k, preferred_element_type=jnp.float32) * scale
        p = jax.nn.softmax(s, axis=-1).astype(v.dtype)
        return jnp.einsum('bgrqk,bgkd->bgrqd', p, v)

    o = lax.map(one_block, qb)
    return jnp.moveaxis(o, 0, 3).reshape(b, hq, nq, d)

def chunk_sgu(u, v, w_sgu, b_sgu, v_norm_w):
    b, n, _ = u.shape
    u = jax.nn.gelu(u)
    v = jax.nn.gelu(v).reshape(b, n // CHUNK, CHUNK, SGU_GROUPS, SGU_GROUP_DIM)
    v = rms_norm(v, v_norm_w)
    s = jnp.einsum('gpq,bcqgd->bcpgd', w_sgu, v) + b_sgu.T[:, :, None]
    return u * s.reshape(b, n, SGU_WIDTH)

def first_inputs(seed: int = 0) -> dict:
    key = jax.random.key(seed)
    ks = jax.random.split(key, 16)
    f32 = jnp.float32
    nrm = lambda k, shape: jax.random.normal(k, shape, f32)
    return {
        "x": nrm(ks[0], (BATCH, SEQ, D_MODEL)),
        "c": nrm(ks[1], (BATCH, D_MODEL)),
        "ctx": nrm(ks[2], (BATCH, CTX_LEN, D_MODEL)),
        "c_ctx": nrm(ks[3], (D_MODEL,)),
        "norm_w": 1.0 + 0.02 * nrm(ks[4], (DEPTH, D_MODEL)),
        "w_mod": 0.5 * D_MODEL ** -0.5 * nrm(ks[5], (DEPTH, D_MODEL, 3 * D_MODEL)),
        "b_mod": 0.01 * nrm(ks[6], (DEPTH, 3 * D_MODEL)),
        "w_in": D_MODEL ** -0.5 * nrm(ks[7], (DEPTH, D_MODEL, D_IN)),
        "w_sgu": CHUNK ** -0.5 * nrm(ks[8], (DEPTH, SGU_GROUPS, CHUNK, CHUNK)),
        "b_sgu": 1.0 + 0.02 * nrm(ks[9], (DEPTH, SGU_GROUPS, CHUNK)),
        "v_norm_w": 1.0 + 0.02 * nrm(ks[10], (DEPTH, SGU_GROUPS, SGU_GROUP_DIM)),
        "q_norm_w": 1.0 + 0.02 * nrm(ks[11], (DEPTH, HEAD_DIM)),
        "k_norm_w": 1.0 + 0.02 * nrm(ks[12], (DEPTH, HEAD_DIM)),
        "w_out": D_MIX ** -0.5 * nrm(ks[13], (DEPTH, D_MIX, D_MODEL)),
    }

def first_block(x, c, ctx, c_ctx, norm_w, w_mod, b_mod, w_in, w_sgu, b_sgu, v_norm_w,
              q_norm_w, k_norm_w, w_out):
    n_lat = x.shape[1]
    cos, sin = axial_rope_tables(n_lat, x.dtype)
    xc = ctx
    for layer in range(DEPTH):
        last = layer == DEPTH - 1
        shift, scale, gate = modulation(c, w_mod[layer], b_mod[layer])
        shift_c, scale_c, gate_c = modulation(c_ctx, w_mod[layer], b_mod[layer])
        h = rms_norm(x, norm_w[layer]) * (1.0 + scale) + shift
        hc = rms_norm(xc, norm_w[layer]) * (1.0 + scale_c) + shift_c

        if last:
            proj_kv_c = hc @ w_in[layer][:, KV_START:KV_END]
            k_c, v_c = jnp.split(proj_kv_c, 2, axis=-1)
            kc, vc = kv_heads(k_c, v_c, k_norm_w[layer])
        else:
            proj_c = hc @ w_in[layer]
            u_c, v_c_sgu, za_c, q_c, k_c, v_c, zb_c = jnp.split(proj_c, SPLIT_POINTS, axis=-1)
            kc, vc = kv_heads(k_c, v_c, k_norm_w[layer])
            qc = rms_norm(split_heads(q_c, N_Q_HEADS), q_norm_w[layer])
            attn_c = blocked_gqa(qc, kc, vc)
            sgu_c = chunk_sgu(u_c, v_c_sgu, w_sgu[layer], b_sgu[layer], v_norm_w[layer])
            y_c = jnp.concatenate([sgu_c * jax.nn.silu(za_c),
                                   merge_heads(attn_c) * jax.nn.silu(zb_c)], axis=-1) @ w_out[layer]

        proj = h @ w_in[layer]
        u, v_sgu, za, q, k, v, zb = jnp.split(proj, SPLIT_POINTS, axis=-1)
        q = apply_axial_rope(rms_norm(split_heads(q, N_Q_HEADS), q_norm_w[layer]), cos, sin)
        k, v = kv_heads(k, v, k_norm_w[layer])
        k = apply_axial_rope(k, cos, sin)
        k_all = jnp.concatenate([kc, k], axis=2)
        v_all = jnp.concatenate([vc, v], axis=2)
        attn = blocked_gqa(q, k_all, v_all)
        sgu = chunk_sgu(u, v_sgu, w_sgu[layer], b_sgu[layer], v_norm_w[layer])
        y = jnp.concatenate([sgu * jax.nn.silu(za),
                             merge_heads(attn) * jax.nn.silu(zb)], axis=-1) @ w_out[layer]
        x = x + gate * y
        if not last:
            xc = xc + gate_c * y_c
    return x


CHUNK_2 = 64
N_EVEN = (DEPTH + 1) // 2
N_ODD = DEPTH // 2
ROPE_THETA_2 = 500000.0
NORM_EPS = 1e-5

A_HEADS = 8
A_HEAD_DIM = 128
A_ROPE_DIM = A_HEAD_DIM // 4
A_NOPE_DIM = A_HEAD_DIM - A_ROPE_DIM
A_V_DIM = 128
A_WIDTH = A_HEADS * A_V_DIM
A_Q_RANK = 512
A_KV_RANK = 256
IDX_HEADS = 16
IDX_DIM = 64
IDX_ROPE_DIM = IDX_DIM // 4
TOPK_MAX = 256

B_HEAD = 64
B_WIDTH = D_MODEL // 2
B_HEADS = B_WIDTH // B_HEAD
B_DECAY_LORA = 64
B_A_LORA = 64
B_GATE_LORA = 160
B_LN_EPS = 64e-5

C_WIDTH = D_MODEL
C_GROUP = 16
C_GROUPS = C_WIDTH // C_GROUP
C_STATE = 64

MEM_LEN = 256
X_HEADS = 4
X_HEAD_DIM = 128

FFN_DIM = 4 * D_MODEL

A_COLS = A_Q_RANK + A_KV_RANK + A_ROPE_DIM + IDX_DIM + IDX_HEADS
B_COLS = 3 * B_WIDTH + B_DECAY_LORA + B_A_LORA + B_GATE_LORA
EVEN_COLS = A_COLS + B_COLS


def rms_norm_2(x, g):
    xf = x.astype(jnp.float32)
    y = xf * lax.rsqrt(jnp.mean(xf * xf, axis=-1, keepdims=True) + NORM_EPS)
    return (y * g.astype(jnp.float32)).astype(x.dtype)

def split_cols(t, sizes):
    offs = np.cumsum(sizes)[:-1].tolist()
    return jnp.split(t, offs, axis=-1)

def rope_tables(pos, rot_dim):
    inv_freq = ROPE_THETA_2 ** (-jnp.arange(0, rot_dim, 2, dtype=jnp.float32) / rot_dim)
    ang = pos[..., None] * inv_freq
    return jnp.cos(ang), jnp.sin(ang)

def apply_partial_rope(x, cos, sin, rot_dim):
    xf = x.astype(jnp.float32)
    half = rot_dim // 2
    x1, x2, rest = xf[..., :half], xf[..., half:rot_dim], xf[..., rot_dim:]
    out = jnp.concatenate([x1 * cos - x2 * sin, x2 * cos + x1 * sin, rest], axis=-1)
    return out.astype(x.dtype)

def token_shift(t):
    return jnp.pad(t[:, :-1], ((0, 0), (1, 0), (0, 0)))

def dsa_mixer(h, cos_a, sin_a, cos_i, sin_i, cq_norm, ckv_norm, kidx_norm, w_uq, w_uk, w_uv, w_qidx):
    f32 = jnp.float32
    bsz, seq, _ = h.shape
    c_q, c_kv, k_rope, k_idx, w_idx = split_cols(h, [A_Q_RANK, A_KV_RANK, A_ROPE_DIM, IDX_DIM, IDX_HEADS])
    c_q = rms_norm_2(c_q, cq_norm)
    c_kv = rms_norm_2(c_kv, ckv_norm)
    k_rope = apply_partial_rope(k_rope, cos_a, sin_a, A_ROPE_DIM)
    q = jnp.einsum('bsr,rhd->bshd', c_q, w_uq)
    q_rope = apply_partial_rope(q[..., :A_ROPE_DIM], cos_a[:, :, None], sin_a[:, :, None], A_ROPE_DIM)
    q_lat = jnp.einsum('bshd,rhd->bshr', q[..., A_ROPE_DIM:], w_uk)
    q_idx = apply_partial_rope(jnp.einsum('bsr,rhd->bshd', c_q, w_qidx), cos_i[:, :, None], sin_i[:, :, None], IDX_ROPE_DIM)
    k_idx = apply_partial_rope(rms_norm_2(k_idx, kidx_norm), cos_i, sin_i, IDX_ROPE_DIM)
    w_idx = w_idx.astype(f32) * (IDX_HEADS ** -0.5) * (IDX_DIM ** -0.5)

    topk = min(TOPK_MAX, seq // 4)
    n_blk = seq // Q_BLOCK
    scale = A_HEAD_DIM ** -0.5
    key_pos = jnp.arange(seq, dtype=jnp.int32)
    gather = jax.vmap(lambda table, idx: table[idx])

    def to_blocks(t):
        return t.reshape((bsz, n_blk, Q_BLOCK) + t.shape[2:]).swapaxes(0, 1)

    def attend_block(args):
        ql, qr, qi, wi, t0 = args
        q_pos = t0 + jnp.arange(Q_BLOCK, dtype=jnp.int32)
        limit = (q_pos // CHUNK_2 + 1) * CHUNK_2
        allowed = key_pos[None, :] < limit[:, None]
        logits = jnp.einsum('bqhd,bsd->bqhs', qi.astype(f32), k_idx.astype(f32))
        score = jnp.einsum('bqh,bqhs->bqs', wi, jax.nn.relu(logits))
        score = jnp.where(allowed[None], score, -jnp.inf)
        _, sel = lax.top_k(score, topk)
        valid = sel < limit[None, :, None]
        ckv_sel = gather(c_kv, sel)
        kr_sel = gather(k_rope, sel)
        s = (jnp.einsum('bqhr,bqkr->bqhk', ql, ckv_sel).astype(f32)
             + jnp.einsum('bqhd,bqkd->bqhk', qr, kr_sel).astype(f32)) * scale
        s = jnp.where(valid[:, :, None, :], s, -jnp.inf)
        p = jax.nn.softmax(s, axis=-1).astype(ckv_sel.dtype)
        return jnp.einsum('bqhk,bqkr->bqhr', p, ckv_sel)

    blk_start = jnp.arange(n_blk, dtype=jnp.int32) * Q_BLOCK
    o_lat = lax.map(attend_block, (to_blocks(q_lat), to_blocks(q_rope), to_blocks(q_idx), to_blocks(w_idx), blk_start))
    o_lat = o_lat.swapaxes(0, 1).reshape(bsz, seq, A_HEADS, A_KV_RANK)
    return jnp.einsum('bshr,rhd->bshd', o_lat, w_uv).reshape(bsz, seq, A_WIDTH)

def rwkv7_mixer(h, mu, w0, w2, a0, a2, g2, k_k, k_a, r_k, ln_w, ln_b):
    f32 = jnp.float32
    bsz, seq, _ = h.shape
    hm = h + (token_shift(h) - h) * mu
    r, k, v, wl, al, gl = split_cols(hm, [B_WIDTH, B_WIDTH, B_WIDTH, B_DECAY_LORA, B_A_LORA, B_GATE_LORA])
    log_w = -jax.nn.softplus(-(w0 + jnp.tanh(wl) @ w2).astype(f32)) - 0.5
    decay = jnp.exp(-jnp.exp(log_w))
    a = jax.nn.sigmoid((a0 + al @ a2).astype(f32))
    g = (jax.nn.sigmoid(gl) @ g2).astype(f32)

    def heads(t):
        return t.reshape(bsz, seq, B_HEADS, B_HEAD)

    r, k, v = heads(r.astype(f32)), heads(k.astype(f32)), heads(v.astype(f32))
    decay, a = heads(decay), heads(a)
    kk = k * k_k.astype(f32).reshape(B_HEADS, B_HEAD)
    kk = kk * lax.rsqrt(jnp.maximum(jnp.sum(kk * kk, axis=-1, keepdims=True), 1e-24))
    k = k * (1.0 + (a - 1.0) * k_a.astype(f32).reshape(B_HEADS, B_HEAD))

    def step(state, inp):
        r_t, w_t, k_t, v_t, kk_t, a_t = inp
        sa = jnp.einsum('bhvk,bhk->bhv', state, -kk_t)
        state = (state * w_t[:, :, None, :] + sa[..., None] * (kk_t * a_t)[:, :, None, :]
                 + v_t[..., None] * k_t[:, :, None, :])
        return state, jnp.einsum('bhvk,bhk->bhv', state, r_t)

    tm = lambda t: jnp.moveaxis(t, 1, 0)
    state0 = jnp.zeros((bsz, B_HEADS, B_HEAD, B_HEAD), f32)
    _, out = lax.scan(step, state0, (tm(r), tm(decay), tm(k), tm(v), tm(kk), tm(a)))
    out = jnp.moveaxis(out, 0, 1)
    mean = jnp.mean(out, axis=-1, keepdims=True)
    var = jnp.mean(jnp.square(out - mean), axis=-1, keepdims=True)
    out = ((out - mean) * lax.rsqrt(var + B_LN_EPS)).reshape(bsz, seq, B_WIDTH)
    out = out * ln_w.astype(f32) + ln_b.astype(f32)
    bonus = jnp.sum(r * k * r_k.astype(f32), axis=-1, keepdims=True) * v
    out = (out + bonus.reshape(bsz, seq, B_WIDTH)) * g
    return out.astype(h.dtype)

def s5_mixer(u, lam_re, lam_im, log_dt, b_re, b_im, c_re, c_im, d_skip, w_glu, b_glu):
    f32 = jnp.float32
    bsz, seq, _ = u.shape
    lam = lax.complex(jnp.minimum(lam_re.astype(f32), -1e-4), lam_im.astype(f32))
    dt = jnp.exp(log_dt.astype(f32))[:, None]
    lam_bar = jnp.exp(lam * dt)
    b_bar = ((lam_bar - 1.0) / lam)[..., None] * lax.complex(b_re.astype(f32), b_im.astype(f32))
    c_mat = lax.complex(c_re.astype(f32), c_im.astype(f32))
    n_chunk = seq // CHUNK_2
    uf = u.astype(f32)
    u_chunks = jnp.moveaxis(uf.reshape(bsz, n_chunk, CHUNK_2, C_GROUPS, C_GROUP), 1, 0)
    a_elem = jnp.broadcast_to(lam_bar, (bsz, CHUNK_2, C_GROUPS, C_STATE))

    def combine(e1, e2):
        a1, x1 = e1
        a2, x2 = e2
        return a1 * a2, a2 * x1 + x2

    def chunk_step(state, u_c):
        bu = jnp.einsum('bcgi,gpi->bcgp', u_c.astype(jnp.complex64), b_bar)
        bu = bu.at[:, 0].add(lam_bar * state)
        _, states = lax.associative_scan(combine, (a_elem, bu), axis=1)
        y = jnp.einsum('bcgp,gip->bcgi', states, c_mat).real
        return states[:, -1], y

    state0 = jnp.zeros((bsz, C_GROUPS, C_STATE), jnp.complex64)
    _, y = lax.scan(chunk_step, state0, u_chunks)
    y = jnp.moveaxis(y, 0, 1).reshape(bsz, seq, C_WIDTH) + d_skip.astype(f32) * uf
    z = jax.nn.gelu(y)
    out = z * jax.nn.sigmoid(z @ w_glu.astype(f32) + b_glu.astype(f32))
    return out.astype(u.dtype)

def memory_cross_attention(xn, memn, wq, wkv, wo):
    f32 = jnp.float32
    bsz, seq, _ = xn.shape
    q = (xn @ wq).reshape(bsz, seq, X_HEADS, X_HEAD_DIM)
    kv = (memn @ wkv).reshape(bsz, memn.shape[1], 2, X_HEADS, X_HEAD_DIM)
    s = jnp.einsum('bshd,bmhd->bshm', q, kv[:, :, 0]).astype(f32) * (X_HEAD_DIM ** -0.5)
    p = jax.nn.softmax(s, axis=-1).astype(xn.dtype)
    o = jnp.einsum('bshm,bmhd->bshd', p, kv[:, :, 1]).reshape(bsz, seq, X_HEADS * X_HEAD_DIM)
    return o @ wo

def squared_relu_mlp(xn, w_up, w_down):
    return jnp.square(jax.nn.relu(xn @ w_up)) @ w_down

def second_inputs(seed: int = 0) -> dict:
    key = jax.random.key(seed)
    ks = iter(jax.random.split(key, 64))
    f32 = jnp.float32

    def nrm(shape, scale):
        return scale * jax.random.normal(next(ks), shape, f32)

    def gain(shape):
        return 1.0 + 0.02 * jax.random.normal(next(ks), shape, f32)

    ramp = (jnp.arange(B_WIDTH, dtype=f32) / (B_WIDTH - 1)) ** 0.85
    inp = {}
    inp['x'] = nrm((BATCH, SEQ, D_MODEL), 1.0)
    inp['mem'] = nrm((BATCH, MEM_LEN, D_MODEL), 1.0)
    inp['start_frame'] = jax.random.randint(next(ks), (BATCH,), 0, 256, dtype=jnp.int32) * CHUNK_2
    inp['norm_mix'] = gain((DEPTH, D_MODEL))
    inp['norm_xattn'] = gain((DEPTH, D_MODEL))
    inp['norm_mem'] = gain((DEPTH, D_MODEL))
    inp['norm_ffn'] = gain((DEPTH, D_MODEL))
    inp['final_norm'] = gain((D_MODEL,))
    inp['xattn_wq'] = nrm((DEPTH, D_MODEL, X_HEADS * X_HEAD_DIM), D_MODEL ** -0.5)
    inp['xattn_wkv'] = nrm((DEPTH, D_MODEL, 2 * X_HEADS * X_HEAD_DIM), D_MODEL ** -0.5)
    inp['xattn_wo'] = nrm((DEPTH, X_HEADS * X_HEAD_DIM, D_MODEL), (X_HEADS * X_HEAD_DIM) ** -0.5)
    inp['ffn_up'] = nrm((DEPTH, D_MODEL, FFN_DIM), D_MODEL ** -0.5)
    inp['ffn_down'] = nrm((DEPTH, FFN_DIM, D_MODEL), FFN_DIM ** -0.5)
    inp['even_w_in'] = nrm((N_EVEN, D_MODEL, EVEN_COLS), D_MODEL ** -0.5)
    inp['even_w_out'] = nrm((N_EVEN, A_WIDTH + B_WIDTH, D_MODEL), (A_WIDTH + B_WIDTH) ** -0.5)
    inp['dsa_cq_norm'] = gain((N_EVEN, A_Q_RANK))
    inp['dsa_ckv_norm'] = gain((N_EVEN, A_KV_RANK))
    inp['dsa_kidx_norm'] = gain((N_EVEN, IDX_DIM))
    inp['dsa_w_uq'] = nrm((N_EVEN, A_Q_RANK, A_HEADS, A_HEAD_DIM), A_Q_RANK ** -0.5)
    inp['dsa_w_uk'] = nrm((N_EVEN, A_KV_RANK, A_HEADS, A_NOPE_DIM), A_KV_RANK ** -0.5)
    inp['dsa_w_uv'] = nrm((N_EVEN, A_KV_RANK, A_HEADS, A_V_DIM), A_KV_RANK ** -0.5)
    inp['dsa_w_qidx'] = nrm((N_EVEN, A_Q_RANK, IDX_HEADS, IDX_DIM), A_Q_RANK ** -0.5)
    inp['rwkv_mu'] = jax.random.uniform(next(ks), (N_EVEN, B_COLS), f32)
    inp['rwkv_w0'] = -6.0 + 5.0 * ramp + nrm((N_EVEN, B_WIDTH), 0.1)
    inp['rwkv_w2'] = nrm((N_EVEN, B_DECAY_LORA, B_WIDTH), 0.5 * B_DECAY_LORA ** -0.5)
    inp['rwkv_a0'] = nrm((N_EVEN, B_WIDTH), 0.1)
    inp['rwkv_a2'] = nrm((N_EVEN, B_A_LORA, B_WIDTH), B_A_LORA ** -0.5)
    inp['rwkv_g2'] = nrm((N_EVEN, B_GATE_LORA, B_WIDTH), B_GATE_LORA ** -0.5)
    inp['rwkv_k_k'] = 0.85 + nrm((N_EVEN, B_WIDTH), 0.02)
    inp['rwkv_k_a'] = gain((N_EVEN, B_WIDTH))
    inp['rwkv_r_k'] = -0.04 + nrm((N_EVEN, B_HEADS, B_HEAD), 0.1)
    inp['rwkv_ln_w'] = gain((N_EVEN, B_WIDTH))
    inp['rwkv_ln_b'] = nrm((N_EVEN, B_WIDTH), 0.02)
    inp['odd_w_in'] = nrm((N_ODD, D_MODEL, C_WIDTH), D_MODEL ** -0.5)
    inp['odd_w_out'] = nrm((N_ODD, C_WIDTH, D_MODEL), C_WIDTH ** -0.5)
    inp['s5_lam_re'] = -0.5 + nrm((N_ODD, C_GROUPS, C_STATE), 0.01)
    inp['s5_lam_im'] = math.pi * jnp.arange(C_STATE, dtype=f32) + nrm((N_ODD, C_GROUPS, C_STATE), 0.01)
    inp['s5_log_dt'] = jax.random.uniform(next(ks), (N_ODD, C_GROUPS), f32, math.log(1e-3), math.log(1e-1))
    inp['s5_b_re'] = nrm((N_ODD, C_GROUPS, C_STATE, C_GROUP), (2 * C_GROUP) ** -0.5)
    inp['s5_b_im'] = nrm((N_ODD, C_GROUPS, C_STATE, C_GROUP), (2 * C_GROUP) ** -0.5)
    inp['s5_c_re'] = nrm((N_ODD, C_GROUPS, C_GROUP, C_STATE), C_STATE ** -0.5)
    inp['s5_c_im'] = nrm((N_ODD, C_GROUPS, C_GROUP, C_STATE), C_STATE ** -0.5)
    inp['s5_d'] = nrm((N_ODD, C_WIDTH), 1.0)
    inp['s5_w_glu'] = nrm((N_ODD, C_WIDTH, C_WIDTH), C_WIDTH ** -0.5)
    inp['s5_b_glu'] = nrm((N_ODD, C_WIDTH), 0.02)
    return inp

def second_block(x, mem, start_frame, norm_mix, norm_xattn, norm_mem, norm_ffn, final_norm,
              xattn_wq, xattn_wkv, xattn_wo, ffn_up, ffn_down, even_w_in, even_w_out,
              dsa_cq_norm, dsa_ckv_norm, dsa_kidx_norm, dsa_w_uq, dsa_w_uk, dsa_w_uv, dsa_w_qidx,
              rwkv_mu, rwkv_w0, rwkv_w2, rwkv_a0, rwkv_a2, rwkv_g2, rwkv_k_k, rwkv_k_a, rwkv_r_k,
              rwkv_ln_w, rwkv_ln_b, odd_w_in, odd_w_out, s5_lam_re, s5_lam_im, s5_log_dt,
              s5_b_re, s5_b_im, s5_c_re, s5_c_im, s5_d, s5_w_glu, s5_b_glu):
    bsz, seq, _ = x.shape
    pos = (start_frame[:, None] + jnp.arange(seq, dtype=jnp.int32)[None, :]).astype(jnp.float32)
    cos_a, sin_a = rope_tables(pos, A_ROPE_DIM)
    cos_i, sin_i = rope_tables(pos, IDX_ROPE_DIM)
    for layer in range(DEPTH):
        i = layer // 2
        xn = rms_norm_2(x, norm_mix[layer])
        if layer % 2 == 0:
            h = xn @ even_w_in[i]
            y_a = dsa_mixer(h[..., :A_COLS], cos_a, sin_a, cos_i, sin_i, dsa_cq_norm[i], dsa_ckv_norm[i],
                            dsa_kidx_norm[i], dsa_w_uq[i], dsa_w_uk[i], dsa_w_uv[i], dsa_w_qidx[i])
            y_b = rwkv7_mixer(h[..., A_COLS:], rwkv_mu[i], rwkv_w0[i], rwkv_w2[i], rwkv_a0[i], rwkv_a2[i],
                              rwkv_g2[i], rwkv_k_k[i], rwkv_k_a[i], rwkv_r_k[i], rwkv_ln_w[i], rwkv_ln_b[i])
            mix = jnp.concatenate([y_a, y_b], axis=-1) @ even_w_out[i]
        else:
            y_c = s5_mixer(xn @ odd_w_in[i], s5_lam_re[i], s5_lam_im[i], s5_log_dt[i], s5_b_re[i], s5_b_im[i],
                           s5_c_re[i], s5_c_im[i], s5_d[i], s5_w_glu[i], s5_b_glu[i])
            mix = y_c @ odd_w_out[i]
        x = x + mix
        x = x + memory_cross_attention(rms_norm_2(x, norm_xattn[layer]), rms_norm_2(mem, norm_mem[layer]),
                                       xattn_wq[layer], xattn_wkv[layer], xattn_wo[layer])
        x = x + squared_relu_mlp(rms_norm_2(x, norm_ffn[layer]), ffn_up[layer], ffn_down[layer])
    return rms_norm_2(x, final_norm)


def setup_inputs(seed=0):
    out = dict(first_inputs(seed))
    for name, value in second_inputs(seed + 1).items():
        if name != "x":
            out[name + "_2"] = value
    return out


def reference(
    x, c, ctx, c_ctx, norm_w, w_mod, b_mod, w_in, w_sgu, b_sgu, v_norm_w, q_norm_w, k_norm_w,
    w_out, mem_2, start_frame_2, norm_mix_2, norm_xattn_2, norm_mem_2, norm_ffn_2, final_norm_2,
    xattn_wq_2, xattn_wkv_2, xattn_wo_2, ffn_up_2, ffn_down_2, even_w_in_2, even_w_out_2,
    dsa_cq_norm_2, dsa_ckv_norm_2, dsa_kidx_norm_2, dsa_w_uq_2, dsa_w_uk_2, dsa_w_uv_2,
    dsa_w_qidx_2, rwkv_mu_2, rwkv_w0_2, rwkv_w2_2, rwkv_a0_2, rwkv_a2_2, rwkv_g2_2, rwkv_k_k_2,
    rwkv_k_a_2, rwkv_r_k_2, rwkv_ln_w_2, rwkv_ln_b_2, odd_w_in_2, odd_w_out_2, s5_lam_re_2,
    s5_lam_im_2, s5_log_dt_2, s5_b_re_2, s5_b_im_2, s5_c_re_2, s5_c_im_2, s5_d_2, s5_w_glu_2,
    s5_b_glu_2,
):
    x = first_block(
        x, c, ctx, c_ctx, norm_w, w_mod, b_mod, w_in, w_sgu, b_sgu, v_norm_w, q_norm_w,
        k_norm_w, w_out,
    )
    return second_block(
        x, mem_2, start_frame_2, norm_mix_2, norm_xattn_2, norm_mem_2, norm_ffn_2, final_norm_2,
        xattn_wq_2, xattn_wkv_2, xattn_wo_2, ffn_up_2, ffn_down_2, even_w_in_2, even_w_out_2,
        dsa_cq_norm_2, dsa_ckv_norm_2, dsa_kidx_norm_2, dsa_w_uq_2, dsa_w_uk_2, dsa_w_uv_2,
        dsa_w_qidx_2, rwkv_mu_2, rwkv_w0_2, rwkv_w2_2, rwkv_a0_2, rwkv_a2_2, rwkv_g2_2,
        rwkv_k_k_2, rwkv_k_a_2, rwkv_r_k_2, rwkv_ln_w_2, rwkv_ln_b_2, odd_w_in_2, odd_w_out_2,
        s5_lam_re_2, s5_lam_im_2, s5_log_dt_2, s5_b_re_2, s5_b_im_2, s5_c_re_2, s5_c_im_2,
        s5_d_2, s5_w_glu_2, s5_b_glu_2,
    )


_drawn_inputs = setup_inputs


def setup_inputs(seed=0):
    import zlib

    import numpy as np

    out = dict(_drawn_inputs(seed))
    spreads = {}
    factors = {'ctx': 2.713,
     'norm_w': 3.719,
     'b_mod': 3.207,
     'b_sgu': 5.991,
     'v_norm_w': 7.041,
     'q_norm_w': 8.0,
     'k_norm_w': 8.0,
     'norm_xattn_2': 8.0,
     'norm_mem_2': 8.0,
     'final_norm_2': 23.643,
     'dsa_cq_norm_2': 3.555,
     'dsa_ckv_norm_2': 8.0,
     'dsa_kidx_norm_2': 3.547,
     'rwkv_w2_2': 3.675,
     'rwkv_a0_2': 3.6,
     'rwkv_k_k_2': 117.491,
     'rwkv_k_a_2': 17.704,
     'rwkv_ln_w_2': 25.082,
     'rwkv_ln_b_2': 28.987,
     's5_lam_re_2': 64.0,
     's5_lam_im_2': 22.176,
     's5_log_dt_2': 25.2,
     's5_b_re_2': 30.728,
     's5_b_im_2': 31.28,
     's5_c_re_2': 30.744,
     's5_c_im_2': 31.008,
     's5_b_glu_2': 200.0,
     'norm_ffn_2': 8.0,
     's5_w_glu_2': 38.224,
     'odd_w_in_2': 8.0,
     'odd_w_out_2': 8.0,
     's5_d_2': 8.0}
    for name, (base, spread) in spreads.items():
        noise = np.random.default_rng([zlib.crc32(name.encode()), seed]).standard_normal(out[name].shape)
        drawn = base * np.exp(spread * noise) if base else spread * noise
        out[name] = jnp.asarray(drawn.astype(out[name].dtype))
    for name, factor in factors.items():
        out[name] = (out[name] * factor).astype(out[name].dtype)
    return out
```

```python
from contextlib import ExitStack, contextmanager
from collections import defaultdict
import numpy as np

import concourse.bass as bass
from concourse import mybir
from concourse.alu_op_type import AluOpType as ALU

ACT = mybir.ActivationFunctionType
AX = mybir.AxisListType.X
F32 = mybir.dt.float32
I32 = mybir.dt.int32

P = 128
D = 2048
SEQ = 256
TT = SEQ // P
KT = D // P
CH = 512
RING = 8
HD = 128
B1_COLS, B1_HALF = 5632, 1024
EVEN_COLS = 4240
A_COLS = 880
B_W, B_H, B_D = 1024, 16, 64
RC = 32
NRC = SEQ // RC
FFN = 8192
S5_STEP = 32
PAIRS = 64
NEG = -3.0e38
TAKEN = -1.0e38
DECAY = float(np.exp(np.float32(-0.5)))
TWO_PI = 6.283185307179586


def cody_waite():
    c1 = 6.28125
    c2 = float(np.float32(np.round((TWO_PI - c1) * 2**19) / 2**19))
    return c1, c2, float(np.float32(TWO_PI - c1 - c2))


class Eng:

    def __init__(self, e, sem, own):
        self.e, self.sem, self.own = e, sem, own
        self.cnt, self.seen = defaultdict(int), defaultdict(int)
        self.last, self.i, self.slopes = None, None, {}

    def at(self, name, v):
        return v if self.i is None or name not in self.slopes else self.i * self.slopes[name] + v

    def count(self, name):
        self.cnt[name] += 1
        return 1

    def up(self, name=None):
        name = name or self.own
        self.cnt[name] += 1
        self.last = (name, self.cnt[name])
        return 1

    def last_sem(self):
        return self.sem(self.last[0])

    def last_count(self):
        return self.at(*self.last)

    def due(self, name, k=1):
        self.seen[name] += k
        return self.at(name, self.seen[name])

    @contextmanager
    def loop(self, n, slopes):
        before = {k: self.cnt[k] + self.seen[k] for k in slopes}
        if n == 1:
            yield 0
        else:
            with self.e.Fori(0, n) as i:
                self.i, self.slopes = i, slopes
                yield i
                self.i, self.slopes = None, {}
        for k, v in slopes.items():
            assert self.cnt[k] + self.seen[k] - before[k] == v, (k, v, self.cnt[k] + self.seen[k] - before[k])
            if self.cnt[k]:
                self.cnt[k] += v * (n - 1)
            else:
                self.seen[k] += v * (n - 1)
        if self.last and self.last[0] in slopes:
            self.last = (self.last[0], self.cnt[self.last[0]])


class Gemm:

    def __init__(self, name, w, k, cols, tiles, owner, lead=0, hook=0):
        self.name, self.w, self.tiles, self.owner = name, w, tiles, owner
        self.kt = k // P
        self.slots = -(-self.kt // 4)
        self.cols = cols
        self.n = len(cols)
        body = 1
        while body * self.slots % RING or body * tiles % 4:
            body += 1
        self.body, self.lead = body, lead
        self.turns = (self.n - lead) // body
        if self.turns < 2:
            self.turns, self.lead = 0, self.n
        self.tail = self.lead + self.turns * body

    def chunk_slots(self):
        return [min(4, self.kt - 4 * s) for s in range(self.slots)]


def chunks(first, last):
    return [(c, min(CH, last - c)) for c in range(first, last, CH)]


def two_blocks(nc, I, out, stop=None, dbg=None, dump=()):
    ctx = ExitStack()
    with ctx:
        sems = {}

        def sem(name):
            if name not in sems:
                sems[name] = ctx.enter_context(nc.semaphore(name))
            return sems[name]

        def sb(name, shape, dt=F32):
            return ctx.enter_context(nc.sbuf_tensor(name, shape, dt))

        BIG_W = 30720
        big = sb("big", [P, BIG_W])
        ring = sb("ring", [P, RING, 4, CH])
        ident = sb("ident", [P, P])
        tri = sb("tri", [P, P])
        rope = sb("rope", [P, 2, TT, HD])
        mask32 = sb("mask32", [P, 2 * RC])
        ind = sb("ind", [P, P // RC])
        gmask = sb("gmask", [P, 2])
        invf = sb("invf", [P, 24])
        tokid = sb("tokid", [P, TT], I32)
        frame = sb("frame", [P, 1], I32)
        posi = sb("posi", [P, TT], I32)
        qk_w = sb("qk_w", [P, 2, 2, HD])
        cols1 = sb("cols1", [P, P])
        cols2 = sb("cols2", [P, P])
        modc = sb("modc", [P, P])
        silu_c = sb("silu_c", [P, KT, 2])
        eps = sb("eps", [P, 3])
        stat = sb("stat", [P, 80])
        stat2 = sb("stat2", [P, 80])
        att_s = sb("att_s", [P, 16])
        stage = sb("stage", [P, 2, CH])
        prob = sb("prob", [P, 2, CH])
        prob_t = sb("prob_t", [P, 2, 4, P])
        angle = sb("angle", [P, 4, PAIRS])
        trig = sb("trig", [P, 2, 48])
        acc = [ctx.enter_context(nc.psum_tensor(f"acc{i}", [P, CH], F32)) for i in range(4)]
        tp = [ctx.enter_context(nc.psum_tensor(f"tp{i}", [P, CH], F32)) for i in range(4)]

        def dram(name, shape):
            return nc.dram_tensor(name, shape, F32, kind="Internal").ap()

        mod_d = dram("mod_d", (2, 2, 3 * D))
        x_d = dram("x_d", (SEQ, D))
        a_d = dram("a_d", (NRC, B_H, RC, RC))
        t_d = dram("t_d", (NRC, B_H, RC, RC))
        kbv_d = dram("kbv_d", (SEQ, 2, 3, CH))
        o_d = dram("o_d", (SEQ, B_W))

        def view(off, *shape):
            n = int(np.prod(shape))
            v = big[:, off:off + n]
            if len(shape) == 1:
                return v
            names = "abcd"[:len(shape)]
            return v.rearrange(f"p ({' '.join(names)}) -> p {' '.join(names)}", **dict(zip(names[1:], shape[1:])))

        x4 = view(0, 4, D)
        vb = view(4096, 4, B1_HALF)
        feat4 = view(8192, KT, 4 * P)
        mix = view(16384, 4, D)
        qb = view(24576, 4, B1_HALF)
        kvb = view(28672, 4, 512)
        q_t = view(8192, 8, 4 * P)
        k_t = view(12288, 2, 4 * P)
        sgu_t = view(13312, 8, P)
        sgu_raw = view(14336, 8, P)
        vnw_row = view(15360, B1_HALF)
        gate = view(24576, 2, D)
        gate_b = view(28672, D)
        mod_row = [view(8192 + 6144 * l, 3 * D) for l in range(2)]
        rows1, rows2, rows3, rows3b = (view(i * P, P) for i in range(4))
        feat = view(8192, KT, SEQ)
        hid_t = view(12288, FFN // P, SEQ)
        HID = [stage, prob]
        xn2 = view(16384, TT, D)
        memb = view(20480, TT, D)

        C1 = {"norm_w0": 0, "norm_w1": 16, "norm_mix0": 32, "norm_mix1": 48, "norm_xattn0": 64, "norm_xattn1": 80,
              "norm_mem0": 96, "norm_mem1": 112}
        C2 = {"norm_ffn0": 0, "norm_ffn1": 16, "s5_d": 32, "s5_b_glu": 48, "c": 64, "c_ctx": 80,
              "b_sgu0": 96, "b_sgu1": 104, "cq": 112}

        CONSTS = 14 + len(C1) + len(C2)

        def col(name, n=KT):
            t, at = (cols1, C1[name]) if name in C1 else (cols2, C2[name])
            return t[:, at:at + n]

        def mod_col(layer, cond, part):
            at = ((layer * 2 + cond) * 2 + part) * KT
            return modc[:, at:at + KT]

        W = lambda name, i=None: I[name] if i is None else I[name][i]
        gemms = defaultdict(list)
        for l in range(2):
            gemms["mod"].append(Gemm(f"mod{l}", W("w_mod", l), D, chunks(0, 3 * D), 1, "act_free"))
        for l in range(2):
            t = 4 if l == 0 else 2
            g = gemms[f"b1_{l}"]
            g.append(Gemm(f"in{l}", W("w_in", l), D, chunks(0, 4096), t, "act_free"))
            g.append(Gemm(f"kv{l}", W("w_in", l), D, chunks(4096, 4608), 4, "act_free"))
            g.append(Gemm(f"zb{l}", W("w_in", l), D, chunks(4608, 5632), t, "act_free"))
            g.append(Gemm(f"out{l}", W("w_out", l), D, chunks(0, D), t, "dve_free"))
        g = gemms["even"]
        g.append(Gemm("even_in", W("even_w_in_2", 0), D, chunks(0, EVEN_COLS), 2, "act_free"))
        flat = lambda a: a.rearrange("r h d -> r (h d)")
        g.append(Gemm("uq", flat(W("dsa_w_uq_2", 0)), 512, chunks(0, 1024), 2, "act_free"))
        g.append(Gemm("qidx", flat(W("dsa_w_qidx_2", 0)), 512, chunks(0, 1024), 2, "act_free"))
        g.append(Gemm("uv", flat(W("dsa_w_uv_2", 0)), 256, chunks(0, 1024), 2, "act_free"))
        g.append(Gemm("even_out", W("even_w_out_2", 0), D, chunks(0, D), 2, "dve_free"))
        g = gemms["odd"]
        g.append(Gemm("odd_in", W("odd_w_in_2", 0), D, chunks(0, D), 2, "act_free"))
        g.append(Gemm("glu", W("s5_w_glu_2", 0), D, chunks(0, D), 2, "act_free"))
        g.append(Gemm("odd_out", W("odd_w_out_2", 0), D, chunks(0, D), 2, "dve_free"))
        for l in range(2):
            g = gemms[f"xat{l}"]
            g.append(Gemm(f"xq{l}", W("xattn_wq_2", l), D, chunks(0, 512), 2, "act_free"))
            g.append(Gemm(f"xkv{l}", W("xattn_wkv_2", l), D, chunks(0, 1024), 2, "act_free"))
            g.append(Gemm(f"xo{l}", W("xattn_wo_2", l), 512, chunks(0, D), 2, "dve_free"))
            g = gemms[f"ffn{l}"]
            g.append(Gemm(f"up{l}", W("ffn_up_2", l), D, chunks(0, FFN), 2, "act_free", lead=1))
            g.append(Gemm(f"down{l}", W("ffn_down_2", l), FFN, chunks(0, D), 2, "dve_free"))
        ORDER = ["load", "mod", "b1_0", "b1_1", "even", "xat0", "ffn0", "odd", "xat1", "ffn1", "final"]
        stages = ORDER if stop is None else ORDER[:ORDER.index(stop) + 1]

        def b1_units(layer):
            units = []
            for t in ([0, 1, 2, 3] if layer == 0 else [0, 1]):
                keys = [0, 1, 2, 3] if t < 2 else [2, 3]
                for h in range(8):
                    units.append(dict(
                        q=q_t[:, h, t * P:(t + 1) * P], k=k_t[:, h // 4, keys[0] * P:(keys[-1] + 1) * P],
                        v=[kvb[:, j, 256 + (h // 4) * HD:256 + (h // 4 + 1) * HD] for j in keys],
                        out=mix[:, t, B1_HALF + h * HD:B1_HALF + (h + 1) * HD], gated=True, bias=None))
            return units

        xa_q = view(12288, TT, 512)
        xa_kv = view(13312, TT, 1024)
        xa_qt = view(24576, 4, SEQ)
        xa_kt = view(25600, 4, SEQ)
        xa_o = view(26624, TT, 512)
        xa_ot = view(27648, 4, SEQ)

        def xat_units():
            return [dict(q=xa_qt[:, h, t * P:(t + 1) * P], k=xa_kt[:, h, :],
                         v=[xa_kv[:, j, 512 + h * HD:512 + (h + 1) * HD] for j in range(TT)],
                         out=xa_o[:, t, h * HD:(h + 1) * HD], gated=False, bias=None)
                    for t in range(TT) for h in range(4)]

        feat_e = view(4096, KT, SEQ)
        hb = view(8192, TT, EVEN_COLS)
        ya = view(16672, TT, 1024)
        d_q = view(18720, TT, 1024)
        d_qi = view(20768, TT, 1024)
        d_qt = view(22816, 8, SEQ)
        d_qit = view(24864, 8, SEQ)
        d_v = view(26912, TT, 1024)
        d_kt = view(4096, 8, SEQ)
        d_uk = view(6144, 2, 8, HD)
        d_cqt = view(28960, 4, SEQ)
        d_ckt = view(29984, 2, SEQ)
        d_kid = view(0, TT, P)
        d_kit = view(256, 2 * SEQ)
        d_score = view(768, TT, SEQ)
        d_work = view(1280, TT, SEQ)
        d_bias = view(1792, TT, SEQ)
        d_ckw = view(2304, 256)
        d_kiw = view(2560, 64)
        d_krt = view(2624, SEQ)
        d_tmp = view(2880, 1024)
        d_top = view(3904, 8)

        def dsa_units():
            return [dict(q=d_qt[:, h, t * P:(t + 1) * P], k=d_kt[:, h, :],
                         v=[d_v[:, j, h * HD:(h + 1) * HD] for j in range(TT)],
                         out=ya[:, t, h * HD:(h + 1) * HD], gated=False, bias=d_bias[:, t, :])
                    for t in range(TT) for h in range(8)]

        R0, K0, V0, WL0, AL0, GL0 = 880, 1904, 2928, 3952, 4016, 4080
        w_sh = view(18720, TT, 3360)
        w_ar = view(18720, 8, NRC, 2, RC)
        w_bk = view(22816, 8, NRC, 2, RC)
        w_row = view(0, 5, B_W)
        w_mu = [view(5120, 2048), view(5120, 1312)]
        w_t = view(5120, 3, B_W)
        w_t4 = view(26912, B_W)
        w_lt = view(27936, 4, P)
        w_w2 = view(28448, 2, B_W)
        w_g2a = view(0, 2, B_W)
        w_tt = view(0, 64, RC)
        w_kbv = [view(2048 + 1536 * i, 3, 8, B_D) for i in range(2)]
        w_G = view(26912, 8, 3, RC)
        w_z = view(27936, CH)
        w_u = view(28448, CH)
        w_A = view(5120, RC, RC)
        w_T = view(6144, RC, RC)
        w_tm = view(0, RC, RC)
        w_a = view(2048, 2, 8 * RC)
        w_st = view(7168, 8, B_D)
        w_pc = sb("w_pc", [P, 8, NRC])
        w_bon = sb("w_bon", [P, TT, B_H])
        w_ln = view(0, 2, B_W)
        w_o = stage

        s_u = view(8192 + 8192, TT, D)
        s_ut = view(4096, KT, SEQ)
        s_zt = view(8192, KT, SEQ)
        s_B = view(12288, KT, 2, P)
        s_C = view(16384, PAIRS, 2, 32)
        s_h = [view(20480 + 4096 * i, S5_STEP, 2, PAIRS) for i in range(2)]
        s_lam = view(28672, 12, PAIRS)
        s_l2 = view(29440, 2, 2, PAIRS)
        s_car = view(29696, 3, 2, PAIRS)
        s_br = view(20480, PAIRS, 16)
        s_bi = view(21504, PAIRS, 16)
        s_be = [view(22528 + 2048 * i, PAIRS, 2, 16) for i in range(2)]
        s_cn = [view(26624 + 1024 * i, KT, 64) for i in range(2)]
        s_ce = view(22528, KT, 2, 64)
        s_ld = view(30080, P)
        s_lr = view(30208, 2, P)
        s_pre = view(12288, KT, SEQ)
        s_sig = view(16384, TT, D)

        block = ctx.enter_context(nc.Block())

        @block.sync
        def _(sp):
            q = 0
            freed, full = 0, 0
            uses = []

            def load(g, w_cols, s, slot):
                kt = g.chunk_slots()[s]
                src = g.w[s * 512:s * 512 + kt * P, :].rearrange("(q p) n -> p q n", p=P)
                n0, width = w_cols
                sp.dma_start(ring[:, slot, 0:kt, 0:width], src[:, :, bass.ds(n0, width)]) \
                    .then_inc(sem(f"ring_full{slot}"), 16)

            for st in stages:
                for g in gemms[st]:
                    for c in range(g.n):
                        for s in range(g.slots):
                            if s < g.slots - 1:
                                freed += 1
                                uses.append(("ring_free", freed))
                            else:
                                uses.append(("gemm_full", full + (c + 1) * g.tiles))
                    full += g.n * g.tiles
                    per = g.body * g.slots

                    def plain(c):
                        nonlocal q
                        for s in range(g.slots):
                            if q >= RING:
                                name, v = uses[q - RING]
                                sp.wait_ge(sem(name), v)
                            load(g, g.cols[c], s, q % RING)
                            q += 1

                    for c in range(g.lead):
                        plain(c)
                    first = g.lead + (g.body if g.turns else 0)
                    for c in range(g.lead, first):
                        plain(c)
                    if g.turns:
                        with sp.Fori(0, g.turns - 1) as i:
                            for j in range(per):
                                name, v = uses[q + j - RING]
                                slope = uses[q + j - RING + per][1] - v if g.turns > 2 else 0
                                sp.wait_ge(sem(name), i * slope + v if slope else v)
                                c, s = first + j // g.slots, j % g.slots
                                load(g, (i * (g.body * CH) + g.cols[c][0], CH), s, (q + j) % RING)
                        q += per * (g.turns - 1)
                    for c in range(g.tail, g.n):
                        plain(c)
            if dbg is not None:
                sp.wait_ge(sem("all_done"), 3)
                for a, b in dump:
                    sp.dma_start(dbg[:, a:b], big[:, a:b]).then_inc(sem("dbg"), 16)
                sp.dma_start(dbg[:, 30000:30128], modc[:, :]).then_inc(sem("dbg"), 16)
                sp.wait_ge(sem("dbg"), 16 * len(dump) + 16)

        @block.gpsimd
        def _(pool):
            L = Eng(pool, sem, "pool_step")

            def dma(dst, src, name):
                with nc.allow_non_contiguous_dma(reason="small constant"):
                    pool.dma_start(dst, src).then_inc(sem(name), 16)

            def row(src, n):
                return src.rearrange("(o n) -> o n", o=1).to_broadcast([P, n])

            for name, dst in (("ident", ident[:, :]), ("tri", tri[:, :]), ("mask32", mask32[:, :]),
                              ("ind", ind[:, :]), ("gmask", gmask[:, :]), ("tokid", tokid[:, :])):
                dma(dst, I["const_" + name], "consts")
            dma(rope[:, 0], I["const_cos"].rearrange("(t p) d -> p t d", p=P), "consts")
            dma(rope[:, 1], I["const_sin"].rearrange("(t p) d -> p t d", p=P), "consts")
            dma(invf[:, :], row(I["const_invf"], 24), "consts")
            dma(frame[:, :], row(I["start_frame_2"], 1), "consts")
            for l in range(2):
                dma(qk_w[:, l, 0], row(I["q_norm_w"][l], HD), "consts")
                dma(qk_w[:, l, 1], row(I["k_norm_w"][l], HD), "consts")
            for name, at in C1.items():
                dma(rows1[at:at + 16, :], I[name[:-1] + ("" if name[:-1] == "norm_w" else "_2")][int(name[-1])]
                    .rearrange("(k p) -> k p", p=P), "consts")
            src2 = {"norm_ffn0": I["norm_ffn_2"][0], "norm_ffn1": I["norm_ffn_2"][1], "s5_d": I["s5_d_2"][0],
                    "s5_b_glu": I["s5_b_glu_2"][0], "c": I["c"][0], "c_ctx": I["c_ctx"], "cq": I["dsa_cq_norm_2"][0]}
            for name, at in C2.items():
                src = I["b_sgu"][int(name[-1])] if "sgu" in name else src2[name].rearrange("(k p) -> k p", p=P)
                dma(rows2[at:at + src.shape[0], :], src, "consts")
            if "mod" in stages:
                for l in range(2):
                    pool.wait_ge(sem("mod_rows"), L.due("mod_rows"))
                    dma(mod_d[l], mod_row[l][0:2, :], "mod_out")
                pool.wait_ge(sem("mod_out"), 32)
                for l in range(2):
                    for c in range(2):
                        at = (l * 2 + c) * 32
                        dma(rows3[at:at + 32, :], mod_d[l, c, 0:2 * D].rearrange("(k p) -> k p", p=P), "mod_in")
                        dma(rows3b[at:at + 32, :], I["b_mod"][l, 0:2 * D].rearrange("(k p) -> k p", p=P), "mod_in")
            for l in range(2):
                if f"b1_{l}" not in stages:
                    continue
                if l == 0:
                    pool.wait_ge(sem("mod_cols"), L.due("mod_cols"))
                    dma(x4[:, 0:2], I["x"][0].rearrange("(t p) d -> p t d", p=P), "x_in")
                    dma(x4[:, 2:4], I["ctx"][0].rearrange("(t p) d -> p t d", p=P), "x_in")
                pool.wait_ge(sem("proj_done"), L.due("proj_done"))
                dma(vnw_row, row(I["v_norm_w"][l].rearrange("g d -> (g d)"), B1_HALF), "sgu_in")
                dma(sgu_raw, I["w_sgu"][l].rearrange("g p q -> p g q"), "sgu_in")
                pool.wait_ge(sem("att_done"), L.due("att_done"))
                for c in range(2):
                    dma(gate[:, c], row(mod_d[l, c, 2 * D:3 * D], D), "gate_in")
                dma(gate_b, row(I["b_mod"][l, 2 * D:3 * D], D), "gate_in")
                if l == 0:
                    dma(x4[:, 2:4], I["ctx"][0].rearrange("(t p) d -> p t d", p=P), "gate_in")
            if "even" in stages:
                pool.wait_ge(sem("x_norm_even"), L.due("x_norm_even"))
                dma(x_d.rearrange("(t p) d -> p t d", p=P), x4[:, 0:2], "x_out")
                pool.wait_ge(sem("x_out"), 16)
                pool.wait_ge(sem("even_h"), L.due("even_h"))
                dma(d_ckw, row(I["dsa_ckv_norm_2"][0], 256), "dsa_in")
                dma(d_kiw, row(I["dsa_kidx_norm_2"][0], 64), "dsa_in")
                pool.wait_ge(sem("uk_zero"), L.due("uk_zero"))
                for rt in range(2):
                    dma(d_uk[:, rt, :, 32:128], I["dsa_w_uk_2"][0][rt * P:(rt + 1) * P], "dsa_in")
                pool.wait_ge(sem("dsa_done"), L.due("dsa_done"))
                pool.wait_ge(sem("shift_zero"), L.due("shift_zero"))
                for t in range(TT):
                    dma(w_sh[1:P, t], hb[0:P - 1, t, A_COLS:], "shift_in")
                dma(w_sh[0:1, 1], hb[P - 1:P, 0, A_COLS:], "shift_in")
                for j, name in enumerate(("w0", "a0", "k_k", "k_a")):
                    dma(w_row[:, j], row(I[f"rwkv_{name}_2"][0], B_W), "rwkv_in")
                dma(w_row[:, 4], row(I["rwkv_r_k_2"][0].rearrange("h d -> (h d)"), B_W), "rwkv_in")
                dma(w_w2[0:64, 0], I["rwkv_w2_2"][0], "rwkv_in")
                dma(w_w2[0:64, 1], I["rwkv_a2_2"][0], "rwkv_in")
                for half, (c0, cw) in enumerate(((0, 2048), (2048, 1312))):
                    dma(w_mu[half], row(I["rwkv_mu_2"][0, c0:c0 + cw], cw), "mu_in")
                    if half == 0:
                        pool.wait_ge(sem("mu_used"), L.due("mu_used"))
                for t in range(TT):
                    pool.wait_ge(sem("arbk_ready"), L.due("arbk_ready"))
                    for j, src in enumerate((hb[:, t, K0:K0 + B_W], w_t4, hb[:, t, V0:V0 + B_W])):
                        by_half = src.rearrange("p (h o d) -> p o h d", o=2, d=B_D)
                        for o in range(2):
                            dma(kbv_d[t * P:(t + 1) * P, o, j].rearrange("s (h d) -> s h d", d=B_D), by_half[:, o], "kbv_out")
                pool.wait_ge(sem("rows_done"), L.due("rows_done"))
                dma(w_g2a[:, 0], I["rwkv_g2_2"][0, 0:P], "g2_in")
                dma(w_g2a[0:32, 1], I["rwkv_g2_2"][0, P:160], "g2_in")
                for c in range(NRC):
                    pool.wait_ge(sem("a_ready"), L.due("a_ready"))
                    for o in range(2):
                        dma(a_d[c].rearrange("(h o) s t -> o s h t", o=2)[o],
                            w_a[64 * o:64 * o + RC, c % 2].rearrange("p (h t) -> p h t", t=RC), f"a_out{c % 2}")
                for j in range(2):
                    pool.wait_ge(sem(f"a_out{j}"), 16 * NRC)
                dma(w_A.rearrange("p s t -> p (s t)"), a_d.rearrange("c h s t -> (c h) (s t)"), "solve_in")
                pool.wait_ge(sem("solved"), L.due("solved"))
                dma(t_d.rearrange("c h s t -> (c h) (s t)"), w_T.rearrange("p s t -> p (s t)"), "t_out")
                pool.wait_ge(sem("t_out"), 16)
                pool.wait_ge(sem("kbv_out"), 16 * 6 * TT)
                by_unit = t_d.rearrange("c h s t -> (c h) s t").rearrange("(u o) s t -> o s u t", o=2)

                def chunk_in(c):
                    for o in range(2):
                        dma(w_kbv[c % 2][64 * o:64 * o + RC].rearrange("p a h d -> p (a h d)"),
                            kbv_d[c * RC:(c + 1) * RC, o].rearrange("s a n -> s (a n)"), f"kbv_in{c % 2}")

                for o in range(2):
                    dma(w_tt[64 * o:64 * o + RC], by_unit[o], "t_in")
                chunk_in(0)
                chunk_in(1)
                for c in range(NRC):
                    pool.wait_ge(sem("o_ready"), L.due("o_ready"))
                    for o in range(2):
                        dma(o_d[c * RC:(c + 1) * RC].rearrange("s (h o d) -> o s h d", o=2, d=B_D)[o],
                            w_o[64 * o:64 * o + RC, c % 2].rearrange("p (h d) -> p h d", d=B_D), f"o_out{c % 2}")
                    if c + 2 < NRC:
                        pool.wait_ge(sem("st_ready"), L.due("st_ready"))
                        chunk_in(c + 2)
                for j in range(2):
                    pool.wait_ge(sem(f"o_out{j}"), 16 * NRC)
                for t in range(TT):
                    dma(hb[:, t, R0:R0 + B_W], o_d[t * P:(t + 1) * P], "o_in")
                dma(w_ln[:, 0], row(I["rwkv_ln_w_2"][0], B_W), "o_in")
                dma(w_ln[:, 1], row(I["rwkv_ln_b_2"][0], B_W), "o_in")
                pool.wait_ge(sem("rwkv_done"), L.due("rwkv_done"))
                dma(x4[:, 0:2], x_d.rearrange("(t p) d -> p t d", p=P), "x_back")
            for l in range(2):
                if l == 1 and "odd" in stages:
                    pool.wait_ge(sem("s5_free"), L.due("s5_free"))
                    for s, d in ((I["s5_b_re_2"], s_br), (I["s5_b_im_2"], s_bi)):
                        dma(d, s[0].rearrange("(r g) p i -> (g p) r i", g=2), "s5_in")
                    for s, d in ((I["s5_c_re_2"], s_cn[0]), (I["s5_c_im_2"], s_cn[1])):
                        dma(d, s[0].rearrange("g i p -> (g i) p").rearrange("(k c) p -> c k p", c=P), "s5_in")
                    for s, d in ((I["s5_lam_re_2"], s_lr[0:64, 0]), (I["s5_lam_im_2"], s_lr[0:64, 1])):
                        dma(d, s[0].rearrange("(r g) p -> r (g p)", g=2), "s5_in")
                    dma(s_ld, row(I["s5_log_dt_2"][0], P), "s5_in")
                if f"xat{l}" in stages:
                    pool.wait_ge(sem("mem_free"), L.due("mem_free"))
                    dma(memb, I["mem_2"][0].rearrange("(t p) d -> p t d", p=P), "mem_in")
            if "final" in stages:
                pool.wait_ge(sem("fin_free"), L.due("fin_free"))
                dma(view(8192, D), row(I["final_norm_2"], D), "fin_in")
                for t in range(TT):
                    pool.wait_ge(sem("y_ready"), L.due("y_ready"))
                    dma(out[0, t * P:(t + 1) * P], xn2[:, t], "y_out")
                pool.wait_ge(sem("y_out"), 16 * TT)

        @block.tensor
        def _(pe):
            E = Eng(pe, sem, "pe_step")
            owners, given = [], defaultdict(int)
            given["act_free"] = 4
            q = 0
            n_tp = 0

            def begin(owner):
                g = len(owners)
                if g >= 4:
                    pe.wait_ge(sem(owners[g - 4][0]), owners[g - 4][1])
                given[owner] += 1
                owners.append((owner, given[owner]))
                return acc[g % 4]

            def gemm(g, lhs, hook=None):
                nonlocal q
                for name, v in dict(owners[-4:]).items():
                    pe.wait_ge(sem(name), v)
                base, g0 = given[g.owner], len(owners)
                per_slots, per_groups = g.body * g.slots, g.body * g.tiles

                def chunk(c, i, j0, s0):
                    width = g.cols[c][1]
                    for s, kt in enumerate(g.chunk_slots()):
                        use = q + s0 + s
                        v = 16 * (use // RING + 1)
                        full = v if isinstance(i, int) else i * (16 * per_slots // RING) + v
                        pe.wait_ge(sem(f"ring_full{use % RING}"), full)
                        for t in range(g.tiles):
                            bank = acc[(g0 + j0 + t) % 4]
                            if s == 0:
                                v = base + j0 + t - 3
                                pe.wait_ge(sem(g.owner), v if isinstance(i, int) else i * per_groups + v)
                            for k in range(kt):
                                lt = lhs(4 * s + k, t)
                                mm = pe.matmul(bank[0:lt.shape[-1], 0:width], lt, ring[:, use % RING, k, 0:width],
                                               start=(s + k == 0), stop=(4 * s + k == g.kt - 1))
                            if s == g.slots - 1:
                                mm.then_inc(sem("gemm_full"), E.up("gemm_full"))
                        if s < g.slots - 1:
                            mm.then_inc(sem("ring_free"), E.up("ring_free"))
                    if hook:
                        hook(c, i)

                for c in range(g.lead):
                    chunk(c, 0, c * g.tiles, c * g.slots)
                if g.turns:
                    slopes = {"gemm_full": per_groups}
                    if g.slots > 1:
                        slopes["ring_free"] = g.body * (g.slots - 1)
                    if hook:
                        slopes |= {"sq_ready": per_groups, "tp_full": per_groups, "tp_free": per_groups}
                    with E.loop(g.turns, slopes) as i:
                        for b in range(g.body):
                            c = g.lead + b
                            chunk(c, i, c * g.tiles, c * g.slots)
                for c in range(g.tail, g.n):
                    chunk(c, 0, c * g.tiles, c * g.slots)
                q += g.n * g.slots
                for _ in range(g.n * g.tiles):
                    given[g.owner] += 1
                    owners.append((g.owner, given[g.owner]))

            def turn(blocks, name="tp_full"):
                nonlocal n_tp
                bank = tp[n_tp % 4]
                if n_tp >= 4:
                    E.seen["tp_free"] = max(E.seen["tp_free"], n_tp - 3)
                    pe.wait_ge(sem("tp_free"), n_tp - 3)
                n_tp += 1
                for j, b in enumerate(blocks):
                    mm = pe.transpose(bank[0:b.shape[-1], j * P:j * P + b.shape[0]], b, ident[0:b.shape[0], 0:b.shape[0]])
                mm.then_inc(sem("tp_full"), E.up("tp_full"))
                return n_tp

            def turn_all(src, tiles, width, ready=None):
                if ready:
                    pe.wait_ge(sem(ready), E.due(ready))
                for t in range(tiles):
                    if not ready:
                        pe.wait_ge(sem("src_ready"), E.due("src_ready"))
                    for k in range(0, width // P, 4):
                        turn([src(t)[:, (k + j) * P:(k + j + 1) * P] for j in range(min(4, width // P - k))])

            def attend(units):
                n = len(units)
                score_at, turned = {}, {}
                for i in range(n + 2):
                    if i < n:
                        u = units[i]
                        bank = begin("act_free" if u["bias"] is None else "dve_free")
                        score_at[i] = owners[-1]
                        pe.matmul(bank[:, 0:u["k"].shape[-1]], u["q"], u["k"], start=True, stop=True) \
                            .then_inc(sem("score_full"), E.up("score_full"))
                    if 0 <= i - 1 < n:
                        u = units[i - 1]
                        if u["bias"] is None:
                            pe.wait_ge(sem(score_at[i - 1][0]), score_at[i - 1][1])
                        else:
                            pe.wait_ge(sem("p_ready"), E.due("p_ready"))
                        turned[i - 1] = turn([prob[:, (i - 1) % 2, j * P:(j + 1) * P] for j in range(len(u["v"]))])
                    if i >= 2:
                        u = units[i - 2]
                        pe.wait_ge(sem("tp_free"), turned[i - 2])
                        bank = begin("dve_free")
                        for j, v in enumerate(u["v"]):
                            mm = pe.matmul(bank[:, 0:HD], prob_t[:, (i - 2) % 2, j, :], v,
                                           start=(j == 0), stop=(j == len(u["v"]) - 1))
                        mm.then_inc(sem("pv_full"), E.up("pv_full"))

            def feat_lhs(f):
                return lambda k, t: f[:, k, t * P:(t + 1) * P]

            if "load" in stages:
                pe.wait_ge(sem("consts"), 16 * CONSTS)
                turn([rows1])
                turn([rows2[0:116, :]])
            if "mod" in stages:
                pe.wait_ge(sem("silu_ready"), E.due("silu_ready"))
                for g in gemms["mod"]:
                    gemm(g, lambda k, t: silu_c[:, k, :])
                pe.wait_ge(sem("src_ready"), E.due("src_ready"))
                turn([rows3])

            def block1(l):
                g_in, g_kv, g_zb, g_out = gemms[f"b1_{l}"]
                turn_all(lambda t: mix[:, t, :], 4, D)
                pe.wait_ge(sem("feat_ready"), E.due("feat_ready"))
                gemm(g_in, feat_lhs(feat4))
                gemm(g_kv, feat_lhs(feat4))
                gemm(g_zb, feat_lhs(feat4))
                tiles = g_out.tiles
                pe.wait_ge(sem("sgu_in"), 32 * (l + 1))
                for g in (0, 4):
                    turn([sgu_raw[:, g + j, :] for j in range(4)])
                pe.wait_ge(sem("sgu_t_ready"), E.due("sgu_t_ready"))
                for t in range(tiles):
                    pe.wait_ge(sem("vn_ready"), E.due("vn_ready"))
                    for half in range(2):
                        bank = begin("dve_free")
                        for j in range(4):
                            g = half * 4 + j
                            mm = pe.matmul(bank[:, j * P:(j + 1) * P], sgu_t[:, g, :], vb[:, t, g * P:(g + 1) * P],
                                           start=True, stop=True)
                        mm.then_inc(sem("unit_full"), E.up("unit_full"))
                for t in range(4):
                    pe.wait_ge(sem("qk_ready"), E.due("qk_ready"))
                    if t < tiles:
                        for h in (0, 4):
                            turn([qb[:, t, (h + j) * HD:(h + j + 1) * HD] for j in range(4)])
                    turn([kvb[:, t, j * HD:(j + 1) * HD] for j in range(2)])
                pe.wait_ge(sem("qkt_ready"), E.due("qkt_ready"))
                attend(b1_units(l))
                turn_all(lambda t: mix[:, t, :], tiles, D)
                pe.wait_ge(sem("feat_ready"), E.due("feat_ready"))
                gemm(g_out, feat_lhs(feat4))

            def even():
                g_in, g_uq, g_qi, g_uv, g_out = gemms["even"]
                turn_all(lambda t: xn2[:, t, :], TT, D)
                pe.wait_ge(sem("feat_ready"), E.due("feat_ready"))
                gemm(g_in, feat_lhs(feat_e))
                pe.wait_ge(sem("lat_ready"), E.due("lat_ready"))
                for t in range(TT):
                    turn([hb[:, t, j * P:(j + 1) * P] for j in range(4)])
                    turn([hb[:, t, 512 + j * P:512 + (j + 1) * P] for j in range(2)])
                    turn([d_kid[:, t, :], hb[:, t, 768:800]])
                pe.wait_ge(sem("lat_t_ready"), E.due("lat_t_ready"))
                gemm(g_uq, feat_lhs(d_cqt))
                gemm(g_qi, feat_lhs(d_cqt))
                gemm(g_uv, feat_lhs(d_ckt))
                pe.wait_ge(sem("dsa_in"), 64)
                for h in range(8):
                    bank = begin("act_free")
                    for rt in range(2):
                        mm = pe.matmul(bank[:, 0:SEQ], d_uk[:, rt, h, :], d_ckt[:, rt, :], start=(rt == 0), stop=(rt == 1))
                    mm.then_inc(sem("unit_full"), E.up("unit_full"))
                for t in range(TT):
                    pe.wait_ge(sem("dq_ready"), E.due("dq_ready"))
                    for h in (0, 4):
                        turn([d_q[:, t, (h + j) * P:(h + j + 1) * P] for j in range(4)])
                    for h in (0, 4):
                        turn([d_qi[:, t, (h + j) * P:(h + j + 1) * P] for j in range(4)])
                pe.wait_ge(sem("dqt_ready"), E.due("dqt_ready"))
                for t in range(TT):
                    for hp in range(8):
                        bank = begin("act_free")
                        pe.matmul(bank[:, :], d_qit[:, hp, t * P:(t + 1) * P], d_kit, start=True, stop=True) \
                            .then_inc(sem("unit_full"), E.up("unit_full"))
                pe.wait_ge(sem("bias_ready"), E.due("bias_ready"))
                pe.wait_ge(sem("kt_ready"), E.due("kt_ready"))
                attend(dsa_units())
                rwkv()
                for t in range(TT):
                    pe.wait_ge(sem("src_ready"), E.due("src_ready"))
                    for src in (ya[:, t, :], hb[:, t, R0:R0 + B_W]):
                        for k in (0, 4):
                            turn([src[:, (k + j) * P:(k + j + 1) * P] for j in range(4)])
                pe.wait_ge(sem("feat_ready"), E.due("feat_ready"))
                gemm(g_out, feat_lhs(feat_e))

            def rwkv():
                pe.wait_ge(sem("rwkv_in"), 16 * 7)
                for t in range(TT):
                    pe.wait_ge(sem("lora_ready"), E.due("lora_ready"))
                    turn([hb[:, t, WL0:WL0 + 64], hb[:, t, AL0:AL0 + 64]])
                    pe.wait_ge(sem("lora_t"), E.due("lora_t"))
                    for j in range(2):
                        for half in range(2):
                            bank = begin("dve_free")
                            pe.matmul(bank[:, :], w_lt[0:64, j, :], w_w2[0:64, j, half * CH:(half + 1) * CH],
                                            start=True, stop=True).then_inc(sem("unit_full"), E.up("unit_full"))
                    pe.wait_ge(sem("sig_ready"), E.due("sig_ready"))
                    for half in range(2):
                        bank = begin("act_free")
                        pe.matmul(bank[:, :], tri[:, :], w_t[:, 0, half * CH:(half + 1) * CH], start=True, stop=True) \
                            .then_inc(sem("unit_full"), E.up("unit_full"))
                    bank = begin("act_free")
                    for hp in range(8):
                        mm = pe.matmul(bank[:, hp * 4:hp * 4 + 4], w_t[:, 0, hp * P:(hp + 1) * P], ind[:, :],
                                       start=True, stop=True)
                    mm.then_inc(sem("unit_full"), E.up("unit_full"))
                    pe.wait_ge(sem("arbk_ready"), E.due("arbk_ready"))
                    for a in (w_t[:, 1, :], hb[:, t, R0:R0 + B_W], w_t4, hb[:, t, K0:K0 + B_W]):
                        for h in (0, 4):
                            turn([a[:, (h + j) * P:(h + j + 1) * P] for j in range(4)])
                pe.wait_ge(sem("g2_in"), 32)
                for t in range(TT):
                    turn([hb[:, t, GL0:GL0 + P], hb[:, t, GL0 + P:GL0 + 160]])
                    pe.wait_ge(sem("lora_t"), E.due("lora_t"))
                    for half in range(2):
                        bank = begin("act_free")
                        cs = slice(half * CH, (half + 1) * CH)
                        pe.matmul(bank[:, :], w_lt[:, 2, :], w_g2a[:, 0, cs], start=True, stop=False)
                        pe.matmul(bank[:, :], w_lt[0:32, 3, :], w_g2a[0:32, 1, cs], start=False, stop=True) \
                            .then_inc(sem("unit_full"), E.up("unit_full"))

                def heads(owner, products, rows_out=RC):
                    banks = [begin(owner) for _ in range(2)]
                    for hp in range(8):
                        for o in range(2):
                            terms = products(hp, o)
                            n = terms[0][1].free_size()
                            for j, (lt, rhs) in enumerate(terms):
                                mm = pe.matmul(banks[o][64 * o:64 * o + rows_out, hp * n:(hp + 1) * n], lt, rhs,
                                               start=(j == 0), stop=(j == len(terms) - 1))
                            if hp == 7:
                                mm.then_inc(sem("unit_full"), E.up("unit_full"))

                ks = [slice(0, 64), slice(64, 128)]
                ts = [slice(0, RC), slice(64, 64 + RC)]
                for c in range(NRC):
                    heads("dve_free", lambda hp, o: [(w_bk[ks[o], hp, c, 0, :], w_ar[ks[o], hp, c, 0, :])])
                pe.wait_ge(sem("t_in"), 32)
                for c in range(NRC):
                    heads("dve_free", lambda hp, o: [(w_bk[ks[o], hp, c, 1, :],
                                                      w_ar[ks[o], hp, c, :, :].rearrange("p a t -> p (a t)"))])
                    heads("dve_free", lambda hp, o: [(w_bk[ks[o], hp, c, 0, :], w_ar[ks[o], hp, c, 1, :])])
                    pe.wait_ge(sem(f"kbv_in{c % 2}"), 32 * (c // 2 + 1))
                    kbv = w_kbv[c % 2]
                    pe.wait_ge(sem("G_ready"), E.due("G_ready"))
                    if c:
                        pe.wait_ge(sem("st_ready"), E.due("st_ready"))
                    state = lambda hp, o, j: [(w_ar[ks[o], hp, c, j, :], w_st[ks[o], hp, :])] if c else []
                    heads("dve_free", lambda hp, o: state(hp, o, 0) + [(w_G[ts[o], hp, 1, :], kbv[ts[o], 2, hp, :])])
                    pe.wait_ge(sem("z_ready"), E.due("z_ready"))
                    heads("dve_free", lambda hp, o: [(w_tt[ts[o], c * 8 + hp, :], w_z[ts[o], hp * 64:hp * 64 + 64])])
                    pe.wait_ge(sem("u_ready"), E.due("u_ready"))
                    u = lambda hp, o: w_u[ts[o], hp * 64:hp * 64 + 64]
                    heads("act_free", lambda hp, o: state(hp, o, 1) + [(w_G[ts[o], hp, 2, :], kbv[ts[o], 2, hp, :]),
                                                                       (w_G[ts[o], hp, 0, :], u(hp, o))])
                    if c < NRC - 1:
                        heads("dve_free", lambda hp, o: [(kbv[ts[o], 0, hp, :], kbv[ts[o], 2, hp, :]),
                                                         (kbv[ts[o], 1, hp, :], u(hp, o))], rows_out=64)

            def xat(l):
                g_q, g_kv, g_o = gemms[f"xat{l}"]
                turn_all(lambda t: xn2[:, t, :], TT, D)
                pe.wait_ge(sem("feat_ready"), E.due("feat_ready"))
                gemm(g_q, feat_lhs(feat))
                turn_all(lambda t: memb[:, t, :], TT, D)
                pe.wait_ge(sem("feat_ready"), E.due("feat_ready"))
                gemm(g_kv, feat_lhs(feat))
                pe.wait_ge(sem("xqk_ready"), E.due("xqk_ready"))
                for t in range(TT):
                    turn([xa_q[:, t, j * P:(j + 1) * P] for j in range(4)])
                    turn([xa_kv[:, t, j * P:(j + 1) * P] for j in range(4)])
                pe.wait_ge(sem("qkt_ready"), E.due("qkt_ready"))
                attend(xat_units())
                turn_all(lambda t: xa_o[:, t, :], TT, 512)
                pe.wait_ge(sem("feat_ready"), E.due("feat_ready"))
                gemm(g_o, feat_lhs(xa_ot))

            def ffn(l):
                g_up, g_down = gemms[f"ffn{l}"]
                turn_all(lambda t: xn2[:, t, :], TT, D)
                pe.wait_ge(sem("feat_ready"), E.due("feat_ready"))
                n0 = n_tp

                def turn_hidden(c, i):
                    nonlocal n_tp
                    if c == 0:
                        return
                    for t in range(TT):
                        pe.wait_ge(sem("sq_ready"), E.due("sq_ready"))
                        bank = tp[n_tp % 4]
                        n_tp += 1
                        E.seen["tp_free"] += 1
                        pe.wait_ge(sem("tp_free"), E.at("tp_free", n_tp - 4))
                        for j in range(4):
                            mm = pe.transpose(bank[:, j * P:(j + 1) * P],
                                              HID[(c - 1) % 2][:, t, j * P:(j + 1) * P], ident[:, :])
                        mm.then_inc(sem("tp_full"), E.up("tp_full"))
                    if c == g_up.lead + g_up.body - 1 and not isinstance(i, int):
                        n_tp += (g_up.turns - 1) * g_up.body * g_up.tiles

                gemm(g_up, feat_lhs(feat), hook=turn_hidden)
                for t in range(TT):
                    pe.wait_ge(sem("sq_ready"), E.due("sq_ready"))
                    turn([HID[1][:, t, j * P:(j + 1) * P] for j in range(4)])
                pe.wait_ge(sem("feat_ready"), E.due("feat_ready"))
                gemm(g_down, lambda k, t: hid_t[:, k, t * P:(t + 1) * P])

            def odd():
                g_in, g_glu, g_out = gemms["odd"]
                turn_all(lambda t: xn2[:, t, :], TT, D)
                pe.wait_ge(sem("feat_ready"), E.due("feat_ready"))
                gemm(g_in, feat_lhs(feat))
                turn_all(lambda t: s_u[:, t, :], TT, D, "s_u_ready")
                pe.wait_ge(sem("feat_ready"), E.due("feat_ready"))
                pe.wait_ge(sem("s5_in"), 16 * 7)
                turn([s_lr[0:64, j, :] for j in range(2)])
                for ri in range(2):
                    pe.wait_ge(sem("be_ready"), E.due("be_ready"))
                    for k in range(0, KT, 4):
                        turn([s_be[ri][:, (k + j) * 4:(k + j) * 4 + 4].rearrange("p r g i -> p (r g i)") for j in range(4)])
                for ri in range(2):
                    pe.wait_ge(sem("ce_ready"), E.due("ce_ready"))
                    for k in range(0, KT, 4):
                        turn([s_ce[:, k + j].rearrange("p g s -> p (g s)") for j in range(4)])
                pe.wait_ge(sem("bc_ready"), E.due("bc_ready"))
                NB = SEQ // S5_STEP
                for b in range(NB + 1):
                    if b < NB:
                        ts = slice(b * S5_STEP, (b + 1) * S5_STEP)
                        for kq in range(2):
                            banks = [begin("act_free") for _ in range(4)]
                            for kk in range(8):
                                k = kq * 8 + kk
                                for ri in range(2):
                                    for j in range(4):
                                        rows = slice(32 * j, 32 * j + 32)
                                        mm = pe.matmul(banks[j][:, (kk * 2 + ri) * S5_STEP:(kk * 2 + ri + 1) * S5_STEP],
                                                       s_B[rows, k, ri, :], s_ut[rows, k, ts], start=True, stop=True)
                                        if kk == 7 and ri == 1:
                                            mm.then_inc(sem("unit_full"), E.up("unit_full"))
                    if b:
                        pe.wait_ge(sem("scan_done"), E.due("scan_done"))
                        bank = begin("dve_free")
                        for k in range(KT):
                            for j in range(4):
                                for ri in range(2):
                                    mm = pe.matmul(bank[32 * j:32 * j + 32, k * S5_STEP:(k + 1) * S5_STEP],
                                                   s_C[:, k * 4 + j, ri, :], s_h[(b - 1) % 2][:, :, ri, k * 4 + j],
                                                   start=(ri == 0), stop=(ri == 1))
                        mm.then_inc(sem("unit_full"), E.up("unit_full"))
                pe.wait_ge(sem("z_done"), E.due("z_done"))
                gemm(g_glu, feat_lhs(s_zt))
                turn_all(lambda t: s_sig[:, t, :], TT, D, "sig_full")
                pe.wait_ge(sem("feat_ready"), E.due("feat_ready"))
                gemm(g_out, feat_lhs(s_zt))

            for l in range(2):
                if f"b1_{l}" in stages:
                    block1(l)
            if "even" in stages:
                even()
            for l in range(2):
                if l == 1 and "odd" in stages:
                    odd()
                if f"xat{l}" in stages:
                    xat(l)
                if f"ffn{l}" in stages:
                    ffn(l)
            if dbg is not None:
                pe.wait_ge(E.last_sem(), E.last_count())
                pe.nop().then_inc(sem("all_done"), E.count("all_done"))

        @block.scalar
        def _(act):
            E = Eng(act, sem, "act_step")
            f = act.activation
            g_n = 0

            def take(name):
                nonlocal g_n
                act.wait_ge(sem(name), E.due(name))
                g_n += 1
                return acc[(g_n - 1) % 4][:, :]

            def skip(name, k):
                nonlocal g_n
                E.seen[name] += k
                g_n += k

            def evac(g, fn):
                def chunk(c, i):
                    n0, width = g.cols[c]
                    if not isinstance(i, int):
                        n0 = i * (g.body * CH) + n0
                    for t in range(g.tiles):
                        fn(c, bass.ds(n0 - g.cols[0][0], width), t, take("gemm_full")[:, 0:width])

                nonlocal g_n
                for c in range(g.lead):
                    chunk(c, 0)
                if g.turns:
                    per = g.body * g.tiles
                    with E.loop(g.turns, {"gemm_full": per, "act_free": per} | ({"sq_ready": per} if g.name[:2] == "up" else {})) as i:
                        for b in range(g.body):
                            chunk(g.lead + b, i)
                    g_n += per * (g.turns - 1)
                for c in range(g.tail, g.n):
                    chunk(c, 0)

            def copy_to(dst):
                return lambda c, cs, t, bank: f(dst[:, t, cs], bank, ACT.Copy).then_inc(sem("act_free"), E.up("act_free"))

            def square_sums(src, junk, tiles, eps_col):
                for t in range(tiles):
                    f(junk(t), src(t), ACT.Square, accum_out=stat[:, t:t + 1]).then_inc(sem("act_step"), E.up())
                act.wait_ge(E.last_sem(), E.last_count())
                f(stat2[:, 0:tiles], stat[:, 0:tiles], ACT.Sqrt, bias=eps[:, eps_col:eps_col + 1], scale=1.0 / D) \
                    .then_inc(sem("sd_ready"), E.up("sd_ready"))

            def root(n):
                act.wait_ge(sem("ms_ready"), E.due("ms_ready"))
                f(stat2[:, 0:n], stat[:, 0:n], ACT.Sqrt).then_inc(sem("sd_ready"), E.up("sd_ready"))

            def attend(units):
                nonlocal g_n
                n = len(units)
                for i in range(n + 2):
                    if i < n:
                        u, s = units[i], i % 2
                        act.wait_ge(sem("nmax_ready"), E.due("nmax_ready"))
                        nk = u["k"].shape[-1]
                        if u["bias"] is None:
                            bank = take("score_full")
                            f(prob[:, s, 0:nk], bank[:, 0:nk], ACT.Exp, bias=att_s[:, s:s + 1], scale=HD ** -0.5,
                                    accum_out=att_s[:, 2 + s:3 + s]).then_inc(sem("act_free"), E.up("act_free"))
                        else:
                            skip("score_full", 1)
                            f(prob[:, s, 0:nk], prob[:, s, 0:nk], ACT.Exp, bias=att_s[:, s:s + 1],
                                    accum_out=att_s[:, 2 + s:3 + s]).then_inc(sem("p_ready"), E.up("p_ready"))
                    if i >= 2:
                        g_n += 1

            for _ in range(4):
                act.nop().then_inc(sem("act_free"), E.up("act_free"))
            if "load" in stages:
                act.wait_ge(sem("trig_args"), E.due("trig_args"))
                f(trig[:, 0, :], angle[:, 0, 0:48], ACT.Sin).then_inc(sem("act_step"), E.up())
                f(trig[:, 1, :], angle[:, 1, 0:48], ACT.Sin).then_inc(sem("trig_ready"), E.up("trig_ready"))
                act.wait_ge(sem("cols_ready"), E.due("cols_ready"))
                f(silu_c[:, :, 0], col("c"), ACT.Silu).then_inc(sem("act_step"), E.up())
                f(silu_c[:, :, 1], col("c_ctx"), ACT.Silu).then_inc(sem("silu_ready"), E.up("silu_ready"))
            if "mod" in stages:
                for l, g in enumerate(gemms["mod"]):
                    evac(g, lambda c, cs, t, bank: f(mod_row[l][0:2, cs], bank[0:2, :], ACT.Copy) \
                        .then_inc(sem("act_free"), E.up("act_free")))
                    act.wait_ge(E.last_sem(), E.last_count())
                    act.nop().then_inc(sem("mod_rows"), E.count("mod_rows"))

            def block1(l):
                g_in, g_kv, g_zb, g_out = gemms[f"b1_{l}"]
                if l == 0:
                    act.wait_ge(sem("x_in"), E.due("x_in", 32))
                else:
                    act.wait_ge(sem("x_ready"), E.due("x_ready"))
                square_sums(lambda t: x4[:, t], lambda t: mix[:, t], 4, 0)
                za = [0]

                def to_mix(c, cs, t, bank):
                    n0 = c * CH
                    if c < 2:
                        f(mix[:, t, n0:n0 + CH], bank, ACT.Gelu_apprx_tanh).then_inc(sem("act_free"), E.up("act_free"))
                    elif c < 4:
                        f(vb[:, t, n0 - 1024:n0 - 1024 + CH], bank, ACT.Gelu_apprx_tanh) \
                            .then_inc(sem("act_free"), E.up("act_free"))
                    elif c < 6:
                        if za[0] >= 2:
                            act.wait_ge(sem("za_used"), E.due("za_used"))
                        f(stage[:, za[0] % 2], bank, ACT.Silu).then_inc(sem("act_free"), E.up("act_free"))
                        act.wait_ge(E.last_sem(), E.last_count())
                        act.nop().then_inc(sem("za_ready"), E.count("za_ready"))
                        za[0] += 1
                    else:
                        f(qb[:, t, n0 - 3072:n0 - 3072 + CH], bank, ACT.Copy).then_inc(sem("act_free"), E.up("act_free"))

                unrolled(g_in, to_mix)
                act.wait_ge(sem("za_used"), E.due("za_used", 2))
                unrolled(g_kv, lambda c, cs, t, bank: f(kvb[:, t], bank, ACT.Copy) \
                    .then_inc(sem("act_free"), E.up("act_free")))
                unrolled(g_zb, lambda c, cs, t, bank: f(mix[:, t, B1_HALF + c * CH:B1_HALF + (c + 1) * CH], bank, ACT.Silu) \
                    .then_inc(sem("act_free"), E.up("act_free")))
                act.wait_ge(E.last_sem(), E.last_count())
                act.nop().then_inc(sem("proj_done"), E.count("proj_done"))
                root(72)
                skip("unit_full", 2 * g_out.tiles)
                attend(b1_units(l))
                skip("gemm_full", g_out.n * g_out.tiles)

            def unrolled(g, fn):
                for c in range(g.n):
                    for t in range(g.tiles):
                        fn(c, None, t, take("gemm_full")[:, 0:g.cols[c][1]])

            def even():
                g_in, g_uq, g_qi, g_uv, g_out = gemms["even"]
                act.wait_ge(sem("x_ready"), E.due("x_ready"))
                square_sums(lambda t: x4[:, t], lambda t: xn2[:, t], TT, 1)
                evac(g_in, copy_to(hb))
                act.wait_ge(E.last_sem(), E.last_count())
                act.nop().then_inc(sem("even_h"), E.count("even_h"))
                root(6)
                unrolled(g_uq, lambda c, cs, t, bank: f(d_q[:, t, c * CH:(c + 1) * CH], bank, ACT.Copy) \
                    .then_inc(sem("act_free"), E.up("act_free")))
                unrolled(g_qi, lambda c, cs, t, bank: f(d_qi[:, t, c * CH:(c + 1) * CH], bank, ACT.Copy) \
                    .then_inc(sem("act_free"), E.up("act_free")))
                unrolled(g_uv, lambda c, cs, t, bank: f(d_v[:, t, c * CH:(c + 1) * CH], bank, ACT.Copy) \
                    .then_inc(sem("act_free"), E.up("act_free")))
                act.wait_ge(E.last_sem(), E.last_count())
                act.nop().then_inc(sem("dsa_proj"), E.count("dsa_proj"))
                for h in range(8):
                    f(d_kt[:, h, :], take("unit_full")[:, 0:SEQ], ACT.Copy).then_inc(sem("act_free"), E.up("act_free"))
                act.wait_ge(E.last_sem(), E.last_count())
                for h in range(8):
                    f(d_kt[0:32, h, :], d_krt[0:32, :], ACT.Copy).then_inc(sem("act_step"), E.up())
                act.wait_ge(E.last_sem(), E.last_count())
                act.nop().then_inc(sem("kt_ready"), E.count("kt_ready"))
                slots = [stage[:, 0], stage[:, 1], prob[:, 0], prob[:, 1]]
                for n in range(TT * 8):
                    bank = take("unit_full")
                    if n >= 4:
                        act.wait_ge(sem("rl_used"), E.due("rl_used"))
                    f(slots[n % 4], bank, ACT.Relu).then_inc(sem("act_free"), E.up("act_free"))
                    act.wait_ge(E.last_sem(), E.last_count())
                    act.nop().then_inc(sem("rl_ready"), E.count("rl_ready"))
                act.wait_ge(sem("rl_used"), E.due("rl_used", 4))
                attend(dsa_units())
                for t in range(TT):
                    if t == 0:
                        act.wait_ge(sem("mix_done"), E.due("mix_done"))
                        for u in range(TT):
                            f(hb[:, u, GL0:GL0 + 160], hb[:, u, GL0:GL0 + 160], ACT.Sigmoid) \
                                .then_inc(sem("act_step"), E.up())
                    f(hb[:, t, WL0:WL0 + 64], hb[:, t, WL0:WL0 + 64], ACT.Tanh) \
                        .then_inc(sem("lora_ready"), E.up("lora_ready"))
                    skip("unit_full", 4)
                    act.wait_ge(sem("pre_sig"), E.due("pre_sig"))
                    f(w_t[:, 0], w_t[:, 0], ACT.Sigmoid).then_inc(sem("act_step"), E.up())
                    f(w_t4, w_t4, ACT.Sigmoid).then_inc(sem("sig_ready"), E.up("sig_ready"))
                    root(B_H)
                    banks = [take("unit_full") for _ in range(3)]
                    act.wait_ge(sem("einv_go"), E.due("einv_go"))
                    for half in range(2):
                        ins = f(w_t[:, 2, half * CH:(half + 1) * CH], banks[half][:, :], ACT.Exp, scale=DECAY)
                        ins.then_inc(sem("einv_ready"), E.up("einv_ready"))
                    act.wait_ge(sem("einc_go"), E.due("einc_go"))
                    for half in range(2):
                        f(w_t[:, 2, half * CH:(half + 1) * CH], banks[half][:, :], ACT.Exp, scale=-DECAY) \
                            .then_inc(sem("act_free"), E.up("act_free"))
                    f(w_pc[:, :, t * 4:t * 4 + 4], banks[2][:, 0:32].rearrange("p (h c) -> p h c", c=4), ACT.Exp,
                            scale=-DECAY).then_inc(sem("act_free"), E.up("act_free"))
                    f(w_t[:, 0], w_t[:, 0], ACT.Exp, scale=-DECAY).then_inc(sem("eexc_ready"), E.up("eexc_ready"))
                act.wait_ge(sem("kbv_out"), E.due("kbv_out", 16 * 6 * TT))
                for t in range(TT):
                    for half in range(2):
                        f(hb[:, t, K0 + half * CH:K0 + (half + 1) * CH], take("unit_full")[:, :], ACT.Copy) \
                            .then_inc(sem("act_free"), E.up("act_free"))
                act.wait_ge(E.last_sem(), E.last_count())
                act.nop().then_inc(sem("gate_ready"), E.count("gate_ready"))
                skip("unit_full", 2 * NRC)
                for c in range(NRC):
                    skip("unit_full", 8)
                    if c >= 2:
                        act.wait_ge(sem(f"o_out{c % 2}"), E.due(f"o_out{c % 2}", 32))
                    banks = [take("unit_full") for _ in range(2)]
                    for o in range(2):
                        ts = slice(64 * o, 64 * o + RC)
                        f(w_o[ts, c % 2], banks[o][ts, :], ACT.Copy).then_inc(sem("act_free"), E.up("act_free"))
                    act.wait_ge(E.last_sem(), E.last_count())
                    act.nop().then_inc(sem("o_ready"), E.count("o_ready"))
                    if c < NRC - 1:
                        skip("unit_full", 2)
                root(2 * B_H)
                skip("gemm_full", g_out.n * g_out.tiles)

            def xat(l):
                g_q, g_kv, g_o = gemms[f"xat{l}"]
                act.wait_ge(sem("x_ready"), E.due("x_ready"))
                square_sums(lambda t: x4[:, t], lambda t: xn2[:, t], TT, 1)
                unrolled(g_q, lambda c, cs, t, bank: f(xa_q[:, t], bank, ACT.Copy) \
                    .then_inc(sem("act_free"), E.up("act_free")))
                act.wait_ge(sem("mem_in"), E.due("mem_in", 16))
                square_sums(lambda t: memb[:, t], lambda t: xn2[:, t], TT, 1)
                unrolled(g_kv, lambda c, cs, t, bank: f(xa_kv[:, t, c * CH:(c + 1) * CH], bank, ACT.Copy) \
                    .then_inc(sem("act_free"), E.up("act_free")))
                act.wait_ge(E.last_sem(), E.last_count())
                act.nop().then_inc(sem("xqk_ready"), E.count("xqk_ready"))
                attend(xat_units())
                skip("gemm_full", g_o.n * g_o.tiles)

            def ffn(l):
                g_up, g_down = gemms[f"ffn{l}"]
                act.wait_ge(sem("x_ready"), E.due("x_ready"))
                square_sums(lambda t: x4[:, t], lambda t: xn2[:, t], TT, 1)

                def relu2(c, cs, t, bank):
                    dst = HID[c % 2][:, t]
                    f(dst, bank, ACT.Relu).then_inc(sem("act_free"), E.up("act_free"))
                    act.wait_ge(E.last_sem(), E.last_count())
                    f(dst, dst, ACT.Square).then_inc(sem("sq_ready"), E.up("sq_ready"))

                evac(g_up, relu2)
                skip("gemm_full", g_down.n * g_down.tiles)

            def odd():
                g_in, g_glu, g_out = gemms["odd"]
                act.wait_ge(sem("x_ready"), E.due("x_ready"))
                square_sums(lambda t: x4[:, t], lambda t: xn2[:, t], TT, 1)
                evac(g_in, copy_to(s_u))
                act.wait_ge(E.last_sem(), E.last_count())
                act.nop().then_inc(sem("s_u_ready"), E.count("s_u_ready"))
                act.wait_ge(sem("s5_ang"), E.due("s5_ang"))
                f(s_lam[:, 2], s_lam[:, 2], ACT.Exp).then_inc(sem("s5_dt"), E.up("s5_dt"))
                act.wait_ge(sem("s5_ang"), E.due("s5_ang"))
                f(s_lam[:, 3], s_lam[:, 3], ACT.Exp).then_inc(sem("act_step"), E.up())
                f(s_lam[:, 5], s_lam[:, 5], ACT.Sin).then_inc(sem("act_step"), E.up())
                f(s_lam[:, 6], s_lam[:, 6], ACT.Sin).then_inc(sem("s5_trig"), E.up("s5_trig"))
                NB = SEQ // S5_STEP
                for b in range(NB + 1):
                    if b < NB:
                        if b == 1:
                            act.wait_ge(sem("bc_ready"), E.due("bc_ready"))
                        for kq in range(2):
                            for j in range(4):
                                bank = take("unit_full")
                                dst = s_h[b % 2].rearrange("p t r (k j) -> p j k r t", j=4)[:, j, kq * 8:kq * 8 + 8]
                                f(dst, bank[:, :].rearrange("p (k r t) -> p k r t", r=2, t=S5_STEP), ACT.Copy) \
                                    .then_inc(sem("act_free"), E.up("act_free"))
                        act.wait_ge(E.last_sem(), E.last_count())
                        act.nop().then_inc(sem("bu_ready"), E.count("bu_ready"))
                    if b:
                        skip("unit_full", 1)
                        act.wait_ge(sem("y_ready_s5"), E.due("y_ready_s5"))
                        f(s_zt[:, :, (b - 1) * S5_STEP:b * S5_STEP],
                                stage[:, (b - 1) % 2].rearrange("p (k t) -> p k t", t=S5_STEP), ACT.Gelu_apprx_tanh) \
                                    .then_inc(sem("act_step"), E.up())
                act.wait_ge(E.last_sem(), E.last_count())
                act.nop().then_inc(sem("z_done"), E.count("z_done"))
                evac(g_glu, copy_to(s_sig))
                act.wait_ge(E.last_sem(), E.last_count())
                act.nop().then_inc(sem("sig_full"), E.count("sig_full"))
                act.wait_ge(sem("pre_gate"), E.due("pre_gate"))
                for k in range(0, KT, 4):
                    f(s_pre[:, k:k + 4], s_pre[:, k:k + 4], ACT.Sigmoid).then_inc(sem("gate_sig"), E.up("gate_sig"))
                skip("gemm_full", g_out.n * g_out.tiles)

            for l in range(2):
                if f"b1_{l}" in stages:
                    block1(l)
            if "even" in stages:
                even()
            for l in range(2):
                if l == 1 and "odd" in stages:
                    odd()
                if f"xat{l}" in stages:
                    xat(l)
                if f"ffn{l}" in stages:
                    ffn(l)
            if "final" in stages:
                act.wait_ge(sem("x_ready"), E.due("x_ready"))
                square_sums(lambda t: x4[:, t], lambda t: xn2[:, t], TT, 1)
            if dbg is not None:
                act.wait_ge(E.last_sem(), E.last_count())
                act.nop().then_inc(sem("all_done"), E.count("all_done"))

        @block.vector
        def _(dve):
            E = Eng(dve, sem, "dve_step")
            g_n, t_n = 0, 0

            def take(name):
                nonlocal g_n
                dve.wait_ge(sem(name), E.due(name))
                g_n += 1
                return acc[(g_n - 1) % 4][:, :]

            def skip(name, k):
                nonlocal g_n
                E.seen[name] += k
                g_n += k

            def turned():
                nonlocal t_n
                dve.wait_ge(sem("tp_full"), E.due("tp_full"))
                t_n += 1
                return tp[(t_n - 1) % 4]

            tt, stt = dve.tensor_tensor, dve.scalar_tensor_tensor

            def ts(out, a, s1, s2, op0, op1=None):
                return dve.tensor_scalar(out, a, s1, s2, op0, op1) if op1 is not None else dve.tensor_scalar(out, a, s1, s2, op0)

            def along(v, n):
                return v.unsqueeze(2).to_broadcast([v.shape[0], v.shape[1], n])

            def over(v, k):
                return v.unsqueeze(1).to_broadcast([v.shape[0], k, v.shape[1]])

            def blocks(v, d):
                return v.rearrange("p (h d) -> p h d", d=d)

            def norm(src, dst, tiles, name="src_ready"):
                dve.wait_ge(sem("sd_ready"), E.due("sd_ready"))
                dve.reciprocal(stat2[:, 0:tiles], stat2[:, 0:tiles]).then_inc(sem("dve_step"), E.up())
                dve.wait_ge(E.last_sem(), E.last_count())
                for t in range(tiles):
                    ts(dst(t), src(t), stat2[:, t:t + 1], None, ALU.mult).then_inc(sem(name), E.up(name))

            def turn_evac(dst, tiles, width, scale=None, shift=None):
                for t in range(tiles):
                    for k in range(0, width // P, 4):
                        n = min(4, width // P - k)
                        bank = turned()[:, 0:n * P].rearrange("p (k t) -> p k t", t=P)
                        d = dst[:, k:k + n, t * P:(t + 1) * P]
                        if scale is None:
                            dve.tensor_copy(d, bank).then_inc(sem("tp_free"), E.up("tp_free"))
                        else:
                            tt(d, bank, along(scale(t)[:, k:k + n], P), ALU.mult).then_inc(sem("tp_free"), E.up("tp_free"))
                        if shift is not None:
                            dve.wait_ge(E.last_sem(), E.last_count())
                            tt(d, d, along(shift(t)[:, k:k + n], P), ALU.add).then_inc(sem("dve_step"), E.up())
                dve.wait_ge(E.last_sem(), E.last_count())
                dve.nop().then_inc(sem("feat_ready"), E.count("feat_ready"))

            def residual(g):
                for c in range(g.n):
                    for t in range(g.tiles):
                        bank = take("gemm_full")
                        x = x4[:, t, c * CH:(c + 1) * CH]
                        tt(x, x, bank[:, :], ALU.add).then_inc(sem("dve_free"), E.up("dve_free"))
                dve.wait_ge(E.last_sem(), E.last_count())
                dve.nop().then_inc(sem("x_ready"), E.count("x_ready"))

            def means(out, src, heads, d, sq):
                tt(sq, src, src, ALU.mult).then_inc(sem("dve_step"), E.up())
                dve.wait_ge(E.last_sem(), E.last_count())
                dve.tensor_reduce(out, blocks(sq, d), AX, ALU.add).then_inc(sem("dve_step"), E.up())

            def attend(units):
                nonlocal g_n
                n = len(units)
                pending = {}
                for i in range(n + 2):
                    if i < n:
                        u, s = units[i], i % 2
                        nk = u["k"].shape[-1]
                        if u["bias"] is None:
                            dve.wait_ge(sem("score_full"), E.due("score_full"))
                            bank = acc[g_n % 4]
                            g_n += 1
                            dve.tensor_reduce(att_s[:, 4 + s:5 + s], bank[:, 0:nk], AX, ALU.max) \
                                .then_inc(sem("dve_step"), E.up())
                            dve.wait_ge(E.last_sem(), E.last_count())
                            ts(att_s[:, s:s + 1], att_s[:, 4 + s:5 + s], -HD ** -0.5, None, ALU.mult) \
                                .then_inc(sem("nmax_ready"), E.up("nmax_ready"))
                        else:
                            bank = take("score_full")
                            stt(prob[:, s, 0:nk], bank[:, 0:nk], HD ** -0.5, u["bias"], ALU.mult, ALU.add) \
                                .then_inc(sem("dve_free"), E.up("dve_free"))
                            dve.wait_ge(E.last_sem(), E.last_count())
                            dve.tensor_reduce(att_s[:, 4 + s:5 + s], prob[:, s, 0:nk], AX, ALU.max) \
                                .then_inc(sem("dve_step"), E.up())
                            dve.wait_ge(E.last_sem(), E.last_count())
                            ts(att_s[:, s:s + 1], att_s[:, 4 + s:5 + s], -1.0, None, ALU.mult) \
                                .then_inc(sem("nmax_ready"), E.up("nmax_ready"))
                    if 0 <= i - 1 < n:
                        u = units[i - 1]
                        w = len(u["v"])
                        dve.tensor_copy(prob_t[:, (i - 1) % 2, 0:w, :],
                                              turned()[:, 0:w * P].rearrange("p (k t) -> p k t", t=P)) \
                                                  .then_inc(sem("tp_free"), E.up("tp_free"))
                        dve.wait_ge(E.last_sem(), E.last_count())
                        dve.reciprocal(att_s[:, 6 + (i - 1) % 2:7 + (i - 1) % 2], att_s[:, 2 + (i - 1) % 2:3 + (i - 1) % 2]) \
                            .then_inc(sem("dve_step"), E.up())
                    if i >= 2:
                        u, s = units[i - 2], i % 2
                        bank = take("pv_full")
                        dve.wait_ge(E.last_sem(), E.last_count())
                        if u["gated"]:
                            stt(u["out"], bank[:, 0:HD], att_s[:, 6 + s:7 + s], u["out"], ALU.mult, ALU.mult) \
                                .then_inc(sem("dve_free"), E.up("dve_free"))
                        else:
                            ts(u["out"], bank[:, 0:HD], att_s[:, 6 + s:7 + s], None, ALU.mult) \
                                .then_inc(sem("dve_free"), E.up("dve_free"))
                dve.wait_ge(E.last_sem(), E.last_count())

            def wrap(ang, r, rc):
                c1, c2, c3 = cody_waite()
                magic = 12582912.0
                top = 3.1415925
                ts(rc, ang, 1.0 / TWO_PI, magic, ALU.mult, ALU.add).then_inc(sem("dve_step"), E.up())
                dve.wait_ge(E.last_sem(), E.last_count())
                ts(rc, rc, -magic, None, ALU.add).then_inc(sem("dve_step"), E.up())
                dve.wait_ge(E.last_sem(), E.last_count())
                stt(r, rc, -c1, ang, ALU.mult, ALU.add).then_inc(sem("dve_step"), E.up())
                for c in (c2, c3):
                    dve.wait_ge(E.last_sem(), E.last_count())
                    stt(r, rc, -c, r, ALU.mult, ALU.add).then_inc(sem("dve_step"), E.up())
                dve.wait_ge(E.last_sem(), E.last_count())
                ts(rc, r, TWO_PI / 4, TWO_PI / 2, ALU.add, ALU.is_gt).then_inc(sem("dve_step"), E.up())
                dve.wait_ge(E.last_sem(), E.last_count())
                ts(rc, rc, -TWO_PI, TWO_PI / 4, ALU.mult, ALU.add).then_inc(sem("dve_step"), E.up())
                dve.wait_ge(E.last_sem(), E.last_count())
                tt(rc, rc, r, ALU.add).then_inc(sem("dve_step"), E.up())
                dve.wait_ge(E.last_sem(), E.last_count())
                for v in (r, rc):
                    ts(v, v, top, -top, ALU.min, ALU.max).then_inc(sem("dve_step"), E.up())

            if "load" in stages:
                dve.memset(eps[:, 0:1], 1e-6).then_inc(sem("dve_step"), E.up())
                dve.memset(eps[:, 1:2], 1e-5).then_inc(sem("dve_step"), E.up())
                dve.memset(eps[:, 2:3], 64e-5).then_inc(sem("dve_step"), E.up())
                dve.wait_ge(sem("consts"), 16 * CONSTS)
                tt(posi[:, :], tokid[:, :], frame[:, 0:1].to_broadcast([P, TT]), ALU.add).then_inc(sem("dve_step"), E.up())
                dve.wait_ge(E.last_sem(), E.last_count())
                dve.tensor_copy(stat[:, 0:TT], posi[:, :]).then_inc(sem("dve_step"), E.up())
                dve.wait_ge(E.last_sem(), E.last_count())
                for t in range(TT):
                    ts(angle[:, 2, 24 * t:24 * t + 24], invf[:, :], stat[:, t:t + 1], None, ALU.mult) \
                        .then_inc(sem("dve_step"), E.up())
                dve.wait_ge(E.last_sem(), E.last_count())
                for t in range(TT):
                    wrap(angle[:, 2, 24 * t:24 * t + 24], angle[:, t, 24:48], angle[:, t, 0:24])
                dve.wait_ge(E.last_sem(), E.last_count())
                dve.nop().then_inc(sem("trig_args"), E.count("trig_args"))
                dve.tensor_copy(cols1[:, :], turned()[:, 0:P]).then_inc(sem("tp_free"), E.up("tp_free"))
                dve.tensor_copy(cols2[:, 0:116], turned()[:, 0:116]).then_inc(sem("tp_free"), E.up("tp_free"))
                dve.wait_ge(E.last_sem(), E.last_count())
                dve.nop().then_inc(sem("cols_ready"), E.count("cols_ready"))
            if "mod" in stages:
                for g in gemms["mod"]:
                    skip("gemm_full", g.n)
                dve.wait_ge(sem("mod_in"), 16 * 8)
                tt(rows3, rows3, rows3b, ALU.add).then_inc(sem("src_ready"), E.up("src_ready"))
                bank = turned()
                for l in range(2):
                    for c in range(2):
                        at = (l * 2 + c) * 32
                        dve.tensor_copy(mod_col(l, c, 0), bank[:, at:at + KT]).then_inc(sem("dve_step"), E.up())
                        stt(mod_col(l, c, 1), bank[:, at + KT:at + 2 * KT], 1.0, col(f"norm_w{l}"), ALU.add, ALU.mult) \
                            .then_inc(sem("tp_free" if (l, c) == (1, 1) else "dve_step"), E.up("tp_free" if (l, c) == (1, 1) else "dve_step"))
                dve.wait_ge(E.last_sem(), E.last_count())
                dve.nop().then_inc(sem("mod_cols"), E.count("mod_cols"))

            def block1(l):
                g_in, g_kv, g_zb, g_out = gemms[f"b1_{l}"]
                tiles = g_out.tiles
                norm(lambda t: x4[:, t], lambda t: mix[:, t], 4)
                turn_evac(feat4, 4, D, lambda t: mod_col(l, t // 2, 1), lambda t: mod_col(l, t // 2, 0))
                for c in (4, 5):
                    for t in range(tiles):
                        dve.wait_ge(sem("za_ready"), E.due("za_ready"))
                        m = mix[:, t, (c - 4) * CH:(c - 3) * CH]
                        tt(m, m, stage[:, ((c - 4) * tiles + t) % 2], ALU.mult).then_inc(sem("za_used"), E.up("za_used"))
                for g in (g_in, g_kv, g_zb):
                    skip("gemm_full", g.n * g.tiles)
                dve.wait_ge(sem("proj_done"), E.due("proj_done"))
                sq = prob[:, :, :].rearrange("p a b -> p (a b)")
                for t in range(4):
                    if t < tiles:
                        means(stat[:, t * 8:t * 8 + 8], vb[:, t], 8, HD, sq)
                        dve.wait_ge(E.last_sem(), E.last_count())
                        means(stat[:, 32 + t * 8:40 + t * 8], qb[:, t], 8, HD, sq)
                        dve.wait_ge(E.last_sem(), E.last_count())
                    means(stat[:, 64 + t * 2:66 + t * 2], kvb[:, t, 0:256], 2, HD, sq[:, 0:256])
                    dve.wait_ge(E.last_sem(), E.last_count())
                ts(stat[:, 0:72], stat[:, 0:72], 1.0 / HD, 1e-6, ALU.mult, ALU.add) \
                    .then_inc(sem("ms_ready"), E.up("ms_ready"))
                dve.wait_ge(sem("sd_ready"), E.due("sd_ready"))
                dve.reciprocal(stat2[:, 0:72], stat2[:, 0:72]).then_inc(sem("dve_step"), E.up())
                dve.wait_ge(sem("sgu_in"), E.due("sgu_in", 32))
                dve.wait_ge(E.last_sem(), E.last_count())
                for t in range(tiles):
                    v = blocks(vb[:, t], HD)
                    tt(v, v, along(stat2[:, t * 8:t * 8 + 8], HD), ALU.mult).then_inc(sem("dve_step"), E.up())
                    dve.wait_ge(E.last_sem(), E.last_count())
                    tt(vb[:, t], vb[:, t], vnw_row, ALU.mult).then_inc(sem("vn_ready"), E.up("vn_ready"))
                for h in range(2):
                    dve.tensor_copy(sgu_t[:, h * 4:h * 4 + 4], turned()[:, :].rearrange("p (k t) -> p k t", t=P)) \
                        .then_inc(sem("tp_free"), E.up("tp_free"))
                dve.wait_ge(E.last_sem(), E.last_count())
                dve.nop().then_inc(sem("sgu_t_ready"), E.count("sgu_t_ready"))
                for t in range(tiles):
                    for half in range(2):
                        bank = take("unit_full")
                        for j in range(4):
                            g = half * 4 + j
                            m = mix[:, t, g * P:(g + 1) * P]
                            stt(m, bank[:, j * P:(j + 1) * P], col(f"b_sgu{l}", 8)[:, g:g + 1], m, ALU.add, ALU.mult) \
                                .then_inc(sem("dve_free" if j == 3 else "dve_step"), E.up("dve_free" if j == 3 else "dve_step"))
                for t in range(4):
                    q, k = blocks(qb[:, t], HD), blocks(kvb[:, t, 0:256], HD)
                    parts = [(k, 2, stat2[:, 64 + t * 2:66 + t * 2], 1)]
                    if t < tiles:
                        parts.append((q, 8, stat2[:, 32 + t * 8:40 + t * 8], 0))
                    for v, n, r, w in parts:
                        tt(v, v, along(r, HD), ALU.mult).then_inc(sem("dve_step"), E.up())
                        dve.wait_ge(E.last_sem(), E.last_count())
                        tt(v, v, over(qk_w[:, l, w], n), ALU.mult).then_inc(sem("dve_step"), E.up())
                        dve.wait_ge(E.last_sem(), E.last_count())
                        if t < TT:
                            rot = sq[:, 0:n * HD]
                            for a in range(2):
                                half = lambda z, x: z.rearrange("p h (r a d) -> p h r a d", r=2, a=2)[:, :, :, x, :]
                                sin = rope[:, 1, t].rearrange("p (r a d) -> p r a d", r=2, a=2)[:, :, a, :]
                                for hh in range(2):
                                    pick = lambda z, x: z.rearrange("p h (r a d) -> p h r a d", r=2, a=2)[:, :, hh, x, :]
                                    tt(pick(blocks(rot, HD), a), pick(v, 1 - a), over(sin[:, hh], n), ALU.mult) \
                                        .then_inc(sem("dve_step"), E.up())
                            dve.wait_ge(E.last_sem(), E.last_count())
                            tt(v, v, over(rope[:, 0, t], n), ALU.mult).then_inc(sem("dve_step"), E.up())
                            dve.wait_ge(E.last_sem(), E.last_count())
                            tt(v, v, blocks(rot, HD), ALU.add).then_inc(sem("dve_step"), E.up())
                            dve.wait_ge(E.last_sem(), E.last_count())
                    dve.wait_ge(E.last_sem(), E.last_count())
                    dve.nop().then_inc(sem("qk_ready"), E.count("qk_ready"))
                for t in range(4):
                    if t < tiles:
                        for h in range(2):
                            dve.tensor_copy(q_t[:, h * 4:h * 4 + 4, t * P:(t + 1) * P],
                                                  turned()[:, :].rearrange("p (k t) -> p k t", t=P)) \
                                                      .then_inc(sem("tp_free"), E.up("tp_free"))
                    dve.tensor_copy(k_t[:, :, t * P:(t + 1) * P],
                                          turned()[:, 0:2 * P].rearrange("p (k t) -> p k t", t=P)) \
                                              .then_inc(sem("tp_free"), E.up("tp_free"))
                dve.wait_ge(E.last_sem(), E.last_count())
                dve.nop().then_inc(sem("qkt_ready"), E.count("qkt_ready"))
                attend(b1_units(l))
                dve.wait_ge(E.last_sem(), E.last_count())
                dve.nop().then_inc(sem("att_done"), E.count("att_done"))
                for t in range(tiles):
                    dve.nop().then_inc(sem("src_ready"), E.up("src_ready"))
                turn_evac(feat4, tiles, D)
                dve.wait_ge(sem("gate_in"), E.due("gate_in", 64 if l == 0 else 48))
                for c in range(2):
                    tt(gate[:, c], gate[:, c], gate_b, ALU.add).then_inc(sem("dve_step"), E.up())
                dve.wait_ge(E.last_sem(), E.last_count())
                n = 0
                for c in range(g_out.n):
                    for t in range(tiles):
                        bank = take("gemm_full")
                        cs = slice(c * CH, (c + 1) * CH)
                        tt(stage[:, n % 2], bank[:, :], gate[:, t // 2, cs], ALU.mult) \
                            .then_inc(sem("dve_free"), E.up("dve_free"))
                        dve.wait_ge(E.last_sem(), E.last_count())
                        tt(x4[:, t, cs], x4[:, t, cs], stage[:, n % 2], ALU.add).then_inc(sem("dve_step"), E.up())
                        n += 1
                dve.wait_ge(E.last_sem(), E.last_count())
                dve.nop().then_inc(sem("x_ready"), E.count("x_ready"))

            def rotate(v1, v2, cos, sin, tmp, n, d):
                q = [tmp[:, j * n * d:(j + 1) * n * d].rearrange("p (h d) -> p h d", d=d) for j in range(4)]
                tt(q[0], v1, over(cos, n), ALU.mult).then_inc(sem("dve_step"), E.up())
                tt(q[1], v2, over(sin, n), ALU.mult).then_inc(sem("dve_step"), E.up())
                tt(q[2], v2, over(cos, n), ALU.mult).then_inc(sem("dve_step"), E.up())
                tt(q[3], v1, over(sin, n), ALU.mult).then_inc(sem("dve_step"), E.up())
                dve.wait_ge(E.last_sem(), E.last_count())
                tt(v1, q[0], q[1], ALU.subtract).then_inc(sem("dve_step"), E.up())
                tt(v2, q[2], q[3], ALU.add).then_inc(sem("dve_step"), E.up())
                dve.wait_ge(E.last_sem(), E.last_count())

            def even():
                g_in, g_uq, g_qi, g_uv, g_out = gemms["even"]
                norm(lambda t: x4[:, t], lambda t: xn2[:, t], TT)
                dve.wait_ge(E.last_sem(), E.last_count())
                dve.nop().then_inc(sem("x_norm_even"), E.count("x_norm_even"))
                turn_evac(feat_e, TT, D, lambda t: col("norm_mix0"))
                skip("gemm_full", g_in.n * g_in.tiles)
                dve.wait_ge(sem("even_h"), E.due("even_h"))
                dve.wait_ge(sem("x_out"), E.due("x_out", 16))
                dve.memset(d_uk[:, :, :, 0:32], 0.0).then_inc(sem("dve_step"), E.up())
                dve.memset(d_kit, 0.0).then_inc(sem("dve_step"), E.up())
                dve.wait_ge(E.last_sem(), E.last_count())
                dve.nop().then_inc(sem("uk_zero"), E.count("uk_zero"))
                for t in range(TT):
                    for j, (c0, cw) in enumerate(((0, 512), (512, 256), (800, 64))):
                        v = hb[:, t, c0:c0 + cw]
                        tt(d_tmp[:, 0:cw], v, v, ALU.mult).then_inc(sem("dve_step"), E.up())
                        dve.wait_ge(E.last_sem(), E.last_count())
                        s = stat[:, 3 * t + j:3 * t + j + 1]
                        dve.tensor_reduce(s, d_tmp[:, 0:cw], AX, ALU.add).then_inc(sem("dve_step"), E.up())
                        dve.wait_ge(E.last_sem(), E.last_count())
                        ts(s, s, 1.0 / cw, 1e-5, ALU.mult, ALU.add).then_inc(sem("dve_step"), E.up())
                dve.wait_ge(E.last_sem(), E.last_count())
                dve.nop().then_inc(sem("ms_ready"), E.count("ms_ready"))
                dve.wait_ge(sem("sd_ready"), E.due("sd_ready"))
                dve.reciprocal(stat2[:, 0:6], stat2[:, 0:6]).then_inc(sem("dve_step"), E.up())
                dve.wait_ge(sem("trig_ready"), E.due("trig_ready"))
                dve.wait_ge(sem("dsa_in"), E.due("dsa_in", 64))
                dve.wait_ge(E.last_sem(), E.last_count())
                for t in range(TT):
                    for j, (c0, cw) in enumerate(((0, 512), (512, 256), (800, 64))):
                        v = hb[:, t, c0:c0 + cw]
                        dst = v if j < 2 else d_kid[:, t, 0:64]
                        ts(dst, v, stat2[:, 3 * t + j:3 * t + j + 1], None, ALU.mult).then_inc(sem("dve_step"), E.up())
                        if j:
                            dve.wait_ge(E.last_sem(), E.last_count())
                            tt(dst, dst, d_ckw if j == 1 else d_kiw, ALU.mult).then_inc(sem("dve_step"), E.up())
                    ts(hb[:, t, 864:880], hb[:, t, 864:880], 0.25 * 0.125, None, ALU.mult).then_inc(sem("dve_step"), E.up())
                    dve.wait_ge(E.last_sem(), E.last_count())
                    rotate(hb[:, t, 768:784].unsqueeze(1), hb[:, t, 784:800].unsqueeze(1),
                           trig[:, t, 0:16], trig[:, t, 24:40], d_tmp, 1, 16)
                    rotate(d_kid[:, t, 0:8].unsqueeze(1), d_kid[:, t, 8:16].unsqueeze(1),
                           trig[:, t, 16:24], trig[:, t, 40:48], d_tmp, 1, 8)
                    dve.tensor_copy(d_kid[:, t, 64:128], d_kid[:, t, 0:64]).then_inc(sem("dve_step"), E.up())
                dve.wait_ge(E.last_sem(), E.last_count())
                dve.nop().then_inc(sem("lat_ready"), E.count("lat_ready"))
                for t in range(TT):
                    cs = slice(t * P, (t + 1) * P)
                    sq = lambda b, n: b[:, 0:n * P].rearrange("p (k t) -> p k t", t=P)
                    tt(d_cqt[:, :, cs], sq(turned(), 4), along(col("cq", 4), P), ALU.mult) \
                        .then_inc(sem("tp_free"), E.up("tp_free"))
                    dve.tensor_copy(d_ckt[:, :, cs], sq(turned(), 2)).then_inc(sem("tp_free"), E.up("tp_free"))
                    bank = turned()
                    dve.tensor_copy(d_kit[0:64, t * P:(t + 1) * P], bank[0:64, 0:P]).then_inc(sem("dve_step"), E.up())
                    dve.tensor_copy(d_kit[64:128, SEQ + t * P:SEQ + (t + 1) * P], bank[64:128, 0:P]) \
                        .then_inc(sem("dve_step"), E.up())
                    dve.tensor_copy(d_krt[0:32, cs], bank[0:32, P:2 * P]).then_inc(sem("tp_free"), E.up("tp_free"))
                dve.wait_ge(E.last_sem(), E.last_count())
                dve.nop().then_inc(sem("lat_t_ready"), E.count("lat_t_ready"))
                for g in (g_uq, g_qi, g_uv):
                    skip("gemm_full", g.n * g.tiles)
                skip("unit_full", 8)
                dve.wait_ge(sem("dsa_proj"), E.due("dsa_proj"))
                for t in range(TT):
                    q = blocks(d_q[:, t], HD)
                    rotate(q[:, :, 0:16], q[:, :, 16:32], trig[:, t, 0:16], trig[:, t, 24:40], d_tmp, 8, 16)
                    q = blocks(d_qi[:, t], 64)
                    rotate(q[:, :, 0:8], q[:, :, 8:16], trig[:, t, 16:24], trig[:, t, 40:48], d_tmp, 16, 8)
                    dve.wait_ge(E.last_sem(), E.last_count())
                    dve.nop().then_inc(sem("dq_ready"), E.count("dq_ready"))
                    for dst in (d_qt, d_qit):
                        for h in range(2):
                            dve.tensor_copy(dst[:, h * 4:h * 4 + 4, t * P:(t + 1) * P],
                                                  turned()[:, :].rearrange("p (k t) -> p k t", t=P)) \
                                                      .then_inc(sem("tp_free"), E.up("tp_free"))
                dve.wait_ge(E.last_sem(), E.last_count())
                dve.nop().then_inc(sem("dqt_ready"), E.count("dqt_ready"))
                slots = [stage[:, 0], stage[:, 1], prob[:, 0], prob[:, 1]]
                for t in range(TT):
                    score = d_score[:, t]
                    for hp in range(8):
                        dve.wait_ge(sem("rl_ready"), E.due("rl_ready"))
                        r = slots[(t * 8 + hp) % 4]
                        for o in range(2):
                            h = 2 * hp + o
                            w = hb[:, t, 864 + h:865 + h]
                            name = "rl_used" if o else "dve_step"
                            if h == 0:
                                ts(score, r[:, 0:SEQ], w, None, ALU.mult).then_inc(sem("dve_step"), E.up())
                            else:
                                stt(score, r[:, o * SEQ:(o + 1) * SEQ], w, score, ALU.mult, ALU.add) \
                                    .then_inc(sem(name), E.up(name))
                            dve.wait_ge(E.last_sem(), E.last_count())
                    for half in range(2):
                        limit = (2 * t + half + 1) * 64
                        if limit < SEQ:
                            dve.memset(d_score[64 * half:64 * half + 64, t, limit:], NEG).then_inc(sem("dve_step"), E.up())
                    dve.wait_ge(E.last_sem(), E.last_count())
                    work = d_work[:, t]
                    for r in range(8):
                        src = d_score[:, t] if r == 0 else work
                        dve.max(d_top, src).then_inc(sem("dve_step"), E.up())
                        dve.wait_ge(E.last_sem(), E.last_count())
                        dve.match_replace(out=work, in_to_replace=d_top, in_values=src, imm_value=TAKEN) \
                            .then_inc(sem("dve_step"), E.up())
                        dve.wait_ge(E.last_sem(), E.last_count())
                    ts(d_bias[:, t], work, TAKEN, None, ALU.is_equal).then_inc(sem("dve_step"), E.up())
                    dve.wait_ge(E.last_sem(), E.last_count())
                    ts(d_bias[:, t], d_bias[:, t], -1.0, 1e30, ALU.add, ALU.mult).then_inc(sem("dve_step"), E.up())
                skip("unit_full", 16)
                dve.wait_ge(E.last_sem(), E.last_count())
                dve.nop().then_inc(sem("bias_ready"), E.count("bias_ready"))
                attend(dsa_units())
                dve.wait_ge(E.last_sem(), E.last_count())
                dve.nop().then_inc(sem("dsa_done"), E.count("dsa_done"))
                rwkv()
                for t in range(TT):
                    for src in range(2):
                        for k in range(2):
                            at = src * 8 + k * 4
                            dve.tensor_copy(feat_e[:, at:at + 4, t * P:(t + 1) * P],
                                                  turned()[:, :].rearrange("p (k t) -> p k t", t=P)) \
                                                      .then_inc(sem("tp_free"), E.up("tp_free"))
                dve.wait_ge(E.last_sem(), E.last_count())
                dve.nop().then_inc(sem("feat_ready"), E.count("feat_ready"))
                dve.wait_ge(sem("x_back"), E.due("x_back", 16))
                residual(g_out)

            def rwkv():
                dve.memset(w_sh[0:1, 0], 0.0).then_inc(sem("dve_step"), E.up())
                dve.wait_ge(E.last_sem(), E.last_count())
                dve.nop().then_inc(sem("shift_zero"), E.count("shift_zero"))
                dve.wait_ge(sem("shift_in"), E.due("shift_in", 48))
                for half, (c0, cw) in enumerate(((0, 2048), (2048, 1312))):
                    dve.wait_ge(sem("mu_in"), E.due("mu_in", 16))
                    for t in range(TT):
                        h, s = hb[:, t, A_COLS + c0:A_COLS + c0 + cw], w_sh[:, t, c0:c0 + cw]
                        tt(s, s, h, ALU.subtract).then_inc(sem("dve_step"), E.up())
                        dve.wait_ge(E.last_sem(), E.last_count())
                        tt(s, s, w_mu[half], ALU.mult).then_inc(sem("dve_step"), E.up())
                        dve.wait_ge(E.last_sem(), E.last_count())
                        tt(h, h, s, ALU.add).then_inc(sem("dve_step"), E.up())
                    if half == 0:
                        dve.wait_ge(E.last_sem(), E.last_count())
                        dve.nop().then_inc(sem("mu_used"), E.count("mu_used"))
                dve.wait_ge(E.last_sem(), E.last_count())
                dve.nop().then_inc(sem("mix_done"), E.count("mix_done"))
                dve.wait_ge(sem("rwkv_in"), E.due("rwkv_in", 16 * 7))
                for t in range(TT):
                    T0, T1, T2, T4 = w_t[:, 0], w_t[:, 1], w_t[:, 2], w_t4
                    r, k, v = (hb[:, t, o:o + B_W] for o in (R0, K0, V0))
                    w0, a0, kk, ka, rk = (w_row[:, j] for j in range(5))
                    bank = turned()
                    dve.tensor_copy(w_lt[0:64, 0:2], bank[0:64, 0:2 * P].rearrange("p (k t) -> p k t", t=P)) \
                        .then_inc(sem("tp_free"), E.up("tp_free"))
                    dve.wait_ge(E.last_sem(), E.last_count())
                    dve.nop().then_inc(sem("lora_t"), E.count("lora_t"))
                    if t:
                        dve.wait_ge(sem("kbv_out"), E.due("kbv_out", 16 * 6))
                    for dst, b in ((T0, w0), (T4, a0)):
                        for half in range(2):
                            cs = slice(half * CH, (half + 1) * CH)
                            tt(dst[:, cs], take("unit_full")[:, :], b[:, cs], ALU.add) \
                                .then_inc(sem("dve_free"), E.up("dve_free"))
                    dve.wait_ge(E.last_sem(), E.last_count())
                    dve.nop().then_inc(sem("pre_sig"), E.count("pre_sig"))
                    tt(T1, k, kk, ALU.mult).then_inc(sem("dve_step"), E.up())
                    dve.wait_ge(E.last_sem(), E.last_count())
                    means(stat[:, 0:B_H], T1, B_H, B_D, T2)
                    dve.wait_ge(E.last_sem(), E.last_count())
                    ts(stat[:, 0:B_H], stat[:, 0:B_H], 1e-24, None, ALU.max).then_inc(sem("ms_ready"), E.up("ms_ready"))
                    dve.wait_ge(sem("sd_ready"), E.due("sd_ready"))
                    dve.reciprocal(stat2[:, 0:B_H], stat2[:, 0:B_H]).then_inc(sem("dve_step"), E.up())
                    dve.wait_ge(E.last_sem(), E.last_count())
                    tt(blocks(T1, B_D), blocks(T1, B_D), along(stat2[:, 0:B_H], B_D), ALU.mult) \
                        .then_inc(sem("dve_step"), E.up())
                    stt(T2, T4, -1.0, ka, ALU.add, ALU.mult).then_inc(sem("dve_step"), E.up())
                    dve.wait_ge(E.last_sem(), E.last_count())
                    stt(k, T2, 1.0, k, ALU.add, ALU.mult).then_inc(sem("dve_step"), E.up())
                    dve.wait_ge(E.last_sem(), E.last_count())
                    tt(T2, r, k, ALU.mult).then_inc(sem("dve_step"), E.up())
                    dve.wait_ge(E.last_sem(), E.last_count())
                    tt(T2, T2, rk, ALU.mult).then_inc(sem("dve_step"), E.up())
                    dve.wait_ge(E.last_sem(), E.last_count())
                    dve.tensor_reduce(w_bon[:, t], blocks(T2, B_D), AX, ALU.add).then_inc(sem("dve_step"), E.up())
                    tt(T4, T4, T1, ALU.mult).then_inc(sem("dve_step"), E.up())
                    dve.wait_ge(E.last_sem(), E.last_count())
                    dve.nop().then_inc(sem("einv_go"), E.count("einv_go"))
                    banks = [take("unit_full") for _ in range(3)]
                    dve.wait_ge(sem("einv_ready"), E.due("einv_ready", 2))
                    for half in range(2):
                        cs = slice(half * CH, (half + 1) * CH)
                        tt(T0[:, cs], banks[half][:, :], T0[:, cs], ALU.subtract).then_inc(sem("dve_step"), E.up())
                    tt(k, k, T2, ALU.mult).then_inc(sem("dve_step"), E.up())
                    tt(T4, T4, T2, ALU.mult).then_inc(sem("dve_step"), E.up())
                    dve.wait_ge(E.last_sem(), E.last_count())
                    dve.nop().then_inc(sem("einc_go"), E.count("einc_go"))
                    dve.wait_ge(sem("eexc_ready"), E.due("eexc_ready"))
                    tt(r, r, T2, ALU.mult).then_inc(sem("dve_step"), E.up())
                    tt(T1, T1, T0, ALU.mult).then_inc(sem("dve_step"), E.up())
                    dve.wait_ge(E.last_sem(), E.last_count())
                    dve.nop().then_inc(sem("arbk_ready"), E.count("arbk_ready"))
                    for dst, j in ((w_ar, 0), (w_ar, 1), (w_bk, 0), (w_bk, 1)):
                        for h in range(2):
                            bank = turned()[:, :].rearrange("p (h c t) -> p h c t", h=4, t=RC)
                            dve.tensor_copy(dst[:, h * 4:h * 4 + 4, t * 4:t * 4 + 4, j, :], bank) \
                                .then_inc(sem("tp_free"), E.up("tp_free"))
                dve.wait_ge(E.last_sem(), E.last_count())
                dve.nop().then_inc(sem("rows_done"), E.count("rows_done"))
                for t in range(TT):
                    bank = turned()
                    dve.tensor_copy(w_lt[:, 2], bank[:, 0:P]).then_inc(sem("dve_step"), E.up())
                    dve.tensor_copy(w_lt[0:32, 3], bank[0:32, P:2 * P]).then_inc(sem("tp_free"), E.up("tp_free"))
                    dve.wait_ge(E.last_sem(), E.last_count())
                    dve.nop().then_inc(sem("lora_t"), E.count("lora_t"))
                    skip("unit_full", 2)
                dve.wait_ge(sem("gate_ready"), E.due("gate_ready"))
                strict, upto = (lambda o, n: over(mask32[64 * o:64 * o + RC, 0:RC], n)), (lambda o, n: over(mask32[64 * o:64 * o + RC, RC:], n))
                for c in range(NRC):
                    if c >= 2:
                        dve.wait_ge(sem(f"a_out{c % 2}"), E.due(f"a_out{c % 2}", 32))
                    for o in range(2):
                        rs = slice(64 * o, 64 * o + RC)
                        bank = take("unit_full")
                        tt(blocks(w_a[rs, c % 2], RC), blocks(bank[rs, 0:8 * RC], RC), strict(o, 8), ALU.mult) \
                            .then_inc(sem("dve_free"), E.up("dve_free"))
                    dve.wait_ge(E.last_sem(), E.last_count())
                    dve.nop().then_inc(sem("a_ready"), E.count("a_ready"))
                dve.wait_ge(sem("solve_in"), E.due("solve_in", 16))
                flat_t = w_T.rearrange("p s t -> p (s t)")
                dve.memset(flat_t, 0.0).then_inc(sem("dve_step"), E.up())
                dve.wait_ge(E.last_sem(), E.last_count())
                dve.memset(flat_t[:, 0:RC * RC:RC + 1], 1.0).then_inc(sem("dve_step"), E.up())
                dve.wait_ge(E.last_sem(), E.last_count())
                for i in range(1, RC):
                    tt(w_tm[:, 0:i, 0:i], w_T[:, 0:i, 0:i], over(w_A[:, 0:i, i], i), ALU.mult) \
                        .then_inc(sem("dve_step"), E.up())
                    dve.wait_ge(E.last_sem(), E.last_count())
                    dve.tensor_reduce(w_T[:, 0:i, i], w_tm[:, 0:i, 0:i], AX, ALU.add, negate=True) \
                        .then_inc(sem("dve_step"), E.up())
                    dve.wait_ge(E.last_sem(), E.last_count())
                dve.wait_ge(E.last_sem(), E.last_count())
                dve.nop().then_inc(sem("solved"), E.count("solved"))
                for c in range(NRC):
                    rs = [slice(64 * o, 64 * o + RC) for o in range(2)]
                    for o in range(2):
                        bank = take("unit_full")[rs[o], :].rearrange("p (h a t) -> p h a t", a=2, t=RC)
                        for a, m in ((0, strict), (1, upto)):
                            tt(w_G[rs[o], :, 1 + a, :], bank[:, :, a, :], m(o, 8), ALU.mult) \
                                .then_inc(sem("dve_free" if a else "dve_step"), E.up("dve_free" if a else "dve_step"))
                    for o in range(2):
                        bank = take("unit_full")[rs[o], 0:8 * RC]
                        tt(w_G[rs[o], :, 0, :], blocks(bank, RC), upto(o, 8), ALU.mult) \
                            .then_inc(sem("dve_free"), E.up("dve_free"))
                    dve.wait_ge(E.last_sem(), E.last_count())
                    dve.nop().then_inc(sem("G_ready"), E.count("G_ready"))
                    for o in range(2):
                        dve.tensor_copy(w_z[rs[o]], take("unit_full")[rs[o], :]).then_inc(sem("dve_free"), E.up("dve_free"))
                    dve.wait_ge(E.last_sem(), E.last_count())
                    dve.nop().then_inc(sem("z_ready"), E.count("z_ready"))
                    for o in range(2):
                        ts(w_u[rs[o]], take("unit_full")[rs[o], :], -1.0, None, ALU.mult) \
                            .then_inc(sem("dve_free"), E.up("dve_free"))
                    dve.wait_ge(E.last_sem(), E.last_count())
                    dve.nop().then_inc(sem("u_ready"), E.count("u_ready"))
                    skip("unit_full", 2)
                    if c < NRC - 1:
                        for o in range(2):
                            ks = slice(64 * o, 64 * o + 64)
                            st = w_st[ks].rearrange("p h d -> p (h d)")
                            bank = take("unit_full")[ks, :]
                            if c == 0:
                                dve.tensor_copy(st, bank).then_inc(sem("dve_free"), E.up("dve_free"))
                            else:
                                tt(st, st, bank, ALU.add).then_inc(sem("dve_free"), E.up("dve_free"))
                        dve.wait_ge(E.last_sem(), E.last_count())
                        tt(w_st, w_st, along(w_pc[:, :, c], B_D), ALU.mult).then_inc(sem("dve_step"), E.up())
                        dve.wait_ge(E.last_sem(), E.last_count())
                        dve.nop().then_inc(sem("st_ready"), E.count("st_ready"))
                dve.wait_ge(sem("o_in"), E.due("o_in", 64))
                for t in range(TT):
                    o = hb[:, t, R0:R0 + B_W]
                    m = stat[:, t * B_H:(t + 1) * B_H]
                    dve.tensor_reduce(m, blocks(o, B_D), AX, ALU.add).then_inc(sem("dve_step"), E.up())
                    dve.wait_ge(E.last_sem(), E.last_count())
                    ts(m, m, 1.0 / B_D, None, ALU.mult).then_inc(sem("dve_step"), E.up())
                    dve.wait_ge(E.last_sem(), E.last_count())
                    tt(blocks(o, B_D), blocks(o, B_D), along(m, B_D), ALU.subtract).then_inc(sem("dve_step"), E.up())
                    dve.wait_ge(E.last_sem(), E.last_count())
                    means(m, o, B_H, B_D, w_t[:, 0])
                    dve.wait_ge(E.last_sem(), E.last_count())
                    ts(m, m, 1.0 / B_D, 64e-5, ALU.mult, ALU.add).then_inc(sem("dve_step"), E.up())
                    dve.wait_ge(E.last_sem(), E.last_count())
                dve.wait_ge(E.last_sem(), E.last_count())
                dve.nop().then_inc(sem("ms_ready"), E.count("ms_ready"))
                dve.wait_ge(sem("sd_ready"), E.due("sd_ready"))
                dve.reciprocal(stat2[:, 0:2 * B_H], stat2[:, 0:2 * B_H]).then_inc(sem("dve_step"), E.up())
                dve.wait_ge(E.last_sem(), E.last_count())
                for t in range(TT):
                    o, g, v = (hb[:, t, x:x + B_W] for x in (R0, K0, V0))
                    tt(blocks(w_t[:, 0], B_D), blocks(v, B_D), along(w_bon[:, t], B_D), ALU.mult) \
                        .then_inc(sem("dve_step"), E.up())
                    tt(blocks(o, B_D), blocks(o, B_D), along(stat2[:, t * B_H:(t + 1) * B_H], B_D), ALU.mult) \
                        .then_inc(sem("dve_step"), E.up())
                    dve.wait_ge(E.last_sem(), E.last_count())
                    tt(o, o, w_ln[:, 0], ALU.mult).then_inc(sem("dve_step"), E.up())
                    dve.wait_ge(E.last_sem(), E.last_count())
                    tt(o, o, w_ln[:, 1], ALU.add).then_inc(sem("dve_step"), E.up())
                    dve.wait_ge(E.last_sem(), E.last_count())
                    tt(o, o, w_t[:, 0], ALU.add).then_inc(sem("dve_step"), E.up())
                    dve.wait_ge(E.last_sem(), E.last_count())
                    tt(o, o, g, ALU.mult).then_inc(sem("src_ready"), E.up("src_ready"))
                    dve.wait_ge(E.last_sem(), E.last_count())
                dve.wait_ge(E.last_sem(), E.last_count())
                dve.nop().then_inc(sem("rwkv_done"), E.count("rwkv_done"))

            def xat(l):
                g_q, g_kv, g_o = gemms[f"xat{l}"]
                dve.wait_ge(E.last_sem(), E.last_count())
                dve.nop().then_inc(sem("mem_free"), E.count("mem_free"))
                norm(lambda t: x4[:, t], lambda t: xn2[:, t], TT)
                turn_evac(feat, TT, D, lambda t: col(f"norm_xattn{l}"))
                skip("gemm_full", g_q.n * g_q.tiles)
                norm(lambda t: memb[:, t], lambda t: memb[:, t], TT)
                turn_evac(feat, TT, D, lambda t: col(f"norm_mem{l}"))
                skip("gemm_full", g_kv.n * g_kv.tiles)
                for t in range(TT):
                    for dst in (xa_qt, xa_kt):
                        dve.tensor_copy(dst[:, :, t * P:(t + 1) * P],
                                              turned()[:, :].rearrange("p (k t) -> p k t", t=P)) \
                                                  .then_inc(sem("tp_free"), E.up("tp_free"))
                dve.wait_ge(E.last_sem(), E.last_count())
                dve.nop().then_inc(sem("qkt_ready"), E.count("qkt_ready"))
                attend(xat_units())
                for t in range(TT):
                    dve.nop().then_inc(sem("src_ready"), E.up("src_ready"))
                turn_evac(xa_ot, TT, 512)
                residual(g_o)

            def ffn(l):
                nonlocal t_n
                g_up, g_down = gemms[f"ffn{l}"]
                norm(lambda t: x4[:, t], lambda t: xn2[:, t], TT)
                turn_evac(feat, TT, D, lambda t: col(f"norm_ffn{l}"))

                def hidden(c, i):
                    at = 4 * (c - 1)
                    if not isinstance(i, int):
                        at = i * (4 * g_up.body) + at
                    for t in range(TT):
                        dve.tensor_copy(hid_t[:, bass.ds(at, 4), t * P:(t + 1) * P],
                                              turned()[:, :].rearrange("p (k t) -> p k t", t=P)) \
                                                  .then_inc(sem("tp_free"), E.up("tp_free"))

                per = g_up.body * TT
                with E.loop(g_up.turns, {"tp_full": per, "tp_free": per}) as i:
                    for b in range(g_up.body):
                        hidden(g_up.lead + b, i)
                t_n += per * (g_up.turns - 1)
                for c in range(g_up.tail, g_up.n + 1):
                    hidden(c, 0)
                skip("gemm_full", g_up.n * g_up.tiles)
                dve.wait_ge(E.last_sem(), E.last_count())
                dve.nop().then_inc(sem("feat_ready"), E.count("feat_ready"))
                residual(g_down)

            def odd():
                g_in, g_glu, g_out = gemms["odd"]
                norm(lambda t: x4[:, t], lambda t: xn2[:, t], TT)
                turn_evac(feat, TT, D, lambda t: col("norm_mix1"))
                skip("gemm_full", g_in.n * g_in.tiles)
                turn_evac(s_ut, TT, D)
                dve.wait_ge(E.last_sem(), E.last_count())
                dve.nop().then_inc(sem("s5_free"), E.count("s5_free"))
                dve.wait_ge(sem("s5_in"), E.due("s5_in", 16 * 7))
                lam = lambda j: s_lam[:, j]
                bank = turned()
                dve.tensor_copy(lam(0), bank[:, 0:PAIRS]).then_inc(sem("dve_step"), E.up())
                dve.tensor_copy(lam(1), bank[:, P:P + PAIRS]).then_inc(sem("tp_free"), E.up("tp_free"))
                for g in range(2):
                    rs = slice(64 * g, 64 * g + 64)
                    dve.tensor_copy(s_lam[rs, 2], s_ld[rs, g::2]).then_inc(sem("dve_step"), E.up())
                dve.wait_ge(E.last_sem(), E.last_count())
                ts(lam(0), lam(0), -1e-4, None, ALU.min).then_inc(sem("dve_step"), E.up())
                dve.wait_ge(E.last_sem(), E.last_count())
                dve.nop().then_inc(sem("s5_ang"), E.count("s5_ang"))
                dve.wait_ge(sem("s5_dt"), E.due("s5_dt"))
                tt(lam(3), lam(0), lam(2), ALU.mult).then_inc(sem("dve_step"), E.up())
                tt(lam(4), lam(1), lam(2), ALU.mult).then_inc(sem("dve_step"), E.up())
                dve.wait_ge(E.last_sem(), E.last_count())
                wrap(lam(4), lam(5), lam(6))
                dve.wait_ge(E.last_sem(), E.last_count())
                dve.nop().then_inc(sem("s5_ang"), E.count("s5_ang"))
                dve.wait_ge(sem("s5_trig"), E.due("s5_trig"))
                tt(lam(7), lam(3), lam(6), ALU.mult).then_inc(sem("dve_step"), E.up())
                tt(lam(8), lam(3), lam(5), ALU.mult).then_inc(sem("dve_step"), E.up())
                tt(lam(10), lam(0), lam(0), ALU.mult).then_inc(sem("dve_step"), E.up())
                tt(lam(11), lam(1), lam(1), ALU.mult).then_inc(sem("dve_step"), E.up())
                dve.wait_ge(E.last_sem(), E.last_count())
                tt(lam(10), lam(10), lam(11), ALU.add).then_inc(sem("dve_step"), E.up())
                ts(lam(9), lam(7), -1.0, None, ALU.add).then_inc(sem("dve_step"), E.up())
                dve.wait_ge(E.last_sem(), E.last_count())
                dve.reciprocal(lam(10), lam(10)).then_inc(sem("dve_step"), E.up())
                tt(lam(2), lam(9), lam(0), ALU.mult) \
                    .then_inc(sem("dve_step"), E.up())
                tt(lam(3), lam(8), lam(1), ALU.mult).then_inc(sem("dve_step"), E.up())
                tt(lam(5), lam(8), lam(0), ALU.mult).then_inc(sem("dve_step"), E.up())
                tt(lam(6), lam(9), lam(1), ALU.mult).then_inc(sem("dve_step"), E.up())
                dve.wait_ge(E.last_sem(), E.last_count())
                tt(lam(2), lam(2), lam(3), ALU.add).then_inc(sem("dve_step"), E.up())
                tt(lam(5), lam(5), lam(6), ALU.subtract).then_inc(sem("dve_step"), E.up())
                dve.wait_ge(E.last_sem(), E.last_count())
                tt(lam(2), lam(2), lam(10), ALU.mult).then_inc(sem("dve_step"), E.up())
                tt(lam(5), lam(5), lam(10), ALU.mult).then_inc(sem("dve_step"), E.up())
                for j in range(2):
                    dve.tensor_copy(s_l2[:, 0, j], lam(7)).then_inc(sem("dve_step"), E.up())
                dve.tensor_copy(s_l2[:, 1, 0], lam(8)).then_inc(sem("dve_step"), E.up())
                ts(s_l2[:, 1, 1], lam(8), -1.0, None, ALU.mult).then_inc(sem("dve_step"), E.up())
                dve.wait_ge(E.last_sem(), E.last_count())
                t1, t2 = (x[:, :, :].rearrange("p a b -> p (a b)").rearrange("p (r i) -> p r i", i=16) for x in (stage, prob))
                for ri in range(2):
                    dve.memset(s_be[ri], 0.0).then_inc(sem("dve_step"), E.up())
                    tt(t1, (s_br, s_bi)[ri], along(lam(2), 16), ALU.mult).then_inc(sem("dve_step"), E.up())
                    tt(t2, (s_bi, s_br)[ri], along(lam(5), 16), ALU.mult).then_inc(sem("dve_step"), E.up())
                    dve.wait_ge(E.last_sem(), E.last_count())
                    for g in range(2):
                        rs = slice(64 * g, 64 * g + 64)
                        tt(s_be[ri][rs, :, g, :], t1[rs], t2[rs], ALU.add if ri else ALU.subtract) \
                            .then_inc(sem("dve_step"), E.up())
                    dve.wait_ge(E.last_sem(), E.last_count())
                    dve.nop().then_inc(sem("be_ready"), E.count("be_ready"))
                for ri in range(2):
                    for k in range(0, KT, 4):
                        dve.tensor_copy(s_B[:, k:k + 4, ri, :], turned()[:, :].rearrange("p (k t) -> p k t", t=P)) \
                            .then_inc(sem("tp_free"), E.up("tp_free"))
                for ri in range(2):
                    for g in range(2):
                        ts(s_ce[:, :, g, :], s_cn[ri], gmask[:, g:g + 1], -1.0 if ri else 1.0, ALU.mult, ALU.mult) \
                            .then_inc(sem("dve_step"), E.up())
                    dve.wait_ge(E.last_sem(), E.last_count())
                    dve.nop().then_inc(sem("ce_ready"), E.count("ce_ready"))
                    for k in range(0, KT, 4):
                        dve.tensor_copy(s_C[:, 4 * k:4 * k + 16, ri, :],
                                              turned()[:, :].rearrange("p (k c) -> p k c", c=32)) \
                                                  .then_inc(sem("tp_free"), E.up("tp_free"))
                dve.wait_ge(E.last_sem(), E.last_count())
                dve.nop().then_inc(sem("bc_ready"), E.count("bc_ready"))
                NB = SEQ // S5_STEP
                re_im, carry = s_car[:, 0:2], s_car[:, 2]

                def step(h, prev):
                    tt(re_im[:, 0], prev, s_l2[:, 0], ALU.mult).then_inc(sem("dve_step"), E.up())
                    tt(re_im[:, 1], prev, s_l2[:, 1], ALU.mult).then_inc(sem("dve_step"), E.up())
                    dve.wait_ge(E.last_sem(), E.last_count())
                    tt(re_im[:, 0], re_im[:, 0], re_im[:, 1, ::-1, :], ALU.add).then_inc(sem("dve_step"), E.up())
                    dve.wait_ge(E.last_sem(), E.last_count())
                    tt(h, h, re_im[:, 0], ALU.add).then_inc(sem("dve_step"), E.up())
                    dve.wait_ge(E.last_sem(), E.last_count())

                def scan(buf, t0, t1):
                    n = 5
                    assert (t1 - t0) % n == 0
                    with E.loop((t1 - t0) // n, {"dve_step": 4 * n}) as i:
                        for j in range(n):
                            at = t0 + j if isinstance(i, int) else i * n + (t0 + j)
                            step(buf[:, bass.ds(at, 1)].rearrange("p o r k -> p (o r) k"),
                                 buf[:, bass.ds(at - 1, 1)].rearrange("p o r k -> p (o r) k"))

                for b in range(NB + 1):
                    if b < NB:
                        skip("unit_full", 8)
                        buf = s_h[b % 2]
                        dve.wait_ge(sem("bu_ready"), E.due("bu_ready"))
                        if b:
                            step(buf[:, 0], carry)
                        scan(buf, 1, 16)
                    if b:
                        ts_ = slice((b - 1) * S5_STEP, b * S5_STEP)
                        y = stage[:, (b - 1) % 2].rearrange("p (k t) -> p k t", t=S5_STEP)
                        if b >= 3:
                            pass
                        tt(y, s_ut[:, :, ts_], along(col("s5_d"), S5_STEP), ALU.mult).then_inc(sem("dve_step"), E.up())
                        dve.wait_ge(E.last_sem(), E.last_count())
                        bank = take("unit_full")[:, :].rearrange("p (k t) -> p k t", t=S5_STEP)
                        tt(y, y, bank, ALU.add).then_inc(sem("dve_free"), E.up("dve_free"))
                        dve.wait_ge(E.last_sem(), E.last_count())
                        dve.nop().then_inc(sem("y_ready_s5"), E.count("y_ready_s5"))
                    if b < NB:
                        step(buf[:, 16], buf[:, 15])
                        scan(buf, 17, 32)
                        dve.tensor_copy(carry, buf[:, S5_STEP - 1]).then_inc(sem("dve_step"), E.up())
                        dve.wait_ge(E.last_sem(), E.last_count())
                        dve.nop().then_inc(sem("scan_done"), E.count("scan_done"))
                skip("gemm_full", g_glu.n * g_glu.tiles)
                for t in range(TT):
                    for k in range(0, KT, 4):
                        bank = turned()[:, :].rearrange("p (k t) -> p k t", t=P)
                        tt(s_pre[:, k:k + 4, t * P:(t + 1) * P], bank, along(col("s5_b_glu")[:, k:k + 4], P), ALU.add) \
                            .then_inc(sem("tp_free"), E.up("tp_free"))
                dve.wait_ge(E.last_sem(), E.last_count())
                dve.nop().then_inc(sem("pre_gate"), E.count("pre_gate"))
                for k in range(0, KT, 4):
                    dve.wait_ge(sem("gate_sig"), E.due("gate_sig"))
                    tt(s_zt[:, k:k + 4], s_zt[:, k:k + 4], s_pre[:, k:k + 4], ALU.mult).then_inc(sem("dve_step"), E.up())
                dve.wait_ge(E.last_sem(), E.last_count())
                dve.nop().then_inc(sem("feat_ready"), E.count("feat_ready"))
                residual(g_out)

            for l in range(2):
                if f"b1_{l}" in stages:
                    block1(l)
            if "even" in stages:
                even()
            for l in range(2):
                if l == 1 and "odd" in stages:
                    odd()
                if f"xat{l}" in stages:
                    xat(l)
                if f"ffn{l}" in stages:
                    ffn(l)
            if "final" in stages:
                dve.wait_ge(E.last_sem(), E.last_count())
                dve.nop().then_inc(sem("fin_free"), E.count("fin_free"))
                norm(lambda t: x4[:, t], lambda t: xn2[:, t], TT, "dve_step")
                dve.wait_ge(sem("fin_in"), E.due("fin_in", 16))
                dve.wait_ge(E.last_sem(), E.last_count())
                for t in range(TT):
                    tt(xn2[:, t], xn2[:, t], view(8192, D), ALU.mult).then_inc(sem("y_ready"), E.up("y_ready"))
            if dbg is not None:
                dve.wait_ge(E.last_sem(), E.last_count())
                dve.nop().then_inc(sem("all_done"), E.count("all_done"))


_INS = ["x", "c", "ctx", "c_ctx", "norm_w", "w_mod", "b_mod", "w_in", "w_sgu", "b_sgu", "v_norm_w", "q_norm_w",
        "k_norm_w", "w_out"] + [n + "_2" for n in (
            "mem", "start_frame", "norm_mix", "norm_xattn", "norm_mem", "norm_ffn", "final_norm", "xattn_wq",
            "xattn_wkv", "xattn_wo", "ffn_up", "ffn_down", "even_w_in", "even_w_out", "dsa_cq_norm", "dsa_ckv_norm",
            "dsa_kidx_norm", "dsa_w_uq", "dsa_w_uk", "dsa_w_uv", "dsa_w_qidx", "rwkv_mu", "rwkv_w0", "rwkv_w2",
            "rwkv_a0", "rwkv_a2", "rwkv_g2", "rwkv_k_k", "rwkv_k_a", "rwkv_r_k", "rwkv_ln_w", "rwkv_ln_b", "odd_w_in",
            "odd_w_out", "s5_lam_re", "s5_lam_im", "s5_log_dt", "s5_b_re", "s5_b_im", "s5_c_re", "s5_c_im", "s5_d",
            "s5_w_glu", "s5_b_glu")]


def constants():
    s = np.arange(P)
    chunk = s // RC
    c = {"ident": np.eye(P), "tri": (chunk[:, None] == chunk[None]) & (s[:, None] <= s[None]),
         "ind": chunk[:, None] == np.arange(P // RC)[None],
         "gmask": (s[:, None] // 16) % 2 == np.arange(2)[None]}
    a = np.arange(RC)
    m = np.concatenate([a[:, None] < a[None], a[:, None] <= a[None]], 1)
    c["mask32"] = np.tile(m, (P // RC, 1))
    n = np.arange(SEQ)
    freq = np.power(10000.0, (-np.arange(0, 64, 2, dtype=np.float32) / np.float32(64)).astype(np.float64)).astype(np.float32)
    ar, ac = ((p.astype(np.float32)[:, None] * freq) for p in (n // 64, n % 64))
    ang = np.concatenate([ar, ar, ac, ac], 1).astype(np.float64)
    sign = np.tile(np.repeat([-1.0, 1.0], 32), 2)
    c["cos"], c["sin"] = np.cos(ang), np.sin(ang) * sign
    inv = [np.power(500000.0, (-np.arange(0, r, 2, dtype=np.float32) / np.float32(r)).astype(np.float64)) for r in (32, 16)]
    c["invf"] = np.concatenate(inv)
    c = {k: np.ascontiguousarray(v, dtype=np.float32) for k, v in c.items()}
    c["tokid"] = (s[:, None] + P * np.arange(TT)[None]).astype(np.int32)
    return c


def kernel(**inputs):
    import concourse.bacc as bacc
    from concourse.bass_utils import run_bass_kernel_spmd

    nc = bacc.Bacc("TRN2", target_bir_lowering=False, num_devices=1)
    arrays = {n: np.ascontiguousarray(inputs[n]) for n in _INS}
    arrays |= {"const_" + n: a for n, a in constants().items()}
    aps = {n: nc.dram_tensor("in_" + n, a.shape, mybir.dt.from_np(a.dtype), kind="ExternalInput").ap()
           for n, a in arrays.items()}
    out = nc.dram_tensor("out_x", (1, SEQ, D), F32, kind="ExternalOutput").ap()
    two_blocks(nc, aps, out)
    r = run_bass_kernel_spmd(nc, [{"in_" + n: a for n, a in arrays.items()}], core_ids=[0])
    return r.results[0]["out_x"]
```

```python
from contextlib import ExitStack, contextmanager
from collections import defaultdict
import numpy as np

import concourse.bass as bass
from concourse import mybir
from concourse.alu_op_type import AluOpType as ALU

ACT = mybir.ActivationFunctionType
AX = mybir.AxisListType.X
F32 = mybir.dt.float32
F32R = mybir.dt.float32r
I32 = mybir.dt.int32

P = 128
D = 2048
SEQ = 256
TT = SEQ // P
KT = D // P
CH = 512
RING = 8
KS = 2
HD = 128
B1_COLS, B1_HALF = 5632, 1024
EVEN_COLS = 4240
A_COLS = 880
B_W, B_H, B_D = 1024, 16, 64
RC = 32
NRC = SEQ // RC
FFN = 8192
S5_STEP = 64
PAIRS = 64
NEG = -3.0e38
TAKEN = -1.0e38
DECAY = float(np.exp(np.float32(-0.5)))
TWO_PI = 6.283185307179586


def cody_waite():
    c1 = 6.28125
    c2 = float(np.float32(np.round((TWO_PI - c1) * 2**19) / 2**19))
    return c1, c2, float(np.float32(TWO_PI - c1 - c2))


class Eng:

    def __init__(self, e, sem, own):
        self.e, self.sem, self.own = e, sem, own
        self.cnt, self.seen = defaultdict(int), defaultdict(int)
        self.last, self.i, self.slopes = None, None, {}

    def at(self, name, v):
        return v if self.i is None or name not in self.slopes else self.i * self.slopes[name] + v

    def count(self, name):
        self.cnt[name] += 1
        return 1

    def up(self, name=None):
        name = name or self.own
        self.cnt[name] += 1
        self.last = (name, self.cnt[name])
        return 1

    def last_sem(self):
        return self.sem(self.last[0])

    def last_count(self):
        return self.at(*self.last)

    def due(self, name, k=1):
        self.seen[name] += k
        return self.at(name, self.seen[name])

    @contextmanager
    def loop(self, n, slopes):
        before = {k: self.cnt[k] + self.seen[k] for k in slopes}
        if n == 1:
            yield 0
        else:
            with self.e.Fori(0, n) as i:
                self.i, self.slopes = i, slopes
                yield i
                self.i, self.slopes = None, {}
        for k, v in slopes.items():
            assert self.cnt[k] + self.seen[k] - before[k] == v, (k, v, self.cnt[k] + self.seen[k] - before[k])
            if self.cnt[k]:
                self.cnt[k] += v * (n - 1)
            else:
                self.seen[k] += v * (n - 1)
        if self.last and self.last[0] in slopes:
            self.last = (self.last[0], self.cnt[self.last[0]])


class Gemm:

    def __init__(self, name, w, k, cols, tiles, owner, lead=0, split=True, unroll=False):
        self.name, self.w, self.tiles, self.owner, self.split = name, w, tiles, owner, split
        self.kt = k // P
        self.slots = -(-self.kt // KS)
        self.riders = []
        self.cols = cols
        self.n = len(cols)
        body = 1
        while body * self.slots % RING or body * tiles % 4:
            body += 1
        self.body, self.lead = body, lead
        self.turns = (self.n - lead) // body
        if self.turns < 2 or unroll:
            self.turns, self.lead = 0, self.n
        self.tail = self.lead + self.turns * body

    def chunk_slots(self):
        return [min(KS, self.kt - KS * s) for s in range(self.slots)]


class Pair:

    def __init__(self, hi, lo, raw):
        self.hi, self.lo, self.raw = hi, lo, raw

    def at(self, k, n, cols):
        return Pair(*(v[:, k:k + n, cols] for v in (self.hi, self.lo, self.raw)))

    def at_reg(self, k, n, cols):
        return Pair(*(v[:, bass.ds(k, n), cols] for v in (self.hi, self.lo, self.raw)))

    def flat(self):
        return Pair(*(v.rearrange("p k t -> p (k t)") for v in (self.hi, self.lo, self.raw)))


def chunks(first, last):
    return [(c, min(CH, last - c)) for c in range(first, last, CH)]


def two_blocks(nc, I, out):
    ctx = ExitStack()
    with ctx:
        sems = {}

        def sem(name):
            if name not in sems:
                sems[name] = ctx.enter_context(nc.semaphore(name))
            return sems[name]

        def sb(name, shape, dt=F32):
            return ctx.enter_context(nc.sbuf_tensor(name, shape, dt))

        BIG_W = 30720
        def over_big(name, off, n):
            with ExitStack() as place:
                if off:
                    place.enter_context(nc.sbuf_tensor(name + "_before", [P, off], F32))
                return place.enter_context(nc.sbuf_tensor(name, [P, n], F32R))

        pairs = {}
        for name, off, n in (("feat4", 0, KT * 4 * P), ("feat", 4096, KT * SEQ), ("feat_e", 20480, KT * SEQ),
                             ("hid_t", 12288, FFN // 2 // P * SEQ), ("xa_ot", 27648, 4 * SEQ)):
            pairs[off, n] = [over_big(f"{name}_{part}", off + j * n, n) for j, part in enumerate(("hi", "lo"))]
        big = sb("big", [P, BIG_W])
        with nc.sbuf_tensor("ring_r", [P, RING, 2, KS, CH], F32R) as ring_r:
            pass
        ring = sb("ring", [P, RING, 2, KS, CH])
        ident = sb("ident", [P, P])
        tri = sb("tri", [P, P])
        rope = sb("rope", [P, 2, TT, HD])
        mask32 = sb("mask32", [P, 2 * RC])
        ind = sb("ind", [P, P // RC])
        gmask = sb("gmask", [P, 2])
        invf = sb("invf", [P, 24])
        tokid = sb("tokid", [P, TT], I32)
        frame = sb("frame", [P, 1], I32)
        posi = sb("posi", [P, TT], I32)
        qk_w = sb("qk_w", [P, 2, 2, HD])
        cols1 = sb("cols1", [P, P])
        cols2 = sb("cols2", [P, P])
        modc = sb("modc", [P, P])
        silu_c = sb("silu_c", [P, KT, 32])
        cols3 = sb("cols3", [P, 2 * 32])
        sel = sb("sel", [P, 2])
        sel8 = sb("sel8", [8, 2, P])
        eps = sb("eps", [P, 3])
        stat = sb("stat", [P, 80])
        stat2 = sb("stat2", [P, 80])
        att_s = sb("att_s", [P, 16])
        stage = sb("stage", [P, 2, CH])
        prob = sb("prob", [P, 2, CH])
        prob_t = sb("prob_t", [P, 2, 4, P])
        cond = stage[:, 1, 0:2 * KT]
        angle = stage[:, 0, 0:256].rearrange("p (a b) -> p a b", b=64)
        trig = sb("trig", [P, 2, 48])
        mod_s = prob_t[:, :, :, :].rearrange("p a b c -> p a (b c)")
        acc = [ctx.enter_context(nc.psum_tensor(f"acc{i}", [P, CH], F32)) for i in range(4)]
        tp = [ctx.enter_context(nc.psum_tensor(f"tp{i}", [P, CH], F32)) for i in range(4)]

        def dram(name, shape):
            return nc.dram_tensor(name, shape, F32, kind="Internal").ap()

        g_d = dram("g_d", (2, 4, 2, D))
        x_d = dram("x_d", (SEQ, D))
        a_d = dram("a_d", (NRC, B_H, RC, RC))
        t_d = dram("t_d", (NRC, B_H, RC, RC))
        kbv_d = dram("kbv_d", (SEQ, 2, 3, CH))
        o_d = dram("o_d", (SEQ, B_W))
        q_d = dram("q_d", (2 * SEQ, B1_HALF))

        def shaped(v, *shape):
            if len(shape) == 1:
                return v
            names = "abcd"[:len(shape)]
            return v.rearrange(f"p ({' '.join(names)}) -> p {' '.join(names)}", **dict(zip(names[1:], shape[1:])))

        def view(off, *shape):
            return shaped(big[:, off:off + int(np.prod(shape))], *shape)

        def pair(off, *shape):
            n = int(np.prod(shape))
            hi, lo = pairs[off, n]
            return Pair(shaped(hi[:, :], *shape), shaped(lo[:, :], *shape), view(off + n, *shape))

        x4_b1 = view(16384, 4, D)
        b1_junk = view(0, 4, D)
        diag4 = view(28672, 4, P)
        feat4 = pair(0, KT, 4 * P)
        mixes = [view(16384, 4, D), view(20480, 2, D)]
        vb = view(24576, 4, B1_HALF)
        qbs = [view(0, 4, B1_HALF), view(26624, 2, B1_HALF)]
        kvb = view(28672, 4, 512)
        q_t = view(8192, 8, 4 * P)
        k_t = view(12288, 2, 4 * P)
        sgu_t = view(13312, 8, P)
        sgu_raw = stage[:, :, :].rearrange("p a b -> p (a b)").rearrange("p (g q) -> p g q", q=P)
        vnw_row = prob_t[:, :, :, :].rearrange("p a b c -> p (a b c)")
        gate = view(24576, 2, D)
        gate_b = view(14336, D)
        rows1, rows2, rows3, rows_c = (view(24576 + i * P, P) for i in range(4))
        x4 = view(0, TT, D)
        feat = pair(4096, KT, SEQ)
        hid_t = pair(12288, FFN // 2 // P, SEQ)
        HID = [stage, prob]
        xn2 = view(16384, TT, D)
        memb = view(20480, TT, D)
        diag = view(30464, TT, P)

        C1 = {"norm_w0": 0, "norm_w1": 16, "norm_mix0": 32, "norm_mix1": 48, "norm_xattn0": 64, "norm_xattn1": 80,
              "norm_mem0": 96, "norm_mem1": 112}
        C2 = {"norm_ffn0": 0, "norm_ffn1": 16, "s5_d": 32, "s5_b_glu": 48,
              "b_sgu0": 64, "b_sgu1": 72, "cq": 80}
        ROWS2 = 84

        CONSTS, ROWS = 15, 2 + len(C1) + len(C2)

        def col(name, n=KT):
            t, at = (cols1, C1[name]) if name in C1 else (cols2, C2[name])
            return t[:, at:at + n]

        def mod_col(layer, cond, part):
            at = ((layer * 2 + cond) * 2 + part) * KT
            return modc[:, at:at + KT]

        W = lambda name, i=None: I[name] if i is None else I[name][i]
        gemms = defaultdict(list)
        MODS = [(l, c) for l in range(2) for c in range(12)]
        mods = [Gemm(f"mod{l}", W("w_mod", l), D, chunks(c * CH, (c + 1) * CH), 1, "act_free", split=False) for l, c in MODS]
        gemms["mod"] = mods[:8]
        mod_items = [("mod", 0), ("mod", 1), ("rows",), ("cols", 0)]
        for n in range(2, 8):
            mod_items += [("mod", n), ("cols", n - 1)]
        mod_items.append(("cols", 7))
        b1_items = [[], []]
        for l in range(2):
            t = 4 if l == 0 else 2
            g = gemms[f"b1_{l}"]
            if l == 0:
                for c, cols in enumerate(chunks(0, 4096)):
                    g.append(Gemm(f"in{l}", W("w_in", l), D, [cols], t, "act_free"))
                    g[-1].riders = mods[8 + 2 * c:10 + 2 * c]
                    b1_items[0].append(("in", g[-1], c))
                    b1_items[0] += [("cols", n) for n in (6 + 2 * c, 7 + 2 * c) if c]
                    b1_items[0] += [("mod", 8 + 2 * c), ("mod", 9 + 2 * c)]
            else:
                g.append(Gemm(f"in{l}", W("w_in", l), D, chunks(0, 4096), t, "act_free"))
                b1_items[1].append(("in", g[0], 0))
            g.append(Gemm(f"kv{l}", W("w_in", l), D, chunks(4096, 4608), 4, "act_free"))
            g.append(Gemm(f"zb{l}", W("w_in", l), D, chunks(4608, 5632), t, "act_free"))
            b1_items[l] += [("kv", g[-2], 0), ("zb", g[-1], 0, l)]
            g.append(Gemm(f"out{l}", W("w_out", l), D, chunks(0, D), t, "dve_free"))
        g = gemms["even"]
        g.append(Gemm("even_in", W("even_w_in_2", 0), D, chunks(0, EVEN_COLS), 2, "act_free"))
        flat = lambda a: a.rearrange("r h d -> r (h d)")
        g.append(Gemm("uq", flat(W("dsa_w_uq_2", 0)), 512, chunks(0, 1024), 2, "act_free", split=False))
        g.append(Gemm("qidx", flat(W("dsa_w_qidx_2", 0)), 512, chunks(0, 1024), 2, "act_free", split=False))
        g.append(Gemm("uv", flat(W("dsa_w_uv_2", 0)), 256, chunks(0, 1024), 2, "act_free", split=False))
        g.append(Gemm("even_out", W("even_w_out_2", 0), D, chunks(0, D), 2, "dve_free"))
        g = gemms["odd"]
        g.append(Gemm("odd_in", W("odd_w_in_2", 0), D, chunks(0, D), 2, "act_free", unroll=True))
        g.append(Gemm("glu", W("s5_w_glu_2", 0), D, chunks(0, D), 2, "act_free"))
        g.append(Gemm("odd_out", W("odd_w_out_2", 0), D, chunks(0, D), 2, "dve_free"))
        for l in range(2):
            g = gemms[f"xat{l}"]
            g.append(Gemm(f"xq{l}", W("xattn_wq_2", l), D, chunks(0, 512), 2, "act_free"))
            g.append(Gemm(f"xkv{l}", W("xattn_wkv_2", l), D, chunks(0, 1024), 2, "act_free"))
            g.append(Gemm(f"xo{l}", W("xattn_wo_2", l), 512, chunks(0, D), 2, "dve_free"))
            g = gemms[f"ffn{l}"]
            for h in range(0, FFN, FFN // 2):
                g.append(Gemm(f"up{l}", W("ffn_up_2", l), D, chunks(h, h + FFN // 2), 2, "act_free", lead=1))
                g.append(Gemm(f"down{l}", W("ffn_down_2", l)[h:h + FFN // 2], FFN // 2, chunks(0, D), 2, "dve_free"))
        ORDER = ["load", "mod", "b1_0", "b1_1", "even", "xat0", "ffn0", "odd", "xat1", "ffn1", "final"]
        uses = []
        n_split = 0
        for st in ORDER:
            for g in gemms[st]:
                g.q0, g.w0 = len(uses), n_split
                uses += [(h, c if h is g else 0, s) for c in range(g.n) for s in range(g.slots) for h in [g] + g.riders]
                n_split += g.n * g.slots if g.split else 0

        def b1_units(layer):
            units, mix = [], mixes[layer]
            for t in ([0, 1, 2, 3] if layer == 0 else [0, 1]):
                keys = [0, 1, 2, 3] if t < 2 else [2, 3]
                for h in range(8):
                    units.append(dict(
                        q=q_t[:, h, t * P:(t + 1) * P], k=k_t[:, h // 4, keys[0] * P:(keys[-1] + 1) * P],
                        v=[kvb[:, j, 256 + (h // 4) * HD:256 + (h // 4 + 1) * HD] for j in keys],
                        out=mix[:, t, B1_HALF + h * HD:B1_HALF + (h + 1) * HD], gated=True, bias=None))
            return units

        xa_q = view(12288, TT, 512)
        xa_kv = view(13312, TT, 1024)
        xa_qt = view(24576, 4, SEQ)
        xa_kt = view(25600, 4, SEQ)
        xa_o = view(26624, TT, 512)
        xa_ot = pair(27648, 4, SEQ)

        def xat_units():
            return [dict(q=xa_qt[:, h, t * P:(t + 1) * P], k=xa_kt[:, h, :],
                         v=[xa_kv[:, j, 512 + h * HD:512 + (h + 1) * HD] for j in range(TT)],
                         out=xa_o[:, t, h * HD:(h + 1) * HD], gated=False, bias=None)
                    for t in range(TT) for h in range(4)]

        feat_e = pair(20480, KT, SEQ)
        xn_e = view(0, TT, D)
        hb = view(8192, TT, EVEN_COLS)
        ya = view(16672, TT, 1024)
        d_q = view(18720, TT, 1024)
        d_qi = view(20768, TT, 1024)
        d_qt = view(22816, 8, SEQ)
        d_qit = view(24864, 8, SEQ)
        d_v = view(26912, TT, 1024)
        d_kt = view(4096, 8, SEQ)
        d_uk = view(6144, 2, 8, HD)
        d_cqt = view(28960, 4, SEQ)
        d_ckt = view(29984, 2, SEQ)
        d_kid = view(0, TT, P)
        d_kit = view(256, 2 * SEQ)
        d_score = view(768, TT, SEQ)
        d_work = view(1280, TT, SEQ)
        d_bias = view(1792, TT, SEQ)
        d_ckw = view(2304, 256)
        d_kiw = view(2560, 64)
        d_krt = view(2624, SEQ)
        d_tmp = view(2880, 1024)
        d_top = view(3904, 8)

        def dsa_units():
            return [dict(q=d_qt[:, h, t * P:(t + 1) * P], k=d_kt[:, h, :],
                         v=[d_v[:, j, h * HD:(h + 1) * HD] for j in range(TT)],
                         out=ya[:, t, h * HD:(h + 1) * HD], gated=False, bias=d_bias[:, t, :])
                    for t in range(TT) for h in range(8)]

        R0, K0, V0, WL0, AL0, GL0 = 880, 1904, 2928, 3952, 4016, 4080
        w_sh = view(18720, TT, 3360)
        w_ar = view(18720, 8, NRC, 2, RC)
        w_bk = view(22816, 8, NRC, 2, RC)
        w_row = view(0, 5, B_W)
        w_mu = [view(6144, 2048), view(25440, 1312)]
        w_t = view(5120, 3, B_W)
        w_t4 = view(26912, B_W)
        w_lt = view(27936, 4, P)
        w_w2 = view(28448, 2, B_W)
        w_g2a = view(0, 2, B_W)
        w_tt = view(0, 64, RC)
        w_kbv = [view(2048 + 1024 * i, 2, 8, B_D) for i in range(2)]
        w_G = [view(26912, 8, 2, RC), view(5120, 8, 2, RC)]
        w_z = view(27936, CH)
        w_A = view(5120, RC, RC)
        w_T = view(6144, RC, RC)
        w_tm = view(0, RC, RC)
        w_a = view(2048, 2, 8 * RC)
        w_st = [view(7168 + 512 * i, 8, B_D) for i in range(2)]
        w_pc = sb("w_pc", [P, 8, NRC])
        w_bon = sb("w_bon", [P, TT, B_H])
        w_ln = [view(4096, B_W), view(6144, B_W)]
        w_o = stage

        s_B = view(0, KT, 2, P)
        s_ut = view(4096, KT, SEQ)
        s_h = [view(20480, S5_STEP, 2, PAIRS), view(8192, S5_STEP, 2, PAIRS)]
        s_u = view(16384, TT, D)
        s_C = view(16384, PAIRS, 2, 32)
        s_lam = view(28672, 12, PAIRS)
        s_l2 = view(29440, 2, 2, PAIRS)
        s_car = view(29696, 3, 2, PAIRS)
        s_ld = view(30080, P)
        s_lr = view(30208, 2, P)
        s_br = view(20480, PAIRS, 16)
        s_bi = view(21504, PAIRS, 16)
        s_be = [view(22528 + 2048 * i, PAIRS, 2, 16) for i in range(2)]
        s_cn = [view(26624 + 1024 * i, KT, 64) for i in range(2)]
        s_ce = [view(12288 + 2048 * i, KT, 2, 64) for i in range(2)]
        s_zs = pair(20480, KT, SEQ)
        s_pre = view(12288, KT, SEQ)
        s_sig = view(16384, TT, D)

        prob_turns = []

        block = ctx.enter_context(nc.Block())

        @block.sync
        def _(sp):
            q = 0
            freed, full = 0, 0
            free_at = []

            def load(g, w_cols, s, slot):
                kt = g.chunk_slots()[s]
                src = g.w[s * KS * P:(s * KS + kt) * P, :].rearrange("(q p) n -> p q n", p=P)
                n0, width = w_cols
                sp.dma_start(ring[:, slot, 1, 0:kt, 0:width], src[:, :, bass.ds(n0, width)]) \
                    .then_inc(sem(f"ring_full{slot}"), 16)

            for st in ORDER:
                for g in gemms[st]:
                    for c in range(g.n):
                        for s in range(g.slots):
                            for j in range(1 + len(g.riders)):
                                if s < g.slots - 1:
                                    freed += 1
                                    free_at.append(("ring_free", freed))
                                else:
                                    free_at.append(("gemm_full", full + (c + 1) * g.tiles + j))
                    full += g.n * g.tiles + len(g.riders)
                    per = g.body * g.slots

                    def plain(c):
                        nonlocal q
                        for s in range(g.slots):
                            for h in [g] + g.riders:
                                if q >= RING:
                                    name, v = free_at[q - RING]
                                    sp.wait_ge(sem(name), v)
                                load(h, (g.cols[c] if h is g else h.cols[0]), s, q % RING)
                                q += 1

                    for c in range(g.lead):
                        plain(c)
                    first = g.lead + (g.body if g.turns else 0)
                    for c in range(g.lead, first):
                        plain(c)
                    if g.turns:
                        with sp.Fori(0, g.turns - 1) as i:
                            for j in range(per):
                                name, v = free_at[q + j - RING]
                                slope = free_at[q + j - RING + per][1] - v if g.turns > 2 else 0
                                sp.wait_ge(sem(name), i * slope + v if slope else v)
                                c, s = first + j // g.slots, j % g.slots
                                load(g, (i * (g.body * CH) + g.cols[c][0], CH), s, (q + j) % RING)
                        q += per * (g.turns - 1)
                    for c in range(g.tail, g.n):
                        plain(c)
        @block.gpsimd
        def _(pool):
            L = Eng(pool, sem, "pool_step")

            def dma(dst, src, name):
                with nc.allow_non_contiguous_dma(reason="small constant"):
                    pool.dma_start(dst, src).then_inc(sem(name), 16)

            def row(src, n):
                return src.rearrange("(o n) -> o n", o=1).to_broadcast([P, n])

            dma(rows_c[0:16, :], I["c"][0].rearrange("(k p) -> k p", p=P), "cond_in")
            dma(rows_c[16:32, :], I["c_ctx"].rearrange("(k p) -> k p", p=P), "cond_in")
            dma(ident[:, :], I["const_ident"], "cond_in")
            for name, dst in (("tri", tri[:, :]), ("mask32", mask32[:, :]), ("ind", ind[:, :]), ("gmask", gmask[:, :]),
                              ("tokid", tokid[:, :]), ("sel", sel[:, :]), ("sel8", sel8[:, :, :])):
                dma(dst, I["const_" + name], "consts")
            dma(rope[:, 0], I["const_cos"].rearrange("(t p) d -> p t d", p=P), "consts")
            dma(rope[:, 1], I["const_sin"].rearrange("(t p) d -> p t d", p=P), "consts")
            dma(invf[:, :], row(I["const_invf"], 24), "consts")
            dma(frame[:, :], row(I["start_frame_2"], 1), "consts")
            for l in range(2):
                dma(qk_w[:, l, 0], row(I["q_norm_w"][l], HD), "consts")
                dma(qk_w[:, l, 1], row(I["k_norm_w"][l], HD), "consts")
            dma(x4_b1[:, 0:2], I["x"][0].rearrange("(t p) d -> p t d", p=P), "x_in")
            dma(x4_b1[:, 2:4], I["ctx"][0].rearrange("(t p) d -> p t d", p=P), "x_in")
            for l in range(2):
                if l == 0:
                    for n, item in enumerate(b1_items[0]):
                        if item[0] == "mod" and MODS[item[1]][1] >= 8:
                            ml, mc = MODS[item[1]]
                            pool.wait_ge(sem("gate_chunk"), L.due("gate_chunk"))
                            for j in range(4):
                                dma(g_d[ml, j][:, (mc - 8) * CH:(mc - 7) * CH], mod_s[32 * j:32 * j + 2, item[1] % 2], f"g_out{item[1] % 2}")
                        if item[0] == "in" and item[2] >= 6:
                            c = item[2] - 6
                            for t in range(4):
                                pool.wait_ge(sem("q_chunk"), L.due("q_chunk"))
                                dma(q_d[t * P:(t + 1) * P, c * CH:(c + 1) * CH], prob[:, t % 2], f"q_out{t % 2}")
                pool.wait_ge(sem("stage_free"), L.due("stage_free"))
                dma(sgu_raw, I["w_sgu"][l].rearrange("g p q -> p g q"), "sgu_in")
                if l == 0:
                    for j in range(2):
                        pool.wait_ge(sem(f"g_out{j}"), 16 * 4 * 4)
                dma(vnw_row, row(I["v_norm_w"][l].rearrange("g d -> (g d)"), B1_HALF), "vnw_in")
                if l == 0:
                    pool.wait_ge(sem("proj_done"), L.due("proj_done"))
                    for j in range(2):
                        pool.wait_ge(sem(f"q_out{j}"), 16 * 4)
                    dma(qbs[0], q_d.rearrange("(t p) d -> p t d", p=P), "q_in")
                pool.wait_ge(sem("sgu_done"), L.due("sgu_done"))
                dma(gate[0:8, 0], g_d[l].rearrange("j c d -> (j c) d"), "g8_in")
                dma(gate_b, row(I["b_mod"][l, 2 * D:3 * D], D), "gate_in")
                pool.wait_ge(sem("att_done"), L.due("att_done"))
                if l == 0:
                    pool.wait_ge(sem("mix_turned"), L.due("mix_turned"))
                    dma(x4_b1[:, 0:2], I["x"][0].rearrange("(t p) d -> p t d", p=P), "x_again")
                    dma(x4_b1[:, 2:4], I["ctx"][0].rearrange("(t p) d -> p t d", p=P), "x_again")
            pool.wait_ge(sem("x_norm_even"), L.due("x_norm_even"))
            dma(x_d.rearrange("(t p) d -> p t d", p=P), x4_b1[:, 0:2], "x_out")
            pool.wait_ge(sem("x_out"), 16)
            dma(d_ckw, row(I["dsa_ckv_norm_2"][0], 256), "dsa_in")
            dma(d_kiw, row(I["dsa_kidx_norm_2"][0], 64), "dsa_in")
            pool.wait_ge(sem("uk_zero"), L.due("uk_zero"))
            for rt in range(2):
                dma(d_uk[:, rt, :, 32:128], I["dsa_w_uk_2"][0][rt * P:(rt + 1) * P], "dsa_in")
            pool.wait_ge(sem("even_h"), L.due("even_h"))
            pool.wait_ge(sem("dqt_ready"), L.due("dqt_ready"))
            dma(w_sh[1:P, 0], hb[0:P - 1, 0, A_COLS:], "shift_in0")
            pool.wait_ge(sem("kt_ready"), L.due("kt_ready"))
            dma(w_mu[0], row(I["rwkv_mu_2"][0, 0:2048], 2048), "mu_in")
            pool.wait_ge(sem("bias_ready"), L.due("bias_ready"))
            dma(w_mu[1], row(I["rwkv_mu_2"][0, 2048:3360], 1312), "mu_in")
            pool.wait_ge(sem("dsa_done"), L.due("dsa_done"))
            dma(w_sh[0:1, 1], hb[P - 1:P, 0, A_COLS:], "shift_in")
            dma(w_sh[1:P, 1], hb[0:P - 1, 1, A_COLS:], "shift_in")
            for j, name in enumerate(("w0", "a0", "k_k", "k_a")):
                dma(w_row[:, j], row(I[f"rwkv_{name}_2"][0], B_W), "rwkv_in")
            dma(w_row[:, 4], row(I["rwkv_r_k_2"][0].rearrange("h d -> (h d)"), B_W), "rwkv_in")
            dma(w_w2[0:64, 0], I["rwkv_w2_2"][0], "rwkv_in")
            dma(w_w2[0:64, 1], I["rwkv_a2_2"][0], "rwkv_in")
            for t in range(TT):
                pool.wait_ge(sem("arbk_ready"), L.due("arbk_ready"))
                for j, src in enumerate((hb[:, t, K0:K0 + B_W], w_t4, hb[:, t, V0:V0 + B_W])):
                    by_half = src.rearrange("p (h o d) -> p o h d", o=2, d=B_D)
                    for o in range(2):
                        dma(kbv_d[t * P:(t + 1) * P, o, j].rearrange("s (h d) -> s h d", d=B_D), by_half[:, o], "kbv_out")
            pool.wait_ge(sem("rows_done"), L.due("rows_done"))
            dma(w_g2a[:, 0], I["rwkv_g2_2"][0, 0:P], "g2_in")
            dma(w_g2a[0:32, 1], I["rwkv_g2_2"][0, P:160], "g2_in")
            for c in range(NRC):
                pool.wait_ge(sem("a_ready"), L.due("a_ready"))
                for o in range(2):
                    dma(a_d[c].rearrange("(h o) s t -> o s h t", o=2)[o],
                        w_a[64 * o:64 * o + RC, c % 2].rearrange("p (h t) -> p h t", t=RC), f"a_out{c % 2}")
            for j in range(2):
                pool.wait_ge(sem(f"a_out{j}"), 16 * NRC)
            dma(w_A.rearrange("p s t -> p (s t)"), a_d.rearrange("c h s t -> (c h) (s t)"), "solve_in")
            pool.wait_ge(sem("kbv_out"), 16 * 6 * TT)
            by_unit = t_d.rearrange("c h s t -> (c h) s t").rearrange("(u o) s t -> o s u t", o=2)

            def chunk_in(c):
                for o in range(2):
                    for j, (r, x) in enumerate(((0, 0), (RC, 0), (0, 1))):
                        dma(w_kbv[c % 2][64 * o + r:64 * o + r + RC, x].rearrange("p h d -> p (h d)"),
                            kbv_d[c * RC:(c + 1) * RC, o, j], f"kbv_in{c % 2}")

            chunk_in(0)
            chunk_in(1)
            pool.wait_ge(sem("solved"), L.due("solved"))
            dma(t_d.rearrange("c h s t -> (c h) (s t)"), w_T.rearrange("p s t -> p (s t)"), "t_out")
            pool.wait_ge(sem("t_out"), 16)
            for o in range(2):
                dma(w_tt[64 * o:64 * o + RC], by_unit[o], "t_in")
            dma(w_ln[0], row(I["rwkv_ln_w_2"][0], B_W), "ln_in")
            dma(w_ln[1], row(I["rwkv_ln_b_2"][0], B_W), "ln_in")
            for c in range(NRC):
                pool.wait_ge(sem("o_ready"), L.due("o_ready"))
                for o in range(2):
                    dma(o_d[c * RC:(c + 1) * RC].rearrange("s (h o d) -> o s h d", o=2, d=B_D)[o],
                        w_o[64 * o:64 * o + RC, c % 2].rearrange("p (h d) -> p h d", d=B_D), f"o_out{c % 2}")
                if c + 2 < NRC:
                    chunk_in(c + 2)
                if c == NRC // 2 or c == NRC - 1:
                    t = c // (NRC - 1)
                    for j in range(2):
                        pool.wait_ge(sem(f"o_out{j}"), 32 * len(range(j, c + 1, 2)))
                    dma(hb[:, t, R0:R0 + B_W], o_d[t * P:(t + 1) * P], f"o_in{t}")
            pool.wait_ge(sem("rwkv_done"), L.due("rwkv_done"))
            dma(x4, x_d.rearrange("(t p) d -> p t d", p=P), "x_back")
            for l in range(2):
                if l == 1:
                    pool.wait_ge(sem("lr_free"), L.due("lr_free"))
                    for s, d in ((I["s5_lam_re_2"], s_lr[0:64, 0]), (I["s5_lam_im_2"], s_lr[0:64, 1])):
                        dma(d, s[0].rearrange("(r g) p -> r (g p)", g=2), "lam_in")
                    dma(s_ld, row(I["s5_log_dt_2"][0], P), "lam_in")
                    pool.wait_ge(sem("s5_free"), L.due("s5_free"))
                    for s, d in ((I["s5_b_re_2"], s_br), (I["s5_b_im_2"], s_bi)):
                        dma(d, s[0].rearrange("(r g) p i -> (g p) r i", g=2), "s5_in")
                    for s, d in ((I["s5_c_re_2"], s_cn[0]), (I["s5_c_im_2"], s_cn[1])):
                        dma(d, s[0].rearrange("g i p -> (g i) p").rearrange("(k c) p -> c k p", c=P), "s5_in")
                    pool.wait_ge(sem("x_norm_odd"), L.due("x_norm_odd"))
                    dma(x_d.rearrange("(t p) d -> p t d", p=P), x4, "x_out")
                    pool.wait_ge(sem("x_out"), 32)
                    pool.wait_ge(sem("s5_done"), L.due("s5_done"))
                    dma(x4, x_d.rearrange("(t p) d -> p t d", p=P), "x_back")
                pool.wait_ge(sem("mem_free"), L.due("mem_free"))
                dma(memb, I["mem_2"][0].rearrange("(t p) d -> p t d", p=P), "mem_in")
            pool.wait_ge(sem("fin_free"), L.due("fin_free"))
            dma(view(8192, D), row(I["final_norm_2"], D), "fin_in")
            for t in range(TT):
                pool.wait_ge(sem("y_ready"), L.due("y_ready"))
                dma(out[0, t * P:(t + 1) * P], xn2[:, t], "y_out")
            pool.wait_ge(sem("y_out"), 16 * TT)

        @block.tensor
        def _(pe):
            E = Eng(pe, sem, "pe_step")
            owners, given = [], defaultdict(int)
            given["act_free"] = 4
            q = 0
            tp_owners, tp_given = [], defaultdict(int)

            def begin(owner):
                g = len(owners)
                if g >= 4:
                    pe.wait_ge(sem(owners[g - 4][0]), owners[g - 4][1])
                given[owner] += 1
                owners.append((owner, given[owner]))
                return acc[g % 4]

            def mod_product(g, bank, kk, slot, k):
                at = 32 * (kk % 4)
                return pe.matmul(bank[at:at + 32, :], silu_c[:, kk, :], ring[:, slot, 1, k, :], start=(kk < 4), stop=(kk >= g.kt - 4))

            def gemm(g, lhs, hook=None, parts=False, late=None):
                nonlocal q
                if g.turns:
                    for name, v in dict(owners[-4:]).items():
                        pe.wait_ge(sem(name), v)
                base, g0 = given[g.owner], len(owners)
                per_slots, per_groups = g.body * g.slots, g.body * g.tiles

                def chunk(c, i, j0, s0):
                    width = g.cols[c][1]
                    for s, kt in enumerate(g.chunk_slots()):
                        use = q + (s0 + s) * (1 + len(g.riders))
                        slot = use % RING
                        if g.split:
                            v = g.w0 + s0 + s + 1
                            pe.wait_ge(sem("w_lo"), v if isinstance(i, int) else i * per_slots + v)
                        else:
                            v = 16 * (use // RING + 1)
                            pe.wait_ge(sem(f"ring_full{slot}"), v if isinstance(i, int) else i * (16 * per_slots // RING) + v)
                        for t in range(g.tiles):
                            bank = acc[(g0 + j0 + t) % 4]
                            n = g0 + j0 + t - 4
                            if s == 0 and n >= 0:
                                name, v = owners[n] if n < g0 and not g.turns else (g.owner, base + j0 + t - 3)
                                pe.wait_ge(sem(name), v if isinstance(i, int) else i * per_groups + v)
                            if parts and c == 0 and t == 0 and KS * s % 4 == 0:
                                E.seen["feat_part"] += 1
                                pe.wait_ge(sem("feat_part"), E.seen["feat_part"])
                            if late is not None and c == 0 and t == 0 and KS * s == late:
                                E.seen["feat_ready"] += 1
                                pe.wait_ge(sem("feat_ready"), E.seen["feat_ready"])
                            for k in range(kt):
                                lt, kk = lhs(KS * s + k, t), KS * s + k
                                if g.split:
                                    w_hi, w_lo = (ring_r[:, slot, j, k, 0:width] for j in range(2))
                                    terms = [(lt.hi, w_hi), (lt.hi, w_lo), (lt.lo, w_hi)]
                                else:
                                    terms = [(lt, ring[:, slot, 1, k, 0:width])]
                                if g in mods:
                                    mm = mod_product(g, bank, kk, slot, k)
                                    continue
                                for j, (l, r) in enumerate(terms):
                                    mm = pe.matmul(bank[0:l.shape[-1], 0:width], l, r, start=(kk == 0 and j == 0),
                                                   stop=(kk == g.kt - 1 and j == len(terms) - 1))
                            if s == g.slots - 1:
                                mm.then_inc(sem("gemm_full"), E.up("gemm_full"))
                        if s < g.slots - 1:
                            mm.then_inc(sem("ring_free"), E.up("ring_free"))
                        for j, r in enumerate(g.riders):
                            u = use + 1 + j
                            pe.wait_ge(sem(f"ring_full{u % RING}"), 16 * (u // RING + 1))
                            if s == 0:
                                r.bank = len(tp_owners) % 4
                                if len(tp_owners) >= 4:
                                    pe.wait_ge(sem(tp_owners[-4][0]), tp_owners[-4][1])
                                tp_owners.append(("act_free", base + g.tiles + j + 1))
                            for k in range(kt):
                                mm = mod_product(r, tp[r.bank], KS * s + k, u % RING, k)
                            mm \
                                .then_inc(sem("gemm_full" if s == g.slots - 1 else "ring_free"), E.up("gemm_full" if s == g.slots - 1 else "ring_free"))
                    if hook:
                        hook(c, i)

                for c in range(g.lead):
                    chunk(c, 0, c * g.tiles, c * g.slots)
                if g.turns:
                    slopes = {"gemm_full": per_groups}
                    if g.slots > 1:
                        slopes["ring_free"] = g.body * (g.slots - 1)
                    if hook:
                        slopes |= {"sq_ready": per_groups, "tp_full": per_groups, "raw_ready": per_groups}
                    with E.loop(g.turns, slopes) as i:
                        for b in range(g.body):
                            c = g.lead + b
                            chunk(c, i, c * g.tiles, c * g.slots)
                for c in range(g.tail, g.n):
                    chunk(c, 0, c * g.tiles, c * g.slots)
                q += g.n * g.slots * (1 + len(g.riders))
                for _ in range(g.n * g.tiles):
                    given[g.owner] += 1
                    owners.append((g.owner, given[g.owner]))
                given["act_free"] += len(g.riders)

            def turn(blocks, freed="tp_free", scale=None):
                n = len(tp_owners)
                bank = tp[n % 4]
                if n >= 4:
                    pe.wait_ge(sem(tp_owners[n - 4][0]), tp_owners[n - 4][1])
                tp_given[freed] += 1
                tp_owners.append((freed, tp_given[freed]))
                for j, b in enumerate(blocks):
                    if scale is None:
                        mm = pe.transpose(bank[0:b.shape[-1], j * P:j * P + b.shape[0]], b, ident[0:b.shape[0], 0:b.shape[0]])
                    else:
                        mm = pe.matmul(bank[:, j * P:(j + 1) * P], b, scale, start=True, stop=True)
                mm.then_inc(sem("tp_full"), E.up("tp_full"))
                return tp_owners[-1]

            def turn_all(src, tiles, width, ready=None, freed="raw_ready"):
                if ready:
                    pe.wait_ge(sem(ready), E.due(ready))
                for t in range(tiles):
                    if not ready:
                        pe.wait_ge(sem("src_ready"), E.due("src_ready"))
                    for k in range(0, width // P, 4):
                        turn([src(t)[:, (k + j) * P:(k + j + 1) * P] for j in range(min(4, width // P - k))], freed)

            def turn_normed(src, tiles=TT, on=diag):
                pe.wait_ge(sem("diag_ready"), E.due("diag_ready"))
                for k in range(0, KT, 4):
                    for t in range(tiles):
                        turn([src[:, t, (k + j) * P:(k + j + 1) * P] for j in range(4)], "raw_ready", on[:, t])

            def attend(units):
                n = len(units)
                score_at, turned = {}, {}
                for i in range(n + 2):
                    if i < n:
                        u = units[i]
                        bank = begin("act_free" if u["bias"] is None else "dve_free")
                        score_at[i] = owners[-1]
                        pe.matmul(bank[:, 0:u["k"].shape[-1]], u["q"], u["k"], start=True, stop=True) \
                            .then_inc(sem("score_full"), E.up("score_full"))
                    if 0 <= i - 1 < n:
                        u = units[i - 1]
                        if u["bias"] is None:
                            pe.wait_ge(sem(score_at[i - 1][0]), score_at[i - 1][1])
                        else:
                            pe.wait_ge(sem("p_ready"), E.due("p_ready"))
                        prob_turns.append((len(tp_owners) % 4, E.cnt["tp_full"] + 1))
                        turned[i - 1] = turn([prob[:, (i - 1) % 2, j * P:(j + 1) * P] for j in range(len(u["v"]))], "prob_turned")
                    if i >= 2:
                        u = units[i - 2]
                        pe.wait_ge(sem(turned[i - 2][0]), turned[i - 2][1])
                        bank = begin("dve_free")
                        for j, v in enumerate(u["v"]):
                            mm = pe.matmul(bank[:, 0:HD], prob_t[:, (i - 2) % 2, j, :], v,
                                           start=(j == 0), stop=(j == len(u["v"]) - 1))
                        mm.then_inc(sem("pv_full"), E.up("pv_full"))

            def feat_lhs(f):
                if isinstance(f, Pair):
                    return lambda k, t: f.at(k, 1, slice(t * P, (t + 1) * P)).flat()
                return lambda k, t: f[:, k, t * P:(t + 1) * P]

            def project(item, parts=False):
                if item[0] == "rows":
                    pe.wait_ge(sem("rows_in"), 16 * ROWS)
                    turn([rows1, rows2[0:ROWS2, :], rows3[0:64, :]])
                    return
                kind, n = item[0:2]
                if kind == "mod":
                    if n < 8:
                        gemm(mods[n], lambda k, t: silu_c[:, k, :])
                elif kind == "cols":
                    if MODS[n][1] < 8:
                        pe.wait_ge(sem("mod_chunk"), E.due("mod_chunk"))
                        bank = begin("dve_free")
                        for k in range(4):
                            mm = pe.matmul(bank[:, 2 * k:2 * k + 2], mod_s[:, n % 2, k * P:(k + 1) * P], sel[:, :],
                                           start=True, stop=True)
                        mm.then_inc(sem("cols_full"), E.up("cols_full"))
                else:
                    gemm(n, feat_lhs(feat4), parts=parts)

            pe.wait_ge(sem("cond_in"), 48)
            turn([rows_c[0:32, :]])
            pe.wait_ge(sem("silu_ready"), E.due("silu_ready"))
            for item in mod_items:
                project(item)

            def block1(l):
                g_out = gemms[f"b1_{l}"][-1]
                mix, qb = mixes[l], qbs[l]
                turn_normed(x4_b1, 4, diag4)
                for n, item in enumerate(b1_items[l]):
                    project(item, parts=n == 0)
                tiles = g_out.tiles
                pe.wait_ge(sem("sgu_in"), 16 * (l + 1))
                for g in (0, 4):
                    turn([sgu_raw[:, g + j, :] for j in range(4)])
                pe.wait_ge(sem("sgu_t_ready"), E.due("sgu_t_ready"))
                for t in range(tiles):
                    pe.wait_ge(sem("vn_ready"), E.due("vn_ready"))
                    for half in range(2):
                        bank = begin("dve_free")
                        for j in range(4):
                            g = half * 4 + j
                            mm = pe.matmul(bank[:, j * P:(j + 1) * P], sgu_t[:, g, :], vb[:, t, g * P:(g + 1) * P],
                                           start=True, stop=True)
                        mm.then_inc(sem("unit_full"), E.up("unit_full"))
                for t in range(4):
                    pe.wait_ge(sem("qk_ready"), E.due("qk_ready"))
                    if t < tiles:
                        for h in (0, 4):
                            turn([qb[:, t, (h + j) * HD:(h + j + 1) * HD] for j in range(4)])
                    turn([kvb[:, t, j * HD:(j + 1) * HD] for j in range(2)])
                pe.wait_ge(sem("qkt_ready"), E.due("qkt_ready"))
                attend(b1_units(l))
                pe.wait_ge(sem("g8_in"), 16 * (l + 1))
                for c in range(4):
                    for cond_ in (1, 0):
                        bank = begin("dve_free")
                        pe.matmul(bank[:, :], sel8[:, cond_, :], gate[0:8, 0, c * CH:(c + 1) * CH], start=True, stop=True) \
                            .then_inc(sem("unit_full"), E.up("unit_full"))
                for t in range(tiles):
                    pe.wait_ge(sem("src_ready"), E.due("src_ready"))
                for k in range(0, KT, 4):
                    for t in range(tiles):
                        turn([mix[:, t, (k + j) * P:(k + j + 1) * P] for j in range(4)], "raw_ready")
                gemm(g_out, feat_lhs(feat4), parts=True)

            def even():
                g_in, g_uq, g_qi, g_uv, g_out = gemms["even"]
                turn_normed(x4_b1)
                gemm(g_in, feat_lhs(feat_e), parts=True)
                pe.wait_ge(sem("lat_ready"), E.due("lat_ready"))
                for t in range(TT):
                    turn([hb[:, t, j * P:(j + 1) * P] for j in range(4)])
                    turn([hb[:, t, 512 + j * P:512 + (j + 1) * P] for j in range(2)])
                    turn([d_kid[:, t, :], hb[:, t, 768:800]])
                pe.wait_ge(sem("lat_t_ready"), E.due("lat_t_ready"))
                gemm(g_uq, feat_lhs(d_cqt))
                gemm(g_qi, feat_lhs(d_cqt))
                gemm(g_uv, feat_lhs(d_ckt))
                pe.wait_ge(sem("dsa_in"), 64)
                for h in range(8):
                    bank = begin("act_free")
                    for rt in range(2):
                        mm = pe.matmul(bank[:, 0:SEQ], d_uk[:, rt, h, :], d_ckt[:, rt, :], start=(rt == 0), stop=(rt == 1))
                    mm.then_inc(sem("unit_full"), E.up("unit_full"))
                for t in range(TT):
                    pe.wait_ge(sem("dq_ready"), E.due("dq_ready"))
                    for h in (0, 4):
                        turn([d_q[:, t, (h + j) * P:(h + j + 1) * P] for j in range(4)])
                    for h in (0, 4):
                        turn([d_qi[:, t, (h + j) * P:(h + j + 1) * P] for j in range(4)])
                pe.wait_ge(sem("dqt_ready"), E.due("dqt_ready"))
                for t in range(TT):
                    for hp in range(8):
                        bank = begin("act_free")
                        pe.matmul(bank[:, :], d_qit[:, hp, t * P:(t + 1) * P], d_kit, start=True, stop=True) \
                            .then_inc(sem("unit_full"), E.up("unit_full"))
                pe.wait_ge(sem("bias_ready"), E.due("bias_ready"))
                pe.wait_ge(sem("kt_ready"), E.due("kt_ready"))
                attend(dsa_units())
                rwkv()
                for t in range(TT):
                    pe.wait_ge(sem("src_ready"), E.due("src_ready"))
                    for src in (ya[:, t, :], hb[:, t, R0:R0 + B_W]):
                        for k in (0, 4):
                            turn([src[:, (k + j) * P:(k + j + 1) * P] for j in range(4)], "raw_ready")
                pe.wait_ge(sem("feat_ready"), E.due("feat_ready"))
                gemm(g_out, feat_lhs(feat_e))

            def rwkv():
                pe.wait_ge(sem("rwkv_in"), 16 * 7)
                for t in range(TT):
                    pe.wait_ge(sem("lora_ready"), E.due("lora_ready"))
                    turn([hb[:, t, WL0:WL0 + 64], hb[:, t, AL0:AL0 + 64]])
                    pe.wait_ge(sem("lora_t"), E.due("lora_t"))
                    for j in range(2):
                        for half in range(2):
                            bank = begin("dve_free")
                            pe.matmul(bank[:, :], w_lt[0:64, j, :], w_w2[0:64, j, half * CH:(half + 1) * CH],
                                            start=True, stop=True).then_inc(sem("unit_full"), E.up("unit_full"))
                    pe.wait_ge(sem("sig_ready"), E.due("sig_ready"))
                    for half in range(2):
                        bank = begin("act_free")
                        pe.matmul(bank[:, :], tri[:, :], w_t[:, 0, half * CH:(half + 1) * CH], start=True, stop=True) \
                            .then_inc(sem("unit_full"), E.up("unit_full"))
                    bank = begin("act_free")
                    for hp in range(8):
                        mm = pe.matmul(bank[:, hp * 4:hp * 4 + 4], w_t[:, 0, hp * P:(hp + 1) * P], ind[:, :],
                                       start=True, stop=True)
                    mm.then_inc(sem("unit_full"), E.up("unit_full"))
                    pe.wait_ge(sem("arbk_ready"), E.due("arbk_ready"))
                    for a in (w_t[:, 1, :], hb[:, t, R0:R0 + B_W], w_t4, hb[:, t, K0:K0 + B_W]):
                        for h in (0, 4):
                            turn([a[:, (h + j) * P:(h + j + 1) * P] for j in range(4)])
                pe.wait_ge(sem("g2_in"), 32)
                for t in range(TT):
                    turn([hb[:, t, GL0:GL0 + P], hb[:, t, GL0 + P:GL0 + 160]])
                    pe.wait_ge(sem("lora_t"), E.due("lora_t"))
                    for half in range(2):
                        bank = begin("act_free")
                        cs = slice(half * CH, (half + 1) * CH)
                        pe.matmul(bank[:, :], w_lt[:, 2, :], w_g2a[:, 0, cs], start=True, stop=False)
                        pe.matmul(bank[:, :], w_lt[0:32, 3, :], w_g2a[0:32, 1, cs], start=False, stop=True) \
                            .then_inc(sem("unit_full"), E.up("unit_full"))

                def heads(owner, products, rows_out=RC, at=0):
                    banks = [begin(owner) for _ in range(2)]
                    for hp in range(8):
                        for o in range(2):
                            terms = products(hp, o)
                            n = terms[0][1].free_size()
                            for j, (lt, rhs) in enumerate(terms):
                                mm = pe.matmul(banks[o][64 * o + at:64 * o + at + rows_out, hp * n:(hp + 1) * n], lt, rhs,
                                               start=(j == 0), stop=(j == len(terms) - 1))
                            if hp == 7:
                                mm.then_inc(sem("unit_full"), E.up("unit_full"))

                ks = [slice(0, 64), slice(64, 128)]
                ts = [slice(0, RC), slice(64, 64 + RC)]
                two = [slice(0, 2 * RC), slice(64, 64 + 2 * RC)]
                for c in range(NRC):
                    heads("dve_free", lambda hp, o: [(w_bk[ks[o], hp, c, 0, :], w_ar[ks[o], hp, c, 0, :])])

                def within(c):
                    heads("dve_free", lambda hp, o: [(w_bk[ks[o], hp, c, 1, :],
                                                      w_ar[ks[o], hp, c, :, :].rearrange("p a t -> p (a t)"))])
                    heads("dve_free", lambda hp, o: [(w_bk[ks[o], hp, c, 0, :], w_ar[ks[o], hp, c, 1, :])], at=RC)

                within(0)
                for c in range(NRC):
                    pe.wait_ge(sem(f"kbv_in{c % 2}"), 96 * (c // 2 + 1))
                    kbv = w_kbv[c % 2]
                    pe.wait_ge(sem("G_ready"), E.due("G_ready"))
                    if c:
                        pe.wait_ge(sem("st_ready"), E.due("st_ready"))
                    state = lambda hp, o, j: [(w_ar[ks[o], hp, c, j, :], w_st[c % 2][ks[o], hp, :])] if c else []
                    heads("dve_free", lambda hp, o: state(hp, o, 0) + [(w_G[c % 2][ts[o], hp, 0, :], kbv[ts[o], 1, hp, :])])
                    if c < NRC - 1:
                        within(c + 1)
                    pe.wait_ge(sem("z_ready"), E.due("z_ready"))
                    if c == 0:
                        pe.wait_ge(sem("t_in"), 32)
                    heads("dve_free", lambda hp, o: [(w_tt[ts[o], c * 8 + hp, :], w_z[ts[o], hp * 64:hp * 64 + 64])], at=RC)
                    pe.wait_ge(sem("u_ready"), E.due("u_ready"))
                    if c < NRC - 1:
                        heads("dve_free", lambda hp, o: [(kbv[two[o], 0, hp, :], kbv[two[o], 1, hp, :])], rows_out=64)
                    heads("act_free", lambda hp, o: state(hp, o, 1) + [(w_G[c % 2][two[o], hp, 1, :], kbv[two[o], 1, hp, :])])

            def xat(l):
                g_q, g_kv, g_o = gemms[f"xat{l}"]
                turn_normed(x4)
                gemm(g_q, feat_lhs(feat), parts=True)
                turn_normed(memb)
                gemm(g_kv, feat_lhs(feat), parts=True)
                pe.wait_ge(sem("xqk_ready"), E.due("xqk_ready"))
                for t in range(TT):
                    turn([xa_q[:, t, j * P:(j + 1) * P] for j in range(4)])
                    turn([xa_kv[:, t, j * P:(j + 1) * P] for j in range(4)])
                pe.wait_ge(sem("qkt_ready"), E.due("qkt_ready"))
                attend(xat_units())
                turn_all(lambda t: xa_o[:, t, :], TT, 512)
                pe.wait_ge(sem("feat_ready"), E.due("feat_ready"))
                gemm(g_o, feat_lhs(xa_ot))

            def ffn(l):
                turn_normed(x4)
                for half in range(2):
                    g_up, g_down = gemms[f"ffn{l}"][2 * half:2 * half + 2]

                    def turn_hidden(c, i):
                        if c == 0:
                            return
                        for t in range(TT):
                            pe.wait_ge(sem("sq_ready"), E.due("sq_ready"))
                            bank = tp[len(tp_owners) % 4]
                            E.seen["raw_ready"] += 1
                            tp_given["raw_ready"] += 1
                            tp_owners.append(("raw_ready", tp_given["raw_ready"]))
                            pe.wait_ge(sem("raw_ready"), E.at("raw_ready", tp_given["raw_ready"] - 4))
                            for j in range(4):
                                mm = pe.transpose(bank[:, j * P:(j + 1) * P],
                                                  HID[(c - 1) % 2][:, t, j * P:(j + 1) * P], ident[:, :])
                            mm.then_inc(sem("tp_full"), E.up("tp_full"))
                        if c == g_up.lead + g_up.body - 1 and not isinstance(i, int):
                            for _ in range((g_up.turns - 1) * g_up.body * g_up.tiles):
                                tp_given["raw_ready"] += 1
                                tp_owners.append(("raw_ready", tp_given["raw_ready"]))

                    gemm(g_up, feat_lhs(feat), hook=turn_hidden, parts=half == 0)
                    for t in range(TT):
                        pe.wait_ge(sem("sq_ready"), E.due("sq_ready"))
                        turn([HID[1][:, t, j * P:(j + 1) * P] for j in range(4)], "raw_ready")
                    gemm(g_down, feat_lhs(hid_t), late=g_down.kt - 4)

            def odd():
                g_in, g_glu, g_out = gemms["odd"]
                pe.wait_ge(sem("lam_in"), 48)
                turn([s_lr[0:64, j, :] for j in range(2)])
                turn_normed(x4)

                def turn_b(c, i):
                    if c == 3:
                        for ri in range(2):
                            pe.wait_ge(sem("be_ready"), E.due("be_ready"))
                            for k in range(0, KT, 4):
                                turn([s_be[ri][:, (k + j) * 4:(k + j) * 4 + 4].rearrange("p r g i -> p (r g i)") for j in range(4)])

                gemm(g_in, feat_lhs(feat), hook=turn_b, parts=True)
                turn_all(lambda t: s_u[:, t, :], TT, D, "s_u_ready", "tp_free")
                pe.wait_ge(sem("feat_ready"), E.due("feat_ready"))
                pe.wait_ge(sem("b_ready"), E.due("b_ready"))
                NB = SEQ // S5_STEP
                per_bank = CH // S5_STEP
                for b in range(NB + 1):
                    if b < NB:
                        ts = slice(b * S5_STEP, (b + 1) * S5_STEP)
                        for k0 in range(0, KT, per_bank // 2):
                            banks = [begin("act_free") for _ in range(4)]
                            for j in range(4):
                                rows = slice(32 * j, 32 * j + 32)
                                for n in range(per_bank):
                                    k, ri = k0 + n // 2, n % 2
                                    mm = pe.matmul(banks[j][:, n * S5_STEP:(n + 1) * S5_STEP],
                                                   s_B[rows, k, ri, :], s_ut[rows, k, ts], start=True, stop=True)
                                mm.then_inc(sem("unit_full"), E.up("unit_full"))
                    if b == 0:
                        for ri in range(2):
                            for k in range(0, KT, 4):
                                turn([s_ce[ri][:, k + j].rearrange("p g s -> p (g s)") for j in range(4)])
                        pe.wait_ge(sem("c_ready"), E.due("c_ready"))
                    if b:
                        pe.wait_ge(sem("scan_done"), E.due("scan_done"))
                        for k0 in range(0, KT, per_bank):
                            bank = begin("dve_free")
                            for k in range(k0, k0 + per_bank):
                                for j in range(4):
                                    for ri in range(2):
                                        mm = pe.matmul(bank[32 * j:32 * j + 32, (k - k0) * S5_STEP:(k - k0 + 1) * S5_STEP],
                                                       s_C[:, k * 4 + j, ri, :], s_h[(b - 1) % 2][:, :, ri, k * 4 + j],
                                                       start=(ri == 0), stop=(ri == 1))
                            mm.then_inc(sem("unit_full"), E.up("unit_full"))
                gemm(g_glu, feat_lhs(s_zs), parts=True)
                pe.wait_ge(sem("sig_full"), E.due("sig_full"))
                for k in range(0, KT, 4):
                    for t in range(TT):
                        turn([s_sig[:, t, (k + j) * P:(k + j + 1) * P] for j in range(4)])
                gemm(g_out, feat_lhs(s_zs), parts=True)

            for l in range(2):
                block1(l)
            even()
            for l in range(2):
                if l == 1:
                    odd()
                xat(l)
                ffn(l)
        @block.scalar
        def _(act):
            E = Eng(act, sem, "act_step")
            f = act.activation
            g_n = 0
            turn_n = 0

            def take(name):
                nonlocal g_n
                act.wait_ge(sem(name), E.due(name))
                g_n += 1
                return acc[(g_n - 1) % 4][:, :]

            def skip(name, k):
                nonlocal g_n
                E.seen[name] += k
                g_n += k

            def round_hi(u, i=0, turn=0):
                g, c, s = uses[u] if u < len(uses) else (None, 0, 0)
                if g is None or not g.split:
                    return
                slot, kt, width = u % RING, g.chunk_slots()[s], g.cols[c][1]
                v = 16 * (u // RING + 1)
                act.wait_ge(sem(f"ring_full{slot}"), v if isinstance(i, int) else i * (16 * turn // RING) + v)
                f(ring_r[:, slot, 0, 0:kt, 0:width], ring[:, slot, 1, 0:kt, 0:width], ACT.Copy) \
                    .then_inc(sem("w_hi"), E.up("w_hi"))

            def stream(g, empty=None, counts=(), unroll=False):
                nonlocal g_n
                per = g.body * g.slots

                def chunk(c, i):
                    for s in range(g.slots):
                        if s == g.slots - 1 and empty:
                            empty(c, i)
                        for j in range(1 + len(g.riders)):
                            round_hi(g.q0 + (c * g.slots + s) * (1 + len(g.riders)) + j + RING, i, per)

                turns = g.turns - 1
                if turns < 2 or not empty or unroll:
                    turns = 0
                for c in range(g.lead if turns else 0):
                    chunk(c, 0)
                if turns:
                    n = g.body * g.tiles
                    slopes = {"gemm_full": n, "act_free": n} | {name: n for name in counts}
                    if g.split:
                        slopes["w_hi"] = per
                    with E.loop(turns, slopes) as i:
                        for b in range(g.body):
                            chunk(g.lead + b, i)
                    g_n += n * (turns - 1)
                for c in range(g.lead + turns * g.body if turns else 0, g.n):
                    chunk(c, 0)
                if not empty:
                    skip("gemm_full", g.n * g.tiles)

            def evac(g, fn, **kw):
                def empty(c, i):
                    n0, width = g.cols[c][0] - g.cols[0][0], g.cols[c][1]
                    if not isinstance(i, int):
                        n0 = i * (g.body * CH) + n0
                    for t in range(g.tiles):
                        fn(c, bass.ds(n0, width), t, take("gemm_full")[:, 0:width])
                    if g.name[:2] == "up" and c:
                        hi_parts(TT, CH, lambda t, k, n: hidden(c - 1, i, g.body, t))

                stream(g, empty, **kw)

            def hidden(c, i, body, t):
                at = 4 * c if isinstance(i, int) else i * (4 * body) + 4 * c
                return hid_t.at_reg(at, 4, slice(t * P, (t + 1) * P))

            def hi_parts(tiles, width, dst, by_k=False):
                if isinstance(dst, Pair):
                    d = dst
                    dst = lambda t, k, n: d.at(k, n, slice(t * P, (t + 1) * P))
                parts = [(t, k) for t in range(tiles) for k in range(0, width // P, 4)]
                for t, k in sorted(parts, key=lambda tk: tk[1]) if by_k else parts:
                    d_ = dst(t, k, min(4, width // P - k))
                    act.wait_ge(sem("raw_ready"), E.due("raw_ready"))
                    f(d_.hi, d_.raw, ACT.Copy).then_inc(sem("hi_ready"), E.up("hi_ready"))

            def copy_to(dst):
                return lambda c, cs, t, bank: f(dst[:, t, cs], bank, ACT.Copy).then_inc(sem("act_free"), E.up("act_free"))

            def square_sums(src, junk, tiles, eps_col):
                for t in range(tiles):
                    f(junk(t), src(t), ACT.Square, accum_out=stat[:, t:t + 1]).then_inc(sem("act_step"), E.up())
                act.wait_ge(E.last_sem(), E.last_count())
                f(stat2[:, 0:tiles], stat[:, 0:tiles], ACT.Sqrt, bias=eps[:, eps_col:eps_col + 1], scale=1.0 / D) \
                    .then_inc(sem("sd_ready"), E.up("sd_ready"))

            def root(n, n0=0):
                act.wait_ge(sem("ms_ready"), E.due("ms_ready"))
                f(stat2[:, n0:n], stat[:, n0:n], ACT.Sqrt).then_inc(sem("sd_ready"), E.up("sd_ready"))

            def attend(units):
                nonlocal g_n, turn_n
                n = len(units)
                for i in range(n + 2):
                    if i < n:
                        u, s = units[i], i % 2
                        act.wait_ge(sem("nmax_ready"), E.due("nmax_ready"))
                        nk = u["k"].shape[-1]
                        if u["bias"] is None:
                            bank = take("score_full")
                            f(prob[:, s, 0:nk], bank[:, 0:nk], ACT.Exp, bias=att_s[:, s:s + 1], scale=HD ** -0.5,
                                    accum_out=att_s[:, 2 + s:3 + s]).then_inc(sem("act_free"), E.up("act_free"))
                        else:
                            skip("score_full", 1)
                            f(prob[:, s, 0:nk], prob[:, s, 0:nk], ACT.Exp, bias=att_s[:, s:s + 1],
                                    accum_out=att_s[:, 2 + s:3 + s]).then_inc(sem("p_ready"), E.up("p_ready"))
                    if 0 <= i - 1 < n:
                        w = len(units[i - 1]["v"]) * P
                        bank, count = prob_turns[turn_n]
                        turn_n += 1
                        act.wait_ge(sem("tp_full"), count)
                        if i >= 3:
                            act.wait_ge(sem("pv_full"), E.due("pv_full"))
                        f(prob_t[:, (i - 1) % 2].rearrange("p k t -> p (k t)")[:, 0:w], tp[bank][:, 0:w], ACT.Copy) \
                            .then_inc(sem("prob_turned"), E.up("prob_turned"))
                    if i >= 2:
                        g_n += 1
                E.seen["pv_full"] += min(n, 2)

            for _ in range(4):
                act.nop().then_inc(sem("act_free"), E.up("act_free"))
            def act_dma(dst, src, name):
                act.dma_start(dst, src).then_inc(sem(name), 16)

            for l in range(2):
                act_dma(rows3[32 * l:32 * l + 32, :], I["b_mod"][l, 0:2 * D].rearrange("(k p) -> k p", p=P), "rows_in")
            for name, at in C1.items():
                act_dma(rows1[at:at + 16, :], I[name[:-1] + ("" if name[:-1] == "norm_w" else "_2")][int(name[-1])]
                    .rearrange("(k p) -> k p", p=P), "rows_in")
            src2 = {"norm_ffn0": I["norm_ffn_2"][0], "norm_ffn1": I["norm_ffn_2"][1], "s5_d": I["s5_d_2"][0],
                    "s5_b_glu": I["s5_b_glu_2"][0], "cq": I["dsa_cq_norm_2"][0]}
            for name, at in C2.items():
                src = I["b_sgu"][int(name[-1])] if "sgu" in name else src2[name].rearrange("(k p) -> k p", p=P)
                act_dma(rows2[at:at + src.shape[0], :], src, "rows_in")
            act.wait_ge(sem("cond_ready"), E.due("cond_ready"))
            f(silu_c[:, :, 0], cond[:, 0:KT], ACT.Silu).then_inc(sem("act_step"), E.up())
            f(silu_c[:, :, 1], cond[:, KT:], ACT.Silu).then_inc(sem("silu_ready"), E.up("silu_ready"))
            act.wait_ge(sem("trig_args"), E.due("trig_args"))
            f(trig[:, 0, :], angle[:, 0, 0:48], ACT.Sin).then_inc(sem("act_step"), E.up())
            f(trig[:, 1, :], angle[:, 1, 0:48], ACT.Sin).then_inc(sem("trig_ready"), E.up("trig_ready"))

            def project(item, to_mix=None):
                if item[0] == "rows":
                    return
                kind, n = item[0:2]
                if kind == "mod":
                    def keep(c, cs, t, bank):
                        if n >= 2:
                            if MODS[n - 2][1] < 8:
                                E.seen["cols_full"] = max(E.seen["cols_full"], sum(c < 8 for _, c in MODS[:n - 1]))
                                act.wait_ge(sem("cols_full"), E.seen["cols_full"])
                            else:
                                act.wait_ge(sem(f"g_out{n % 2}"), E.due(f"g_out{n % 2}", 64))
                        f(mod_s[:, n % 2], bank, ACT.Copy).then_inc(sem("act_free"), E.up("act_free"))
                        act.wait_ge(E.last_sem(), E.last_count())
                        act.nop() \
                            .then_inc(sem("mod_chunk" if MODS[n][1] < 8 else "gate_chunk"), E.count("mod_chunk" if MODS[n][1] < 8 else "gate_chunk"))
                    if n < 8:
                        evac(mods[n], keep)
                    else:
                        act.wait_ge(sem("gemm_full"), E.due("gemm_full"))
                        keep(0, 0, 0, tp[mods[n].bank][:, :])
                elif kind == "cols":
                    if MODS[n][1] < 8:
                        nonlocal g_n
                        g_n += 1
                elif kind == "in":
                    evac(n, lambda c, cs, t, bank: to_mix(item[2] + c, cs, t, bank), unroll=True)
                elif kind == "kv":
                    act.wait_ge(sem("za_used"), E.due("za_used", 2))
                    evac(n, lambda c, cs, t, bank: f(kvb[:, t], bank, ACT.Copy).then_inc(sem("act_free"), E.up("act_free")))
                else:
                    def keep_zb(c, cs, t, bank):
                        f(mixes[item[3]][:, t, B1_HALF + c * CH:B1_HALF + (c + 1) * CH], bank, ACT.Silu) \
                            .then_inc(sem("act_free"), E.up("act_free"))
                        if c == 0 and t == n.tiles - 1:
                            root(72, 32 if item[3] else 64)
                    evac(n, keep_zb)

            for item in mod_items:
                project(item)

            def block1(l):
                g_out = gemms[f"b1_{l}"][-1]
                mix, qb, tiles = mixes[l], qbs[l], g_out.tiles
                if l:
                    act.wait_ge(sem("x_ready"), E.due("x_ready"))
                else:
                    act.wait_ge(sem("x_in"), E.due("x_in", 32))
                square_sums(lambda t: x4_b1[:, t], lambda t: b1_junk[:, t], 4, 0)
                hi_parts(4, D, feat4, by_k=True)
                za = [0]
                n_q = [0]

                def to_mix(c, cs, t, bank):
                    n0 = c * CH
                    if c < 2:
                        f(mix[:, t, n0:n0 + CH], bank, ACT.Gelu_apprx_tanh).then_inc(sem("act_free"), E.up("act_free"))
                    elif c < 4:
                        f(vb[:, t, n0 - 1024:n0 - 1024 + CH], bank, ACT.Gelu_apprx_tanh) \
                            .then_inc(sem("act_free"), E.up("act_free"))
                    elif c < 6:
                        if za[0] >= 2:
                            act.wait_ge(sem("za_used"), E.due("za_used"))
                        f(stage[:, za[0] % 2], bank, ACT.Silu).then_inc(sem("act_free"), E.up("act_free"))
                        act.wait_ge(E.last_sem(), E.last_count())
                        act.nop().then_inc(sem("za_ready"), E.count("za_ready"))
                        za[0] += 1
                    elif l == 0:
                        if n_q[0] >= 2:
                            act.wait_ge(sem(f"q_out{n_q[0] % 2}"), E.due(f"q_out{n_q[0] % 2}", 16))
                        f(prob[:, n_q[0] % 2], bank, ACT.Copy).then_inc(sem("act_free"), E.up("act_free"))
                        act.wait_ge(E.last_sem(), E.last_count())
                        act.nop().then_inc(sem("q_chunk"), E.count("q_chunk"))
                        n_q[0] += 1
                    else:
                        f(qb[:, t, n0 - 3072:n0 - 3072 + CH], bank, ACT.Copy).then_inc(sem("act_free"), E.up("act_free"))

                for item in b1_items[l]:
                    project(item, to_mix)
                    if item[0] == "kv":
                        root(8 * tiles)
                act.wait_ge(E.last_sem(), E.last_count())
                act.nop().then_inc(sem("proj_done"), E.count("proj_done"))
                if l == 0:
                    act.wait_ge(sem("q_in"), E.due("q_in", 16))
                    for t in range(tiles):
                        for h in range(8):
                            f(prob[:, h // 4, h % 4 * HD:(h % 4 + 1) * HD], qb[:, t, h * HD:(h + 1) * HD], ACT.Square,
                                    accum_out=stat[:, 32 + t * 8 + h:33 + t * 8 + h]).then_inc(sem("act_step"), E.up())
                        act.wait_ge(E.last_sem(), E.last_count())
                    f(stat2[:, 32:64], stat[:, 32:64], ACT.Sqrt, bias=eps[:, 0:1], scale=1.0 / HD) \
                        .then_inc(sem("sd_ready"), E.up("sd_ready"))
                skip("unit_full", 2 * g_out.tiles)
                attend(b1_units(l))
                hi_parts(tiles, D, feat4, by_k=True)
                skip("unit_full", 8)
                stream(g_out)

            def even():
                g_in, g_uq, g_qi, g_uv, g_out = gemms["even"]
                act.wait_ge(sem("x_ready"), E.due("x_ready"))
                square_sums(lambda t: x4_b1[:, t], lambda t: xn_e[:, t], TT, 1)
                hi_parts(TT, D, feat_e, by_k=True)

                def to_hb(c, cs, t, bank):
                    if c == 7 and t == 1:
                        act.wait_ge(sem("x_out"), E.due("x_out", 16))
                    f(hb[:, t, cs], bank, ACT.Copy).then_inc(sem("act_free"), E.up("act_free"))
                    if c == 6 and t == 1:
                        act.wait_ge(E.last_sem(), E.last_count())
                        act.nop().then_inc(sem("lat_in"), E.count("lat_in"))
                        root(6)

                evac(g_in, to_hb)
                act.wait_ge(E.last_sem(), E.last_count())
                act.nop().then_inc(sem("even_h"), E.count("even_h"))
                evac(g_uq, lambda c, cs, t, bank: f(d_q[:, t, c * CH:(c + 1) * CH], bank, ACT.Copy) \
                    .then_inc(sem("act_free"), E.up("act_free")))
                evac(g_qi, lambda c, cs, t, bank: f(d_qi[:, t, c * CH:(c + 1) * CH], bank, ACT.Copy) \
                    .then_inc(sem("act_free"), E.up("act_free")))
                evac(g_uv, lambda c, cs, t, bank: f(d_v[:, t, c * CH:(c + 1) * CH], bank, ACT.Copy) \
                    .then_inc(sem("act_free"), E.up("act_free")))
                act.wait_ge(E.last_sem(), E.last_count())
                act.nop().then_inc(sem("dsa_proj"), E.count("dsa_proj"))
                for h in range(8):
                    f(d_kt[:, h, :], take("unit_full")[:, 0:SEQ], ACT.Copy).then_inc(sem("act_free"), E.up("act_free"))
                act.wait_ge(E.last_sem(), E.last_count())
                for h in range(8):
                    f(d_kt[0:32, h, :], d_krt[0:32, :], ACT.Copy).then_inc(sem("act_step"), E.up())
                act.wait_ge(E.last_sem(), E.last_count())
                act.nop().then_inc(sem("kt_ready"), E.count("kt_ready"))
                slots = [stage[:, 0], stage[:, 1], prob[:, 0], prob[:, 1]]
                for n in range(TT * 8):
                    bank = take("unit_full")
                    if n >= 4:
                        act.wait_ge(sem("rl_used"), E.due("rl_used"))
                    f(slots[n % 4], bank, ACT.Relu).then_inc(sem("act_free"), E.up("act_free"))
                    act.wait_ge(E.last_sem(), E.last_count())
                    act.nop().then_inc(sem("rl_ready"), E.count("rl_ready"))
                act.wait_ge(sem("rl_used"), E.due("rl_used", 4))
                attend(dsa_units())
                for t in range(TT):
                    if t == 0:
                        act.wait_ge(sem("mix_done"), E.due("mix_done"))
                        for u in range(TT):
                            f(hb[:, u, GL0:GL0 + 160], hb[:, u, GL0:GL0 + 160], ACT.Sigmoid) \
                                .then_inc(sem("act_step"), E.up())
                    f(hb[:, t, WL0:WL0 + 64], hb[:, t, WL0:WL0 + 64], ACT.Tanh) \
                        .then_inc(sem("lora_ready"), E.up("lora_ready"))
                    skip("unit_full", 4)
                    act.wait_ge(sem("pre_sig"), E.due("pre_sig"))
                    f(w_t[:, 0], w_t[:, 0], ACT.Sigmoid).then_inc(sem("act_step"), E.up())
                    f(w_t4, w_t4, ACT.Sigmoid).then_inc(sem("sig_ready"), E.up("sig_ready"))
                    root(B_H)
                    banks = [take("unit_full") for _ in range(3)]
                    act.wait_ge(sem("einv_go"), E.due("einv_go"))
                    for half in range(2):
                        ins = f(w_t[:, 2, half * CH:(half + 1) * CH], banks[half][:, :], ACT.Exp, scale=DECAY)
                        ins.then_inc(sem("einv_ready"), E.up("einv_ready"))
                    act.wait_ge(sem("einc_go"), E.due("einc_go"))
                    for half in range(2):
                        f(w_t[:, 2, half * CH:(half + 1) * CH], banks[half][:, :], ACT.Exp, scale=-DECAY) \
                            .then_inc(sem("act_free"), E.up("act_free"))
                    f(w_pc[:, :, t * 4:t * 4 + 4], banks[2][:, 0:32].rearrange("p (h c) -> p h c", c=4), ACT.Exp,
                            scale=-DECAY).then_inc(sem("act_free"), E.up("act_free"))
                    f(w_t[:, 0], w_t[:, 0], ACT.Exp, scale=-DECAY).then_inc(sem("eexc_ready"), E.up("eexc_ready"))
                act.wait_ge(sem("kbv_out"), E.due("kbv_out", 16 * 6 * TT))
                for t in range(TT):
                    for half in range(2):
                        f(hb[:, t, K0 + half * CH:K0 + (half + 1) * CH], take("unit_full")[:, :], ACT.Copy) \
                            .then_inc(sem("act_free"), E.up("act_free"))
                act.wait_ge(E.last_sem(), E.last_count())
                act.nop().then_inc(sem("gate_ready"), E.count("gate_ready"))
                skip("unit_full", 2 * NRC)
                skip("unit_full", 4)
                for c in range(NRC):
                    skip("unit_full", 10 if c < NRC - 1 else 4)
                    if c >= 2:
                        act.wait_ge(sem(f"o_out{c % 2}"), E.due(f"o_out{c % 2}", 32))
                    banks = [take("unit_full") for _ in range(2)]
                    for o in range(2):
                        ts = slice(64 * o, 64 * o + RC)
                        f(w_o[ts, c % 2], banks[o][ts, :], ACT.Copy).then_inc(sem("act_free"), E.up("act_free"))
                    act.wait_ge(E.last_sem(), E.last_count())
                    act.nop().then_inc(sem("o_ready"), E.count("o_ready"))
                for t in range(TT):
                    root((t + 1) * B_H, t * B_H)
                hi_parts(TT, D, feat_e)
                stream(g_out)

            def xat(l):
                g_q, g_kv, g_o = gemms[f"xat{l}"]
                act.wait_ge(sem("x_ready"), E.due("x_ready"))
                square_sums(lambda t: x4[:, t], lambda t: xn2[:, t], TT, 1)
                hi_parts(TT, D, feat, by_k=True)
                act.wait_ge(sem("mem_in"), E.due("mem_in", 16))
                square_sums(lambda t: memb[:, t], lambda t: xn2[:, t], TT, 1)
                evac(g_q, lambda c, cs, t, bank: f(xa_q[:, t], bank, ACT.Copy).then_inc(sem("act_free"), E.up("act_free")))
                hi_parts(TT, D, feat, by_k=True)
                evac(g_kv, lambda c, cs, t, bank: f(xa_kv[:, t, c * CH:(c + 1) * CH], bank, ACT.Copy) \
                    .then_inc(sem("act_free"), E.up("act_free")))
                act.wait_ge(E.last_sem(), E.last_count())
                act.nop().then_inc(sem("xqk_ready"), E.count("xqk_ready"))
                attend(xat_units())
                hi_parts(TT, 512, xa_ot)
                stream(g_o)

            def ffn(l):
                act.wait_ge(sem("x_ready"), E.due("x_ready"))
                square_sums(lambda t: x4[:, t], lambda t: xn2[:, t], TT, 1)
                hi_parts(TT, D, feat, by_k=True)

                def relu2(c, cs, t, bank):
                    dst = HID[c % 2][:, t]
                    f(dst, bank, ACT.Relu).then_inc(sem("act_free"), E.up("act_free"))
                    act.wait_ge(E.last_sem(), E.last_count())
                    f(dst, dst, ACT.Square).then_inc(sem("sq_ready"), E.up("sq_ready"))

                for half in range(2):
                    g_up, g_down = gemms[f"ffn{l}"][2 * half:2 * half + 2]
                    evac(g_up, relu2, counts=("sq_ready", "raw_ready", "hi_ready"))
                    hi_parts(TT, CH, lambda t, k, n: hidden(g_up.n - 1, 0, 0, t))
                    stream(g_down)

            def odd():
                g_in, g_glu, g_out = gemms["odd"]
                act.wait_ge(sem("x_ready"), E.due("x_ready"))
                square_sums(lambda t: x4[:, t], lambda t: xn2[:, t], TT, 1)
                hi_parts(TT, D, feat, by_k=True)
                act.wait_ge(sem("s5_ang"), E.due("s5_ang"))
                f(s_lam[:, 2], s_lam[:, 2], ACT.Exp).then_inc(sem("s5_dt"), E.up("s5_dt"))
                act.wait_ge(sem("s5_ang"), E.due("s5_ang"))
                f(s_lam[:, 3], s_lam[:, 3], ACT.Exp).then_inc(sem("act_step"), E.up())
                f(s_lam[:, 5], s_lam[:, 5], ACT.Sin).then_inc(sem("act_step"), E.up())
                f(s_lam[:, 6], s_lam[:, 6], ACT.Sin).then_inc(sem("s5_trig"), E.up("s5_trig"))
                evac(g_in, copy_to(s_u))
                act.wait_ge(E.last_sem(), E.last_count())
                act.nop().then_inc(sem("s_u_ready"), E.count("s_u_ready"))
                NB = SEQ // S5_STEP
                per_bank = CH // S5_STEP
                for b in range(NB + 1):
                    if b < NB:
                        if b == 1:
                            act.wait_ge(sem("c_ready"), E.due("c_ready"))
                        for k0 in range(0, KT, per_bank // 2):
                            for j in range(4):
                                bank = take("unit_full")
                                dst = s_h[b % 2].rearrange("p t r (k j) -> p j k r t", j=4)[:, j, k0:k0 + per_bank // 2]
                                f(dst, bank[:, :].rearrange("p (k r t) -> p k r t", r=2, t=S5_STEP), ACT.Copy) \
                                    .then_inc(sem("act_free"), E.up("act_free"))
                        act.wait_ge(E.last_sem(), E.last_count())
                        act.nop().then_inc(sem("bu_ready"), E.count("bu_ready"))
                    if b:
                        ts = slice((b - 1) * S5_STEP, b * S5_STEP)
                        for h, k0 in enumerate(range(0, KT, per_bank)):
                            skip("unit_full", 1)
                            act.wait_ge(sem("y_ready_s5"), E.due("y_ready_s5"))
                            f(s_ut[:, k0:k0 + per_bank, ts], stage[:, h].rearrange("p (k t) -> p k t", t=S5_STEP),
                                    ACT.Gelu_apprx_tanh).then_inc(sem("z_part"), E.up("z_part"))
                act.wait_ge(E.last_sem(), E.last_count())
                for k in range(0, KT, 4):
                    f(s_zs.hi[:, k:k + 4], s_ut[:, k:k + 4], ACT.Copy).then_inc(sem("hi_ready"), E.up("hi_ready"))
                evac(g_glu, copy_to(s_sig))
                act.wait_ge(E.last_sem(), E.last_count())
                act.nop().then_inc(sem("sig_full"), E.count("sig_full"))
                for k in range(0, KT, 4):
                    act.wait_ge(sem("pre_gate"), E.due("pre_gate"))
                    f(s_pre[:, k:k + 4], s_pre[:, k:k + 4], ACT.Sigmoid).then_inc(sem("gate_sig"), E.up("gate_sig"))
                for k in range(0, KT, 4):
                    act.wait_ge(sem("zg_ready"), E.due("zg_ready"))
                    f(s_zs.hi[:, k:k + 4], s_zs.raw[:, k:k + 4], ACT.Copy).then_inc(sem("hi_ready"), E.up("hi_ready"))
                stream(g_out)

            for l in range(2):
                block1(l)
            even()
            for l in range(2):
                if l == 1:
                    odd()
                xat(l)
                ffn(l)
            act.wait_ge(sem("x_ready"), E.due("x_ready"))
            square_sums(lambda t: x4[:, t], lambda t: xn2[:, t], TT, 1)
        @block.vector
        def _(dve):
            E = Eng(dve, sem, "dve_step")
            g_n, t_n = 0, 0

            def take(name):
                nonlocal g_n
                dve.wait_ge(sem(name), E.due(name))
                g_n += 1
                return acc[(g_n - 1) % 4][:, :]

            def skip(name, k):
                nonlocal g_n
                E.seen[name] += k
                g_n += k

            def turned():
                nonlocal t_n
                dve.wait_ge(sem("tp_full"), E.due("tp_full"))
                t_n += 1
                return tp[(t_n - 1) % 4]

            tt, stt = dve.tensor_tensor, dve.scalar_tensor_tensor

            def ts(out, a, s1, s2, op0, op1=None):
                return dve.tensor_scalar(out, a, s1, s2, op0, op1) if op1 is not None else dve.tensor_scalar(out, a, s1, s2, op0)

            def along(v, n):
                return v.unsqueeze(2).to_broadcast([v.shape[0], v.shape[1], n])

            def over(v, k):
                return v.unsqueeze(1).to_broadcast([v.shape[0], k, v.shape[1]])

            def blocks(v, d):
                return v.rearrange("p (h d) -> p h d", d=d)

            def norm(src, dst, tiles, name="src_ready"):
                dve.wait_ge(sem("sd_ready"), E.due("sd_ready"))
                dve.reciprocal(stat2[:, 0:tiles], stat2[:, 0:tiles]).then_inc(sem("dve_step"), E.up())
                dve.wait_ge(E.last_sem(), E.last_count())
                for t in range(tiles):
                    ts(dst(t), src(t), stat2[:, t:t + 1], None, ALU.mult).then_inc(sem(name), E.up(name))

            def take_lo(u):
                g, c, s = uses[u] if u < len(uses) else (None, 0, 0)
                if g is None or not g.split:
                    return
                slot, kt, width = u % RING, g.chunk_slots()[s], g.cols[c][1]
                dve.wait_ge(sem("w_hi"), E.due("w_hi"))
                raw, hi, lo = (r[:, slot, j, 0:kt, 0:width] for r, j in ((ring, 1), (ring_r, 0), (ring_r, 1)))
                tt(lo, raw, hi, ALU.subtract).then_inc(sem("w_lo"), E.up("w_lo"))

            def stream(g, hook=None, counts=(), unroll=False):
                nonlocal g_n, t_n
                per = g.body * g.slots

                def chunk(c, i):
                    for s in range(g.slots):
                        if s == g.slots - 1 and hook:
                            hook(c, i)
                        for j in range(1 + len(g.riders)):
                            take_lo(g.q0 + (c * g.slots + s) * (1 + len(g.riders)) + j + RING)

                turns = g.turns - 1
                if turns < 2 or not g.split or unroll:
                    turns = 0
                for c in range(g.lead if turns else 0):
                    chunk(c, 0)
                if turns:
                    n = g.body * g.tiles
                    with E.loop(turns, {"w_hi": per, "w_lo": per} | {name: n for name in counts}) as i:
                        for b in range(g.body):
                            chunk(g.lead + b, i)
                    t_n += n * (turns - 1) if counts else 0
                for c in range(g.lead + turns * g.body if turns else 0, g.n):
                    chunk(c, 0)
                if g.owner == "act_free":
                    skip("gemm_full", g.n * g.tiles)

            def norm_diag(tiles=TT, on=diag):
                dve.wait_ge(sem("sd_ready"), E.due("sd_ready"))
                dve.reciprocal(stat2[:, 0:tiles], stat2[:, 0:tiles]).then_inc(sem("dve_step"), E.up())
                dve.wait_ge(E.last_sem(), E.last_count())
                for t in range(tiles):
                    ts(on[:, t], ident[:, :], stat2[:, t:t + 1], None, ALU.mult).then_inc(sem("dve_step"), E.up())
                dve.wait_ge(E.last_sem(), E.last_count())
                dve.nop().then_inc(sem("diag_ready"), E.count("diag_ready"))

            def take_rest(d, name="dve_step"):
                dve.wait_ge(sem("hi_ready"), E.due("hi_ready"))
                tt(d.lo, d.raw, d.hi, ALU.subtract).then_inc(sem(name), E.up(name))

            def turn_parts(dst, tiles, scale=None, shift=None):
                todo = []
                for k in range(0, KT, 4):
                    for t in range(tiles):
                        bank = turned()[:, :].rearrange("p (k t) -> p k t", t=P)
                        d = dst.at(k, 4, slice(t * P, (t + 1) * P))
                        if scale is None:
                            dve.tensor_copy(d.raw, bank).then_inc(sem("raw_ready"), E.up("raw_ready"))
                        else:
                            tt(d.raw, bank, along(scale(t)[:, k:k + 4], P), ALU.mult) \
                                .then_inc(sem("dve_step" if shift else "raw_ready"), E.up("dve_step" if shift else "raw_ready"))
                        if shift is not None:
                            dve.wait_ge(E.last_sem(), E.last_count())
                            tt(d.raw, d.raw, along(shift(t)[:, k:k + 4], P), ALU.add) \
                                .then_inc(sem("raw_ready"), E.up("raw_ready"))
                        todo.append((d, "feat_part" if t == tiles - 1 else "dve_step"))
                        if len(todo) > 1:
                            take_rest(*todo[-2])
                take_rest(*todo[-1])

            def turn_split(dst, tiles, width, scale=None, shift=None):
                todo = []
                for t in range(tiles):
                    for k in range(0, width // P, 4):
                        n = min(4, width // P - k)
                        bank = turned()[:, 0:n * P].rearrange("p (k t) -> p k t", t=P)
                        d = dst.at(k, n, slice(t * P, (t + 1) * P))
                        if scale is None:
                            dve.tensor_copy(d.raw, bank).then_inc(sem("raw_ready"), E.up("raw_ready"))
                        else:
                            tt(d.raw, bank, along(scale(t)[:, k:k + n], P), ALU.mult) \
                                .then_inc(sem("dve_step" if shift else "raw_ready"), E.up("dve_step" if shift else "raw_ready"))
                        if shift is not None:
                            dve.wait_ge(E.last_sem(), E.last_count())
                            tt(d.raw, d.raw, along(shift(t)[:, k:k + n], P), ALU.add) \
                                .then_inc(sem("raw_ready"), E.up("raw_ready"))
                        todo.append(d)
                        if len(todo) > 1:
                            take_rest(todo[-2])
                take_rest(todo[-1])
                dve.wait_ge(E.last_sem(), E.last_count())
                dve.nop().then_inc(sem("feat_ready"), E.count("feat_ready"))

            def turn_evac(dst, tiles, width, scale=None, shift=None):
                for t in range(tiles):
                    for k in range(0, width // P, 4):
                        n = min(4, width // P - k)
                        bank = turned()[:, 0:n * P].rearrange("p (k t) -> p k t", t=P)
                        d = dst[:, k:k + n, t * P:(t + 1) * P]
                        if scale is None:
                            dve.tensor_copy(d, bank).then_inc(sem("tp_free"), E.up("tp_free"))
                        else:
                            tt(d, bank, along(scale(t)[:, k:k + n], P), ALU.mult).then_inc(sem("tp_free"), E.up("tp_free"))
                        if shift is not None:
                            dve.wait_ge(E.last_sem(), E.last_count())
                            tt(d, d, along(shift(t)[:, k:k + n], P), ALU.add).then_inc(sem("dve_step"), E.up())
                dve.wait_ge(E.last_sem(), E.last_count())
                dve.nop().then_inc(sem("feat_ready"), E.count("feat_ready"))

            def residual(g, done=True):
                def add(c, i):
                    for t in range(g.tiles):
                        bank = take("gemm_full")
                        x = x4[:, t, c * CH:(c + 1) * CH]
                        tt(x, x, bank[:, :], ALU.add).then_inc(sem("dve_free"), E.up("dve_free"))

                stream(g, add)
                if done:
                    dve.wait_ge(E.last_sem(), E.last_count())
                    dve.nop().then_inc(sem("x_ready"), E.count("x_ready"))

            def means(out, src, heads, d, sq):
                tt(sq, src, src, ALU.mult).then_inc(sem("dve_step"), E.up())
                dve.wait_ge(E.last_sem(), E.last_count())
                dve.tensor_reduce(out, blocks(sq, d), AX, ALU.add).then_inc(sem("dve_step"), E.up())

            def attend(units):
                nonlocal g_n, t_n
                n = len(units)
                for i in range(n + 2):
                    if i < n:
                        u, s = units[i], i % 2
                        nk = u["k"].shape[-1]
                        if u["bias"] is None:
                            dve.wait_ge(sem("score_full"), E.due("score_full"))
                            bank = acc[g_n % 4]
                            g_n += 1
                            dve.tensor_reduce(att_s[:, 4 + s:5 + s], bank[:, 0:nk], AX, ALU.max) \
                                .then_inc(sem("dve_step"), E.up())
                            dve.wait_ge(E.last_sem(), E.last_count())
                            ts(att_s[:, s:s + 1], att_s[:, 4 + s:5 + s], -HD ** -0.5, None, ALU.mult) \
                                .then_inc(sem("nmax_ready"), E.up("nmax_ready"))
                        else:
                            bank = take("score_full")
                            stt(prob[:, s, 0:nk], bank[:, 0:nk], HD ** -0.5, u["bias"], ALU.mult, ALU.add) \
                                .then_inc(sem("dve_free"), E.up("dve_free"))
                            dve.wait_ge(E.last_sem(), E.last_count())
                            dve.tensor_reduce(att_s[:, 4 + s:5 + s], prob[:, s, 0:nk], AX, ALU.max) \
                                .then_inc(sem("dve_step"), E.up())
                            dve.wait_ge(E.last_sem(), E.last_count())
                            ts(att_s[:, s:s + 1], att_s[:, 4 + s:5 + s], -1.0, None, ALU.mult) \
                                .then_inc(sem("nmax_ready"), E.up("nmax_ready"))
                    if 0 <= i - 1 < n:
                        dve.wait_ge(sem("tp_full"), E.due("tp_full"))
                        t_n += 1
                        dve.reciprocal(att_s[:, 8 + (i - 1) % 4:9 + (i - 1) % 4], att_s[:, 2 + (i - 1) % 2:3 + (i - 1) % 2]) \
                            .then_inc(sem("dve_step"), E.up())
                    if i >= 2:
                        u, r = units[i - 2], 8 + (i - 2) % 4
                        bank = take("pv_full")
                        dve.wait_ge(E.last_sem(), E.last_count())
                        if u["gated"]:
                            stt(u["out"], bank[:, 0:HD], att_s[:, r:r + 1], u["out"], ALU.mult, ALU.mult) \
                                .then_inc(sem("dve_free"), E.up("dve_free"))
                        else:
                            ts(u["out"], bank[:, 0:HD], att_s[:, r:r + 1], None, ALU.mult) \
                                .then_inc(sem("dve_free"), E.up("dve_free"))
                dve.wait_ge(E.last_sem(), E.last_count())

            def wrap(ang, r, rc):
                c1, c2, c3 = cody_waite()
                magic = 12582912.0
                top = 3.1415925
                ts(rc, ang, 1.0 / TWO_PI, magic, ALU.mult, ALU.add).then_inc(sem("dve_step"), E.up())
                dve.wait_ge(E.last_sem(), E.last_count())
                ts(rc, rc, -magic, None, ALU.add).then_inc(sem("dve_step"), E.up())
                dve.wait_ge(E.last_sem(), E.last_count())
                stt(r, rc, -c1, ang, ALU.mult, ALU.add).then_inc(sem("dve_step"), E.up())
                for c in (c2, c3):
                    dve.wait_ge(E.last_sem(), E.last_count())
                    stt(r, rc, -c, r, ALU.mult, ALU.add).then_inc(sem("dve_step"), E.up())
                dve.wait_ge(E.last_sem(), E.last_count())
                ts(rc, r, TWO_PI / 4, TWO_PI / 2, ALU.add, ALU.is_gt).then_inc(sem("dve_step"), E.up())
                dve.wait_ge(E.last_sem(), E.last_count())
                ts(rc, rc, -TWO_PI, TWO_PI / 4, ALU.mult, ALU.add).then_inc(sem("dve_step"), E.up())
                dve.wait_ge(E.last_sem(), E.last_count())
                tt(rc, rc, r, ALU.add).then_inc(sem("dve_step"), E.up())
                dve.wait_ge(E.last_sem(), E.last_count())
                for v in (r, rc):
                    ts(v, v, top, -top, ALU.min, ALU.max).then_inc(sem("dve_step"), E.up())

            dve.memset(silu_c[:, :, :], 0.0).then_inc(sem("dve_step"), E.up())
            dve.memset(eps[:, 0:1], 1e-6).then_inc(sem("dve_step"), E.up())
            dve.memset(eps[:, 1:2], 1e-5).then_inc(sem("dve_step"), E.up())
            dve.memset(eps[:, 2:3], 64e-5).then_inc(sem("dve_step"), E.up())
            dve.tensor_copy(cond[:, :], turned()[:, 0:2 * KT]).then_inc(sem("tp_free"), E.up("tp_free"))
            dve.wait_ge(E.last_sem(), E.last_count())
            dve.nop().then_inc(sem("cond_ready"), E.count("cond_ready"))
            dve.wait_ge(sem("consts"), 16 * CONSTS)
            tt(posi[:, :], tokid[:, :], frame[:, 0:1].to_broadcast([P, TT]), ALU.add).then_inc(sem("dve_step"), E.up())
            dve.wait_ge(E.last_sem(), E.last_count())
            dve.tensor_copy(stat[:, 0:TT], posi[:, :]).then_inc(sem("dve_step"), E.up())
            dve.wait_ge(E.last_sem(), E.last_count())
            for t in range(TT):
                ts(angle[:, 2, 24 * t:24 * t + 24], invf[:, :], stat[:, t:t + 1], None, ALU.mult) \
                    .then_inc(sem("dve_step"), E.up())
            dve.wait_ge(E.last_sem(), E.last_count())
            for t in range(TT):
                wrap(angle[:, 2, 24 * t:24 * t + 24], angle[:, t, 24:48], angle[:, t, 0:24])
            dve.wait_ge(E.last_sem(), E.last_count())
            dve.nop().then_inc(sem("trig_args"), E.count("trig_args"))

            def project(item, hook=None):
                nonlocal t_n
                if item[0] == "rows":
                    bank = turned()
                    dve.tensor_copy(cols1[:, :], bank[:, 0:P]).then_inc(sem("dve_step"), E.up())
                    dve.tensor_copy(cols2[:, 0:ROWS2], bank[:, P:P + ROWS2]).then_inc(sem("dve_step"), E.up())
                    dve.tensor_copy(cols3[:, :], bank[:, 2 * P:2 * P + 64]).then_inc(sem("tp_free"), E.up("tp_free"))
                    dve.wait_ge(E.last_sem(), E.last_count())
                    return
                kind, n = item[0:2]
                if kind == "mod":
                    if n < 8:
                        stream(mods[n])
                    else:
                        E.seen["gemm_full"] += 1
                        t_n += 1
                elif kind == "cols":
                    l, c = MODS[n]
                    if c < 8:
                        bank = take("cols_full")[:, 0:8].rearrange("p (k c) -> p k c", c=2)
                        part, k0 = c // 4, 4 * (c % 4)
                        for z in range(2):
                            at = mod_col(l, z, part)[:, k0:k0 + 4]
                            tt(at, bank[:, :, z], cols3[:, 32 * l + 4 * c:32 * l + 4 * c + 4], ALU.add) \
                                .then_inc(sem("dve_free" if z else "dve_step"), E.up("dve_free" if z else "dve_step"))
                        if part:
                            dve.wait_ge(E.last_sem(), E.last_count())
                            for z in range(2):
                                at = mod_col(l, z, part)[:, k0:k0 + 4]
                                stt(at, at, 1.0, col(f"norm_w{l}")[:, k0:k0 + 4], ALU.add, ALU.mult) \
                                    .then_inc(sem("dve_step"), E.up())
                        dve.wait_ge(E.last_sem(), E.last_count())
                else:
                    stream(n, hook, unroll=True)

            for item in mod_items:
                project(item)

            def block1(l):
                g_out = gemms[f"b1_{l}"][-1]
                tiles = g_out.tiles
                mix, qb = mixes[l], qbs[l]
                norm_diag(4, diag4)
                turn_parts(feat4, 4, lambda t: mod_col(l, t // 2, 1), lambda t: mod_col(l, t // 2, 0))
                def gate_u(c, i):
                    for t in range(tiles if c in (4, 5) else 0):
                        dve.wait_ge(sem("za_ready"), E.due("za_ready"))
                        m = mix[:, t, (c - 4) * CH:(c - 3) * CH]
                        tt(m, m, stage[:, ((c - 4) * tiles + t) % 2], ALU.mult).then_inc(sem("za_used"), E.up("za_used"))
                    if c == 5:
                        dve.wait_ge(E.last_sem(), E.last_count())
                        for t in range(tiles):
                            means(stat[:, t * 8:t * 8 + 8], vb[:, t], 8, HD, stage[:, :, :].rearrange("p a b -> p (a b)"))
                            dve.wait_ge(E.last_sem(), E.last_count())
                        ts(stat[:, 0:8 * tiles], stat[:, 0:8 * tiles], 1.0 / HD, 1e-6, ALU.mult, ALU.add) \
                            .then_inc(sem("ms_ready"), E.up("ms_ready"))
                        dve.wait_ge(E.last_sem(), E.last_count())
                        dve.nop().then_inc(sem("stage_free"), E.count("stage_free"))

                def norm_v():
                    dve.wait_ge(sem("sd_ready"), E.due("sd_ready"))
                    dve.reciprocal(stat2[:, 0:8 * tiles], stat2[:, 0:8 * tiles]).then_inc(sem("dve_step"), E.up())
                    dve.wait_ge(E.last_sem(), E.last_count())
                    for t in range(tiles):
                        v = blocks(vb[:, t], HD)
                        tt(v, v, along(stat2[:, t * 8:t * 8 + 8], HD), ALU.mult).then_inc(sem("dve_step"), E.up())
                    dve.wait_ge(sem("vnw_in"), E.due("vnw_in", 16))
                    dve.wait_ge(E.last_sem(), E.last_count())
                    for t in range(tiles):
                        tt(vb[:, t], vb[:, t], vnw_row, ALU.mult).then_inc(sem("vn_ready"), E.up("vn_ready"))

                def means_q():
                    for t in range(tiles):
                        means(stat[:, 32 + t * 8:40 + t * 8], qb[:, t], 8, HD, sq)
                        dve.wait_ge(E.last_sem(), E.last_count())

                sq = prob[:, :, :].rearrange("p a b -> p (a b)")

                def norm_heads(t, w):
                    v, n, r = ((blocks(kvb[:, t, 0:256], HD), 2, stat2[:, 64 + t * 2:66 + t * 2]) if w else
                               (blocks(qb[:, t], HD), 8, stat2[:, 32 + t * 8:40 + t * 8]))
                    tt(v, v, along(r, HD), ALU.mult).then_inc(sem("dve_step"), E.up())
                    dve.wait_ge(E.last_sem(), E.last_count())
                    tt(v, v, over(qk_w[:, l, w], n), ALU.mult).then_inc(sem("dve_step"), E.up())
                    dve.wait_ge(E.last_sem(), E.last_count())
                    if t < TT:
                        rot = sq[:, 0:n * HD]
                        for a in range(2):
                            sin = rope[:, 1, t].rearrange("p (r a d) -> p r a d", r=2, a=2)[:, :, a, :]
                            for hh in range(2):
                                pick = lambda z, x: z.rearrange("p h (r a d) -> p h r a d", r=2, a=2)[:, :, hh, x, :]
                                tt(pick(blocks(rot, HD), a), pick(v, 1 - a), over(sin[:, hh], n), ALU.mult) \
                                    .then_inc(sem("dve_step"), E.up())
                        dve.wait_ge(E.last_sem(), E.last_count())
                        tt(v, v, over(rope[:, 0, t], n), ALU.mult).then_inc(sem("dve_step"), E.up())
                        dve.wait_ge(E.last_sem(), E.last_count())
                        tt(v, v, blocks(rot, HD), ALU.add).then_inc(sem("dve_step"), E.up())
                        dve.wait_ge(E.last_sem(), E.last_count())

                def norm_early(c, i):
                    if c:
                        return
                    first = 32 if l else 64
                    dve.wait_ge(sem("sd_ready"), E.due("sd_ready"))
                    dve.reciprocal(stat2[:, first:72], stat2[:, first:72]).then_inc(sem("dve_step"), E.up())
                    dve.wait_ge(E.last_sem(), E.last_count())
                    for t in range(4):
                        norm_heads(t, 1)
                        if l and t < tiles:
                            norm_heads(t, 0)

                for item in b1_items[l]:
                    project(item, (lambda c, i: gate_u(item[2] + c, i)) if item[0] == "in" else norm_early if item[0] == "zb" else None)
                    if item[0] == "kv":
                        norm_v()
                        if l == 0:
                            for j in range(2):
                                dve.wait_ge(sem(f"q_out{j}"), 16 * 4)
                        for t in range(4):
                            means(stat[:, 64 + t * 2:66 + t * 2], kvb[:, t, 0:256], 2, HD, sq[:, 0:256])
                            dve.wait_ge(E.last_sem(), E.last_count())
                        if l:
                            means_q()
                        first = 32 if l else 64
                        ts(stat[:, first:72], stat[:, first:72], 1.0 / HD, 1e-6, ALU.mult, ALU.add) \
                            .then_inc(sem("ms_ready"), E.up("ms_ready"))
                dve.wait_ge(sem("proj_done"), E.due("proj_done"))
                for h in range(2):
                    dve.tensor_copy(sgu_t[:, h * 4:h * 4 + 4], turned()[:, :].rearrange("p (k t) -> p k t", t=P)) \
                        .then_inc(sem("tp_free"), E.up("tp_free"))
                dve.wait_ge(E.last_sem(), E.last_count())
                dve.nop().then_inc(sem("sgu_t_ready"), E.count("sgu_t_ready"))
                for t in range(tiles):
                    for half in range(2):
                        bank = take("unit_full")
                        for j in range(4):
                            g = half * 4 + j
                            m = mix[:, t, g * P:(g + 1) * P]
                            stt(m, bank[:, j * P:(j + 1) * P], col(f"b_sgu{l}", 8)[:, g:g + 1], m, ALU.add, ALU.mult) \
                                .then_inc(sem("dve_free" if j == 3 else "dve_step"), E.up("dve_free" if j == 3 else "dve_step"))
                dve.wait_ge(E.last_sem(), E.last_count())
                dve.nop().then_inc(sem("sgu_done"), E.count("sgu_done"))
                if l == 0:
                    dve.wait_ge(sem("sd_ready"), E.due("sd_ready"))
                    dve.reciprocal(stat2[:, 32:64], stat2[:, 32:64]).then_inc(sem("dve_step"), E.up())
                    dve.wait_ge(E.last_sem(), E.last_count())
                for t in range(4):
                    if l == 0:
                        norm_heads(t, 0)
                    dve.wait_ge(E.last_sem(), E.last_count())
                    dve.nop().then_inc(sem("qk_ready"), E.count("qk_ready"))
                for t in range(4):
                    if t < tiles:
                        for h in range(2):
                            dve.tensor_copy(q_t[:, h * 4:h * 4 + 4, t * P:(t + 1) * P],
                                                  turned()[:, :].rearrange("p (k t) -> p k t", t=P)) \
                                                      .then_inc(sem("tp_free"), E.up("tp_free"))
                    dve.tensor_copy(k_t[:, :, t * P:(t + 1) * P],
                                          turned()[:, 0:2 * P].rearrange("p (k t) -> p k t", t=P)) \
                                              .then_inc(sem("tp_free"), E.up("tp_free"))
                dve.wait_ge(E.last_sem(), E.last_count())
                dve.nop().then_inc(sem("qkt_ready"), E.count("qkt_ready"))
                attend(b1_units(l))
                dve.wait_ge(E.last_sem(), E.last_count())
                dve.nop().then_inc(sem("att_done"), E.count("att_done"))
                dve.wait_ge(sem("gate_in"), E.due("gate_in", 16))
                for c in range(4):
                    for cond_ in (1, 0):
                        cs = slice(c * CH, (c + 1) * CH)
                        tt(gate[:, cond_, cs], take("unit_full")[:, :], gate_b[:, cs], ALU.add) \
                            .then_inc(sem("dve_free"), E.up("dve_free"))
                dve.wait_ge(E.last_sem(), E.last_count())
                for t in range(tiles):
                    dve.nop().then_inc(sem("src_ready"), E.up("src_ready"))
                turn_parts(feat4, tiles)
                if l == 0:
                    dve.wait_ge(E.last_sem(), E.last_count())
                    dve.nop().then_inc(sem("mix_turned"), E.count("mix_turned"))

                def add_gated(c, i):
                    for t in range(tiles):
                        bank = take("gemm_full")
                        cs = slice(c * CH, (c + 1) * CH)
                        tt(stage[:, t % 2], bank[:, :], gate[:, t // 2, cs], ALU.mult) \
                            .then_inc(sem("dve_free"), E.up("dve_free"))
                        dve.wait_ge(E.last_sem(), E.last_count())
                        tt(x4_b1[:, t, cs], x4_b1[:, t, cs], stage[:, t % 2], ALU.add).then_inc(sem("dve_step"), E.up())

                if l == 0:
                    dve.wait_ge(sem("x_again"), E.due("x_again", 32))
                stream(g_out, add_gated, unroll=True)
                dve.wait_ge(E.last_sem(), E.last_count())
                dve.nop().then_inc(sem("x_ready"), E.count("x_ready"))

            def rotate(v1, v2, cos, sin, tmp, n, d):
                q = [tmp[:, j * n * d:(j + 1) * n * d].rearrange("p (h d) -> p h d", d=d) for j in range(4)]
                tt(q[0], v1, over(cos, n), ALU.mult).then_inc(sem("dve_step"), E.up())
                tt(q[1], v2, over(sin, n), ALU.mult).then_inc(sem("dve_step"), E.up())
                tt(q[2], v2, over(cos, n), ALU.mult).then_inc(sem("dve_step"), E.up())
                tt(q[3], v1, over(sin, n), ALU.mult).then_inc(sem("dve_step"), E.up())
                dve.wait_ge(E.last_sem(), E.last_count())
                tt(v1, q[0], q[1], ALU.subtract).then_inc(sem("dve_step"), E.up())
                tt(v2, q[2], q[3], ALU.add).then_inc(sem("dve_step"), E.up())
                dve.wait_ge(E.last_sem(), E.last_count())

            def even():
                g_in, g_uq, g_qi, g_uv, g_out = gemms["even"]
                norm_diag()
                dve.wait_ge(E.last_sem(), E.last_count())
                dve.nop().then_inc(sem("x_norm_even"), E.count("x_norm_even"))
                turn_parts(feat_e, TT, lambda t: col("norm_mix0"))
                dve.memset(d_uk[:, :, :, 0:32], 0.0).then_inc(sem("dve_step"), E.up())
                dve.memset(d_kit, 0.0).then_inc(sem("dve_step"), E.up())
                dve.wait_ge(E.last_sem(), E.last_count())
                dve.nop().then_inc(sem("uk_zero"), E.count("uk_zero"))

                def latents(c, i):
                    if c != 6:
                        return
                    dve.wait_ge(sem("lat_in"), E.due("lat_in"))
                    for t in range(TT):
                        for j, (c0, cw) in enumerate(((0, 512), (512, 256), (800, 64))):
                            v = hb[:, t, c0:c0 + cw]
                            tt(d_tmp[:, 0:cw], v, v, ALU.mult).then_inc(sem("dve_step"), E.up())
                            dve.wait_ge(E.last_sem(), E.last_count())
                            s = stat[:, 3 * t + j:3 * t + j + 1]
                            dve.tensor_reduce(s, d_tmp[:, 0:cw], AX, ALU.add).then_inc(sem("dve_step"), E.up())
                            dve.wait_ge(E.last_sem(), E.last_count())
                            ts(s, s, 1.0 / cw, 1e-5, ALU.mult, ALU.add).then_inc(sem("dve_step"), E.up())
                    dve.wait_ge(E.last_sem(), E.last_count())
                    dve.nop().then_inc(sem("ms_ready"), E.count("ms_ready"))
                    dve.wait_ge(sem("sd_ready"), E.due("sd_ready"))
                    dve.reciprocal(stat2[:, 0:6], stat2[:, 0:6]).then_inc(sem("dve_step"), E.up())
                    dve.wait_ge(sem("trig_ready"), E.due("trig_ready"))
                    dve.wait_ge(sem("dsa_in"), E.due("dsa_in", 64))
                    dve.wait_ge(E.last_sem(), E.last_count())
                    for t in range(TT):
                        for j, (c0, cw) in enumerate(((0, 512), (512, 256), (800, 64))):
                            v = hb[:, t, c0:c0 + cw]
                            dst = v if j < 2 else d_kid[:, t, 0:64]
                            ts(dst, v, stat2[:, 3 * t + j:3 * t + j + 1], None, ALU.mult).then_inc(sem("dve_step"), E.up())
                            if j:
                                dve.wait_ge(E.last_sem(), E.last_count())
                                tt(dst, dst, d_ckw if j == 1 else d_kiw, ALU.mult).then_inc(sem("dve_step"), E.up())
                        ts(hb[:, t, 864:880], hb[:, t, 864:880], 0.25 * 0.125, None, ALU.mult) \
                            .then_inc(sem("dve_step"), E.up())
                        dve.wait_ge(E.last_sem(), E.last_count())
                        rotate(hb[:, t, 768:784].unsqueeze(1), hb[:, t, 784:800].unsqueeze(1),
                               trig[:, t, 0:16], trig[:, t, 24:40], d_tmp, 1, 16)
                        rotate(d_kid[:, t, 0:8].unsqueeze(1), d_kid[:, t, 8:16].unsqueeze(1),
                               trig[:, t, 16:24], trig[:, t, 40:48], d_tmp, 1, 8)
                        dve.tensor_copy(d_kid[:, t, 64:128], d_kid[:, t, 0:64]).then_inc(sem("dve_step"), E.up())
                    dve.wait_ge(E.last_sem(), E.last_count())
                    dve.nop().then_inc(sem("lat_ready"), E.count("lat_ready"))

                stream(g_in, latents)
                dve.wait_ge(sem("even_h"), E.due("even_h"))
                dve.wait_ge(sem("x_out"), E.due("x_out", 16))
                for t in range(TT):
                    cs = slice(t * P, (t + 1) * P)
                    sq = lambda b, n: b[:, 0:n * P].rearrange("p (k t) -> p k t", t=P)
                    tt(d_cqt[:, :, cs], sq(turned(), 4), along(col("cq", 4), P), ALU.mult) \
                        .then_inc(sem("tp_free"), E.up("tp_free"))
                    dve.tensor_copy(d_ckt[:, :, cs], sq(turned(), 2)).then_inc(sem("tp_free"), E.up("tp_free"))
                    bank = turned()
                    dve.tensor_copy(d_kit[0:64, t * P:(t + 1) * P], bank[0:64, 0:P]).then_inc(sem("dve_step"), E.up())
                    dve.tensor_copy(d_kit[64:128, SEQ + t * P:SEQ + (t + 1) * P], bank[64:128, 0:P]) \
                        .then_inc(sem("dve_step"), E.up())
                    dve.tensor_copy(d_krt[0:32, cs], bank[0:32, P:2 * P]).then_inc(sem("tp_free"), E.up("tp_free"))
                dve.wait_ge(E.last_sem(), E.last_count())
                dve.nop().then_inc(sem("lat_t_ready"), E.count("lat_t_ready"))
                for g in (g_uq, g_qi, g_uv):
                    stream(g)
                skip("unit_full", 8)
                dve.wait_ge(sem("dsa_proj"), E.due("dsa_proj"))
                for t in range(TT):
                    q = blocks(d_q[:, t], HD)
                    rotate(q[:, :, 0:16], q[:, :, 16:32], trig[:, t, 0:16], trig[:, t, 24:40], d_tmp, 8, 16)
                    q = blocks(d_qi[:, t], 64)
                    rotate(q[:, :, 0:8], q[:, :, 8:16], trig[:, t, 16:24], trig[:, t, 40:48], d_tmp, 16, 8)
                    dve.wait_ge(E.last_sem(), E.last_count())
                    dve.nop().then_inc(sem("dq_ready"), E.count("dq_ready"))
                    for dst in (d_qt, d_qit):
                        for h in range(2):
                            dve.tensor_copy(dst[:, h * 4:h * 4 + 4, t * P:(t + 1) * P],
                                                  turned()[:, :].rearrange("p (k t) -> p k t", t=P)) \
                                                      .then_inc(sem("tp_free"), E.up("tp_free"))
                dve.wait_ge(E.last_sem(), E.last_count())
                dve.nop().then_inc(sem("dqt_ready"), E.count("dqt_ready"))
                slots = [stage[:, 0], stage[:, 1], prob[:, 0], prob[:, 1]]
                for t in range(TT):
                    score = d_score[:, t]
                    for hp in range(8):
                        dve.wait_ge(sem("rl_ready"), E.due("rl_ready"))
                        r = slots[(t * 8 + hp) % 4]
                        for o in range(2):
                            h = 2 * hp + o
                            w = hb[:, t, 864 + h:865 + h]
                            name = "rl_used" if o else "dve_step"
                            if h == 0:
                                ts(score, r[:, 0:SEQ], w, None, ALU.mult).then_inc(sem("dve_step"), E.up())
                            else:
                                stt(score, r[:, o * SEQ:(o + 1) * SEQ], w, score, ALU.mult, ALU.add) \
                                    .then_inc(sem(name), E.up(name))
                            dve.wait_ge(E.last_sem(), E.last_count())
                    for half in range(2):
                        limit = (2 * t + half + 1) * 64
                        if limit < SEQ:
                            dve.memset(d_score[64 * half:64 * half + 64, t, limit:], NEG).then_inc(sem("dve_step"), E.up())
                    dve.wait_ge(E.last_sem(), E.last_count())
                    work = d_work[:, t]
                    for r in range(8):
                        src = d_score[:, t] if r == 0 else work
                        dve.max(d_top, src).then_inc(sem("dve_step"), E.up())
                        dve.wait_ge(E.last_sem(), E.last_count())
                        dve.match_replace(out=work, in_to_replace=d_top, in_values=src, imm_value=TAKEN) \
                            .then_inc(sem("dve_step"), E.up())
                        dve.wait_ge(E.last_sem(), E.last_count())
                    ts(d_bias[:, t], work, TAKEN, None, ALU.is_equal).then_inc(sem("dve_step"), E.up())
                    dve.wait_ge(E.last_sem(), E.last_count())
                    ts(d_bias[:, t], d_bias[:, t], -1.0, 1e30, ALU.add, ALU.mult).then_inc(sem("dve_step"), E.up())
                skip("unit_full", 16)
                dve.wait_ge(E.last_sem(), E.last_count())
                dve.nop().then_inc(sem("bias_ready"), E.count("bias_ready"))
                attend(dsa_units())
                dve.wait_ge(E.last_sem(), E.last_count())
                dve.nop().then_inc(sem("dsa_done"), E.count("dsa_done"))
                rwkv()
                turn_split(feat_e, TT, D)
                dve.wait_ge(sem("x_back"), E.due("x_back", 16))
                residual(g_out)

            def rwkv():
                dve.memset(w_sh[0:1, 0], 0.0) \
                    .then_inc(sem("dve_step"), E.up())
                dve.wait_ge(E.last_sem(), E.last_count())
                dve.wait_ge(sem("mu_in"), E.due("mu_in", 32))
                dve.wait_ge(sem("shift_in0"), E.due("shift_in0", 16))
                for t in range(TT):
                    if t:
                        dve.wait_ge(sem("shift_in"), E.due("shift_in", 32))
                    parts = [(hb[:, t, A_COLS + c0:A_COLS + c0 + cw], w_sh[:, t, c0:c0 + cw], mu)
                             for c0, cw, mu in ((0, 2048, w_mu[0]), (2048, 1312, w_mu[1]))]
                    for h, s, mu in parts:
                        tt(s, s, h, ALU.subtract).then_inc(sem("dve_step"), E.up())
                        dve.wait_ge(E.last_sem(), E.last_count())
                        tt(s, s, mu, ALU.mult).then_inc(sem("dve_step"), E.up())
                    if t:
                        dve.wait_ge(E.last_sem(), E.last_count())
                        for h, s, mu in before + parts:
                            tt(h, h, s, ALU.add).then_inc(sem("dve_step"), E.up())
                    before = parts
                dve.wait_ge(E.last_sem(), E.last_count())
                dve.nop().then_inc(sem("mix_done"), E.count("mix_done"))
                dve.wait_ge(sem("rwkv_in"), E.due("rwkv_in", 16 * 7))
                for t in range(TT):
                    T0, T1, T2, T4 = w_t[:, 0], w_t[:, 1], w_t[:, 2], w_t4
                    r, k, v = (hb[:, t, o:o + B_W] for o in (R0, K0, V0))
                    w0, a0, kk, ka, rk = (w_row[:, j] for j in range(5))
                    bank = turned()
                    dve.tensor_copy(w_lt[0:64, 0:2], bank[0:64, 0:2 * P].rearrange("p (k t) -> p k t", t=P)) \
                        .then_inc(sem("tp_free"), E.up("tp_free"))
                    dve.wait_ge(E.last_sem(), E.last_count())
                    dve.nop().then_inc(sem("lora_t"), E.count("lora_t"))
                    if t:
                        dve.wait_ge(sem("kbv_out"), E.due("kbv_out", 16 * 6))
                    for dst, b in ((T0, w0), (T4, a0)):
                        for half in range(2):
                            cs = slice(half * CH, (half + 1) * CH)
                            tt(dst[:, cs], take("unit_full")[:, :], b[:, cs], ALU.add) \
                                .then_inc(sem("dve_free"), E.up("dve_free"))
                    dve.wait_ge(E.last_sem(), E.last_count())
                    dve.nop().then_inc(sem("pre_sig"), E.count("pre_sig"))
                    tt(T1, k, kk, ALU.mult).then_inc(sem("dve_step"), E.up())
                    dve.wait_ge(E.last_sem(), E.last_count())
                    means(stat[:, 0:B_H], T1, B_H, B_D, T2)
                    dve.wait_ge(E.last_sem(), E.last_count())
                    ts(stat[:, 0:B_H], stat[:, 0:B_H], 1e-24, None, ALU.max).then_inc(sem("ms_ready"), E.up("ms_ready"))
                    dve.wait_ge(sem("sd_ready"), E.due("sd_ready"))
                    dve.reciprocal(stat2[:, 0:B_H], stat2[:, 0:B_H]).then_inc(sem("dve_step"), E.up())
                    dve.wait_ge(E.last_sem(), E.last_count())
                    tt(blocks(T1, B_D), blocks(T1, B_D), along(stat2[:, 0:B_H], B_D), ALU.mult) \
                        .then_inc(sem("dve_step"), E.up())
                    stt(T2, T4, -1.0, ka, ALU.add, ALU.mult).then_inc(sem("dve_step"), E.up())
                    dve.wait_ge(E.last_sem(), E.last_count())
                    stt(k, T2, 1.0, k, ALU.add, ALU.mult).then_inc(sem("dve_step"), E.up())
                    dve.wait_ge(E.last_sem(), E.last_count())
                    tt(T2, r, k, ALU.mult).then_inc(sem("dve_step"), E.up())
                    dve.wait_ge(E.last_sem(), E.last_count())
                    tt(T2, T2, rk, ALU.mult).then_inc(sem("dve_step"), E.up())
                    dve.wait_ge(E.last_sem(), E.last_count())
                    dve.tensor_reduce(w_bon[:, t], blocks(T2, B_D), AX, ALU.add).then_inc(sem("dve_step"), E.up())
                    tt(T4, T4, T1, ALU.mult).then_inc(sem("dve_step"), E.up())
                    dve.wait_ge(E.last_sem(), E.last_count())
                    dve.nop().then_inc(sem("einv_go"), E.count("einv_go"))
                    banks = [take("unit_full") for _ in range(3)]
                    dve.wait_ge(sem("einv_ready"), E.due("einv_ready", 2))
                    for half in range(2):
                        cs = slice(half * CH, (half + 1) * CH)
                        tt(T0[:, cs], banks[half][:, :], T0[:, cs], ALU.subtract).then_inc(sem("dve_step"), E.up())
                    tt(k, k, T2, ALU.mult).then_inc(sem("dve_step"), E.up())
                    tt(T4, T4, T2, ALU.mult).then_inc(sem("dve_step"), E.up())
                    dve.wait_ge(E.last_sem(), E.last_count())
                    dve.nop().then_inc(sem("einc_go"), E.count("einc_go"))
                    dve.wait_ge(sem("eexc_ready"), E.due("eexc_ready"))
                    tt(r, r, T2, ALU.mult).then_inc(sem("dve_step"), E.up())
                    tt(T1, T1, T0, ALU.mult).then_inc(sem("dve_step"), E.up())
                    dve.wait_ge(E.last_sem(), E.last_count())
                    dve.nop().then_inc(sem("arbk_ready"), E.count("arbk_ready"))
                    for dst, j in ((w_ar, 0), (w_ar, 1), (w_bk, 0), (w_bk, 1)):
                        for h in range(2):
                            bank = turned()[:, :].rearrange("p (h c t) -> p h c t", h=4, t=RC)
                            dve.tensor_copy(dst[:, h * 4:h * 4 + 4, t * 4:t * 4 + 4, j, :], bank) \
                                .then_inc(sem("tp_free"), E.up("tp_free"))
                dve.wait_ge(E.last_sem(), E.last_count())
                dve.nop().then_inc(sem("rows_done"), E.count("rows_done"))
                for t in range(TT):
                    bank = turned()
                    dve.tensor_copy(w_lt[:, 2], bank[:, 0:P]).then_inc(sem("dve_step"), E.up())
                    dve.tensor_copy(w_lt[0:32, 3], bank[0:32, P:2 * P]).then_inc(sem("tp_free"), E.up("tp_free"))
                    dve.wait_ge(E.last_sem(), E.last_count())
                    dve.nop().then_inc(sem("lora_t"), E.count("lora_t"))
                    skip("unit_full", 2)
                dve.wait_ge(sem("gate_ready"), E.due("gate_ready"))
                strict, upto = (lambda o, n: over(mask32[64 * o:64 * o + RC, 0:RC], n)), (lambda o, n: over(mask32[64 * o:64 * o + RC, RC:], n))
                for c in range(NRC):
                    if c >= 2:
                        dve.wait_ge(sem(f"a_out{c % 2}"), E.due(f"a_out{c % 2}", 32))
                    for o in range(2):
                        rs = slice(64 * o, 64 * o + RC)
                        bank = take("unit_full")
                        tt(blocks(w_a[rs, c % 2], RC), blocks(bank[rs, 0:8 * RC], RC), strict(o, 8), ALU.mult) \
                            .then_inc(sem("dve_free"), E.up("dve_free"))
                    dve.wait_ge(E.last_sem(), E.last_count())
                    dve.nop().then_inc(sem("a_ready"), E.count("a_ready"))
                dve.wait_ge(sem("solve_in"), E.due("solve_in", 16))
                flat_t = w_T.rearrange("p s t -> p (s t)")
                dve.memset(flat_t, 0.0).then_inc(sem("dve_step"), E.up())
                dve.wait_ge(E.last_sem(), E.last_count())
                dve.memset(flat_t[:, 0:RC * RC:RC + 1], 1.0).then_inc(sem("dve_step"), E.up())
                dve.wait_ge(E.last_sem(), E.last_count())
                for i in range(1, RC):
                    tt(w_tm[:, 0:i, 0:i], w_T[:, 0:i, 0:i], over(w_A[:, 0:i, i], i), ALU.mult) \
                        .then_inc(sem("dve_step"), E.up())
                    dve.wait_ge(E.last_sem(), E.last_count())
                    dve.tensor_reduce(w_T[:, 0:i, i], w_tm[:, 0:i, 0:i], AX, ALU.add, negate=True) \
                        .then_inc(sem("dve_step"), E.up())
                    dve.wait_ge(E.last_sem(), E.last_count())
                dve.wait_ge(E.last_sem(), E.last_count())
                dve.nop().then_inc(sem("solved"), E.count("solved"))
                rs = [slice(64 * o, 64 * o + RC) for o in range(2)]

                us = [slice(64 * o + RC, 64 * o + 2 * RC) for o in range(2)]

                def within(c):
                    G = w_G[c % 2]
                    for o in range(2):
                        bank = take("unit_full")[rs[o], :].rearrange("p (h a t) -> p h a t", a=2, t=RC)
                        for a, m in ((0, strict), (1, upto)):
                            tt(G[rs[o], :, a, :], bank[:, :, a, :], m(o, 8), ALU.mult) \
                                .then_inc(sem("dve_free" if a else "dve_step"), E.up("dve_free" if a else "dve_step"))
                    for o in range(2):
                        bank = take("unit_full")[us[o], 0:8 * RC]
                        tt(G[us[o], :, 1, :], blocks(bank, RC), over(mask32[us[o], RC:], 8), ALU.mult) \
                            .then_inc(sem("dve_free"), E.up("dve_free"))
                    dve.wait_ge(E.last_sem(), E.last_count())
                    dve.nop().then_inc(sem("G_ready"), E.count("G_ready"))

                within(0)
                for c in range(NRC):
                    for o in range(2):
                        dve.tensor_copy(w_z[rs[o]], take("unit_full")[rs[o], :]).then_inc(sem("dve_free"), E.up("dve_free"))
                    dve.wait_ge(E.last_sem(), E.last_count())
                    dve.nop().then_inc(sem("z_ready"), E.count("z_ready"))
                    if c < NRC - 1:
                        within(c + 1)
                    for o in range(2):
                        ts(w_kbv[c % 2][us[o], 1].rearrange("p h d -> p (h d)"), take("unit_full")[us[o], :], -1.0, None, ALU.mult) \
                            .then_inc(sem("dve_free"), E.up("dve_free"))
                    dve.wait_ge(E.last_sem(), E.last_count())
                    dve.nop().then_inc(sem("u_ready"), E.count("u_ready"))
                    if c < NRC - 1:
                        new = w_st[(c + 1) % 2]
                        for o in range(2):
                            ks = slice(64 * o, 64 * o + 64)
                            old, dst = (w[ks].rearrange("p h d -> p (h d)") for w in (w_st[c % 2], new))
                            bank = take("unit_full")[ks, :]
                            if c == 0:
                                dve.tensor_copy(dst, bank).then_inc(sem("dve_free"), E.up("dve_free"))
                            else:
                                tt(dst, old, bank, ALU.add).then_inc(sem("dve_free"), E.up("dve_free"))
                        dve.wait_ge(E.last_sem(), E.last_count())
                        tt(new, new, along(w_pc[:, :, c], B_D), ALU.mult).then_inc(sem("dve_step"), E.up())
                        dve.wait_ge(E.last_sem(), E.last_count())
                        dve.nop().then_inc(sem("st_ready"), E.count("st_ready"))
                    skip("unit_full", 2)
                dve.wait_ge(sem("unit_full"), E.seen["unit_full"])
                dve.wait_ge(sem("ln_in"), E.due("ln_in", 32))
                for t in range(TT):
                    dve.wait_ge(sem(f"o_in{t}"), E.due(f"o_in{t}", 16))
                    o = hb[:, t, R0:R0 + B_W]
                    m = stat[:, t * B_H:(t + 1) * B_H]
                    dve.tensor_reduce(m, blocks(o, B_D), AX, ALU.add).then_inc(sem("dve_step"), E.up())
                    dve.wait_ge(E.last_sem(), E.last_count())
                    ts(m, m, 1.0 / B_D, None, ALU.mult).then_inc(sem("dve_step"), E.up())
                    dve.wait_ge(E.last_sem(), E.last_count())
                    tt(blocks(o, B_D), blocks(o, B_D), along(m, B_D), ALU.subtract).then_inc(sem("dve_step"), E.up())
                    dve.wait_ge(E.last_sem(), E.last_count())
                    means(m, o, B_H, B_D, w_t[:, 0])
                    dve.wait_ge(E.last_sem(), E.last_count())
                    ts(m, m, 1.0 / B_D, 64e-5, ALU.mult, ALU.add).then_inc(sem("ms_ready"), E.up("ms_ready"))
                    g, v = (hb[:, t, x:x + B_W] for x in (K0, V0))
                    tt(blocks(w_t[:, 0], B_D), blocks(v, B_D), along(w_bon[:, t], B_D), ALU.mult) \
                        .then_inc(sem("dve_step"), E.up())
                    dve.wait_ge(sem("sd_ready"), E.due("sd_ready"))
                    sd = stat2[:, t * B_H:(t + 1) * B_H]
                    dve.reciprocal(sd, sd).then_inc(sem("dve_step"), E.up())
                    dve.wait_ge(E.last_sem(), E.last_count())
                    tt(blocks(o, B_D), blocks(o, B_D), along(stat2[:, t * B_H:(t + 1) * B_H], B_D), ALU.mult) \
                        .then_inc(sem("dve_step"), E.up())
                    dve.wait_ge(E.last_sem(), E.last_count())
                    tt(o, o, w_ln[0], ALU.mult).then_inc(sem("dve_step"), E.up())
                    dve.wait_ge(E.last_sem(), E.last_count())
                    tt(o, o, w_ln[1], ALU.add).then_inc(sem("dve_step"), E.up())
                    dve.wait_ge(E.last_sem(), E.last_count())
                    tt(o, o, w_t[:, 0], ALU.add).then_inc(sem("dve_step"), E.up())
                    dve.wait_ge(E.last_sem(), E.last_count())
                    tt(o, o, g, ALU.mult).then_inc(sem("src_ready"), E.up("src_ready"))
                    dve.wait_ge(E.last_sem(), E.last_count())
                dve.wait_ge(E.last_sem(), E.last_count())
                dve.nop().then_inc(sem("rwkv_done"), E.count("rwkv_done"))

            def xat(l):
                g_q, g_kv, g_o = gemms[f"xat{l}"]
                dve.wait_ge(E.last_sem(), E.last_count())
                dve.nop().then_inc(sem("mem_free"), E.count("mem_free"))
                norm_diag()
                turn_parts(feat, TT, lambda t: col(f"norm_xattn{l}"))
                norm_diag()
                stream(g_q)
                turn_parts(feat, TT, lambda t: col(f"norm_mem{l}"))
                stream(g_kv)
                for t in range(TT):
                    for dst in (xa_qt, xa_kt):
                        dve.tensor_copy(dst[:, :, t * P:(t + 1) * P],
                                              turned()[:, :].rearrange("p (k t) -> p k t", t=P)) \
                                                  .then_inc(sem("tp_free"), E.up("tp_free"))
                dve.wait_ge(E.last_sem(), E.last_count())
                dve.nop().then_inc(sem("qkt_ready"), E.count("qkt_ready"))
                attend(xat_units())
                for t in range(TT):
                    dve.nop().then_inc(sem("src_ready"), E.up("src_ready"))
                turn_split(xa_ot, TT, 512)
                residual(g_o)

            def ffn(l):
                if l == 0:
                    dve.wait_ge(E.last_sem(), E.last_count())
                    dve.nop().then_inc(sem("lr_free"), E.count("lr_free"))
                norm_diag()
                turn_parts(feat, TT, lambda t: col(f"norm_ffn{l}"))
                for half in range(2):
                    g_up, g_down = gemms[f"ffn{l}"][2 * half:2 * half + 2]

                    def hidden(c, i):
                        at = 4 * (c - 1)
                        if c == 0:
                            return
                        if not isinstance(i, int):
                            at = i * (4 * g_up.body) + at
                        parts = [hid_t.at_reg(at, 4, slice(t * P, (t + 1) * P)) for t in range(TT)]
                        for d in parts:
                            bank = turned()[:, :].rearrange("p (k t) -> p k t", t=P)
                            dve.tensor_copy(d.raw, bank).then_inc(sem("raw_ready"), E.up("raw_ready"))
                        for d in parts:
                            take_rest(d)

                    stream(g_up, hidden, ("tp_full", "raw_ready", "hi_ready", "dve_step"))
                    hidden(g_up.n, 0)
                    dve.wait_ge(E.last_sem(), E.last_count())
                    dve.nop().then_inc(sem("feat_ready"), E.count("feat_ready"))
                    residual(g_down, done=half == 1)

            def odd():
                g_in, g_glu, g_out = gemms["odd"]
                dve.wait_ge(E.last_sem(), E.last_count())
                dve.nop().then_inc(sem("s5_free"), E.count("s5_free"))
                lam = lambda j: s_lam[:, j]
                bank = turned()
                dve.tensor_copy(lam(0), bank[:, 0:PAIRS]).then_inc(sem("dve_step"), E.up())
                dve.tensor_copy(lam(1), bank[:, P:P + PAIRS]).then_inc(sem("tp_free"), E.up("tp_free"))
                norm_diag()
                dve.wait_ge(E.last_sem(), E.last_count())
                dve.nop().then_inc(sem("x_norm_odd"), E.count("x_norm_odd"))
                turn_parts(feat, TT, lambda t: col("norm_mix1"))
                dve.wait_ge(sem("lam_in"), E.due("lam_in", 48))
                for g in range(2):
                    rs = slice(64 * g, 64 * g + 64)
                    dve.tensor_copy(s_lam[rs, 2], s_ld[rs, g::2]).then_inc(sem("dve_step"), E.up())
                dve.wait_ge(E.last_sem(), E.last_count())
                ts(lam(0), lam(0), -1e-4, None, ALU.min).then_inc(sem("dve_step"), E.up())
                dve.wait_ge(E.last_sem(), E.last_count())
                dve.nop().then_inc(sem("s5_ang"), E.count("s5_ang"))
                dve.wait_ge(sem("s5_dt"), E.due("s5_dt"))
                tt(lam(3), lam(0), lam(2), ALU.mult).then_inc(sem("dve_step"), E.up())
                tt(lam(4), lam(1), lam(2), ALU.mult).then_inc(sem("dve_step"), E.up())
                dve.wait_ge(E.last_sem(), E.last_count())
                wrap(lam(4), lam(5), lam(6))
                dve.wait_ge(E.last_sem(), E.last_count())
                dve.nop().then_inc(sem("s5_ang"), E.count("s5_ang"))
                dve.wait_ge(sem("s5_trig"), E.due("s5_trig"))
                tt(lam(7), lam(3), lam(6), ALU.mult).then_inc(sem("dve_step"), E.up())
                tt(lam(8), lam(3), lam(5), ALU.mult).then_inc(sem("dve_step"), E.up())
                tt(lam(10), lam(0), lam(0), ALU.mult).then_inc(sem("dve_step"), E.up())
                tt(lam(11), lam(1), lam(1), ALU.mult).then_inc(sem("dve_step"), E.up())
                dve.wait_ge(E.last_sem(), E.last_count())
                tt(lam(10), lam(10), lam(11), ALU.add).then_inc(sem("dve_step"), E.up())
                ts(lam(9), lam(7), -1.0, None, ALU.add).then_inc(sem("dve_step"), E.up())
                dve.wait_ge(E.last_sem(), E.last_count())
                dve.reciprocal(lam(10), lam(10)).then_inc(sem("dve_step"), E.up())
                tt(lam(2), lam(9), lam(0), ALU.mult) \
                    .then_inc(sem("dve_step"), E.up())
                tt(lam(3), lam(8), lam(1), ALU.mult).then_inc(sem("dve_step"), E.up())
                tt(lam(5), lam(8), lam(0), ALU.mult).then_inc(sem("dve_step"), E.up())
                tt(lam(6), lam(9), lam(1), ALU.mult).then_inc(sem("dve_step"), E.up())
                dve.wait_ge(E.last_sem(), E.last_count())
                tt(lam(2), lam(2), lam(3), ALU.add).then_inc(sem("dve_step"), E.up())
                tt(lam(5), lam(5), lam(6), ALU.subtract).then_inc(sem("dve_step"), E.up())
                dve.wait_ge(E.last_sem(), E.last_count())
                tt(lam(2), lam(2), lam(10), ALU.mult).then_inc(sem("dve_step"), E.up())
                tt(lam(5), lam(5), lam(10), ALU.mult).then_inc(sem("dve_step"), E.up())
                for j in range(2):
                    dve.tensor_copy(s_l2[:, 0, j], lam(7)).then_inc(sem("dve_step"), E.up())
                dve.tensor_copy(s_l2[:, 1, 0], lam(8)).then_inc(sem("dve_step"), E.up())
                ts(s_l2[:, 1, 1], lam(8), -1.0, None, ALU.mult).then_inc(sem("dve_step"), E.up())
                dve.wait_ge(E.last_sem(), E.last_count())
                dve.wait_ge(sem("s5_in"), E.due("s5_in", 64))
                t1, t2 = (x[:, :, :].rearrange("p a b -> p (a b)").rearrange("p (r i) -> p r i", i=16) for x in (stage, prob))
                for ri in range(2):
                    dve.memset(s_be[ri], 0.0).then_inc(sem("dve_step"), E.up())
                    tt(t1, (s_br, s_bi)[ri], along(lam(2), 16), ALU.mult).then_inc(sem("dve_step"), E.up())
                    tt(t2, (s_bi, s_br)[ri], along(lam(5), 16), ALU.mult).then_inc(sem("dve_step"), E.up())
                    dve.wait_ge(E.last_sem(), E.last_count())
                    for g in range(2):
                        rs = slice(64 * g, 64 * g + 64)
                        tt(s_be[ri][rs, :, g, :], t1[rs], t2[rs], ALU.add if ri else ALU.subtract) \
                            .then_inc(sem("dve_step"), E.up())
                    dve.wait_ge(E.last_sem(), E.last_count())
                    dve.nop().then_inc(sem("be_ready"), E.count("be_ready"))
                for ri in range(2):
                    for g in range(2):
                        ts(s_ce[ri][:, :, g, :], s_cn[ri], gmask[:, g:g + 1], -1.0 if ri else 1.0, ALU.mult, ALU.mult) \
                            .then_inc(sem("dve_step"), E.up())

                def take_b(c, i):
                    if c == 3:
                        dve.wait_ge(sem("x_out"), E.due("x_out", 16))
                        for ri in range(2):
                            for k in range(0, KT, 4):
                                dve.tensor_copy(s_B[:, k:k + 4, ri, :], turned()[:, :].rearrange("p (k t) -> p k t", t=P)) \
                                    .then_inc(sem("tp_free"), E.up("tp_free"))
                        dve.wait_ge(E.last_sem(), E.last_count())
                        dve.nop().then_inc(sem("b_ready"), E.count("b_ready"))

                stream(g_in, take_b)
                turn_evac(s_ut, TT, D)
                for ri in range(2):
                    for k in range(0, KT, 4):
                        dve.tensor_copy(s_C[:, 4 * k:4 * k + 16, ri, :],
                                              turned()[:, :].rearrange("p (k c) -> p k c", c=32)) \
                                                  .then_inc(sem("tp_free"), E.up("tp_free"))
                dve.wait_ge(E.last_sem(), E.last_count())
                dve.nop().then_inc(sem("c_ready"), E.count("c_ready"))
                NB = SEQ // S5_STEP
                re_im, carry = s_car[:, 0:2], s_car[:, 2]

                def step(h, prev):
                    halves = [slice(0, PAIRS // 2), slice(PAIRS // 2, PAIRS)]
                    for k in halves:
                        both = prev[:, :, k].unsqueeze(1).to_broadcast([P, 2, 2, PAIRS // 2])
                        dve.wait_ge(sem("dve_step"), E.at("dve_step", E.cnt["dve_step"] - 1))
                        tt(re_im[:, :, :, k], both, s_l2[:, :, :, k], ALU.mult).then_inc(sem("dve_step"), E.up())
                    for k in halves:
                        dve.wait_ge(sem("dve_step"), E.at("dve_step", E.cnt["dve_step"] - 1))
                        tt(h[:, :, k], h[:, :, k], re_im[:, 0, :, k], ALU.add).then_inc(sem("dve_step"), E.up())
                    for k in halves:
                        dve.wait_ge(sem("dve_step"), E.at("dve_step", E.cnt["dve_step"] - 1))
                        tt(h[:, :, k], h[:, :, k], re_im[:, 1, ::-1, k], ALU.add).then_inc(sem("dve_step"), E.up())

                def scan(buf, t0, t1):
                    for t in range(t0, t1):
                        step(buf[:, t], buf[:, t - 1])

                part = 9
                per_bank = CH // S5_STEP
                for b in range(NB + 1):
                    if b < NB:
                        skip("unit_full", 2 * KT * S5_STEP * 4 // CH)
                        buf = s_h[b % 2]
                        dve.wait_ge(sem("bu_ready"), E.due("bu_ready"))
                        if b:
                            step(buf[:, 0], carry)
                        scan(buf, 1, part)
                    if b:
                        ts_ = slice((b - 1) * S5_STEP, b * S5_STEP)
                        for h, k0 in enumerate(range(0, KT, per_bank)):
                            y = stage[:, h].rearrange("p (k t) -> p k t", t=S5_STEP)
                            ks = slice(k0, k0 + per_bank)
                            if b >= 2:
                                dve.wait_ge(sem("z_part"), E.due("z_part"))
                            tt(y, s_ut[:, ks, ts_], along(col("s5_d")[:, ks], S5_STEP), ALU.mult) \
                                .then_inc(sem("dve_step"), E.up())
                            dve.wait_ge(E.last_sem(), E.last_count())
                            bank = take("unit_full")[:, :].rearrange("p (k t) -> p k t", t=S5_STEP)
                            tt(y, y, bank, ALU.add).then_inc(sem("dve_free"), E.up("dve_free"))
                            dve.wait_ge(E.last_sem(), E.last_count())
                            dve.nop().then_inc(sem("y_ready_s5"), E.count("y_ready_s5"))
                    if b < NB:
                        scan(buf, part, S5_STEP)
                        dve.wait_ge(E.last_sem(), E.last_count())
                        dve.tensor_copy(carry, buf[:, S5_STEP - 1]).then_inc(sem("dve_step"), E.up())
                        dve.wait_ge(E.last_sem(), E.last_count())
                        dve.nop().then_inc(sem("scan_done"), E.count("scan_done"))
                dve.wait_ge(E.last_sem(), E.last_count())
                dve.nop().then_inc(sem("s5_done"), E.count("s5_done"))
                for k in range(0, KT, 4):
                    dve.wait_ge(sem("hi_ready"), E.due("hi_ready"))
                    tt(s_zs.lo[:, k:k + 4], s_ut[:, k:k + 4], s_zs.hi[:, k:k + 4], ALU.subtract) \
                        .then_inc(sem("feat_part"), E.up("feat_part"))
                stream(g_glu)
                for k in range(0, KT, 4):
                    for t in range(TT):
                        bank = turned()[:, :].rearrange("p (k t) -> p k t", t=P)
                        tt(s_pre[:, k:k + 4, t * P:(t + 1) * P], bank, along(col("s5_b_glu")[:, k:k + 4], P), ALU.add) \
                            .then_inc(sem("tp_free"), E.up("tp_free"))
                    dve.wait_ge(E.last_sem(), E.last_count())
                    dve.nop().then_inc(sem("pre_gate"), E.count("pre_gate"))
                for k in range(0, KT, 4):
                    dve.wait_ge(sem("gate_sig"), E.due("gate_sig"))
                    tt(s_zs.raw[:, k:k + 4], s_ut[:, k:k + 4], s_pre[:, k:k + 4], ALU.mult) \
                        .then_inc(sem("zg_ready"), E.up("zg_ready"))
                for k in range(0, KT, 4):
                    dve.wait_ge(sem("hi_ready"), E.due("hi_ready"))
                    tt(s_zs.lo[:, k:k + 4], s_zs.raw[:, k:k + 4], s_zs.hi[:, k:k + 4], ALU.subtract) \
                        .then_inc(sem("feat_part"), E.up("feat_part"))
                dve.wait_ge(sem("x_back"), E.due("x_back", 16))
                residual(g_out)

            for l in range(2):
                block1(l)
            even()
            for l in range(2):
                if l == 1:
                    odd()
                xat(l)
                ffn(l)
            dve.wait_ge(E.last_sem(), E.last_count())
            dve.nop().then_inc(sem("fin_free"), E.count("fin_free"))
            norm(lambda t: x4[:, t], lambda t: xn2[:, t], TT, "dve_step")
            dve.wait_ge(sem("fin_in"), E.due("fin_in", 16))
            dve.wait_ge(E.last_sem(), E.last_count())
            for t in range(TT):
                tt(xn2[:, t], xn2[:, t], view(8192, D), ALU.mult).then_inc(sem("y_ready"), E.up("y_ready"))
_INS = ["x", "c", "ctx", "c_ctx", "norm_w", "w_mod", "b_mod", "w_in", "w_sgu", "b_sgu", "v_norm_w", "q_norm_w",
        "k_norm_w", "w_out"] + [n + "_2" for n in (
            "mem", "start_frame", "norm_mix", "norm_xattn", "norm_mem", "norm_ffn", "final_norm", "xattn_wq",
            "xattn_wkv", "xattn_wo", "ffn_up", "ffn_down", "even_w_in", "even_w_out", "dsa_cq_norm", "dsa_ckv_norm",
            "dsa_kidx_norm", "dsa_w_uq", "dsa_w_uk", "dsa_w_uv", "dsa_w_qidx", "rwkv_mu", "rwkv_w0", "rwkv_w2",
            "rwkv_a0", "rwkv_a2", "rwkv_g2", "rwkv_k_k", "rwkv_k_a", "rwkv_r_k", "rwkv_ln_w", "rwkv_ln_b", "odd_w_in",
            "odd_w_out", "s5_lam_re", "s5_lam_im", "s5_log_dt", "s5_b_re", "s5_b_im", "s5_c_re", "s5_c_im", "s5_d",
            "s5_w_glu", "s5_b_glu")]


def constants():
    s = np.arange(P)
    chunk = s // RC
    c = {"ident": np.eye(P), "tri": (chunk[:, None] == chunk[None]) & (s[:, None] <= s[None]),
         "ind": chunk[:, None] == np.arange(P // RC)[None],
         "gmask": (s[:, None] // 16) % 2 == np.arange(2)[None],
         "sel": s[:, None] % 32 == np.arange(2)[None],
         "sel8": np.repeat((np.arange(8)[:, None] % 2 == np.arange(2)[None])[:, :, None], P, 2)}
    a = np.arange(RC)
    m = np.concatenate([a[:, None] < a[None], a[:, None] <= a[None]], 1)
    c["mask32"] = np.tile(m, (P // RC, 1))
    n = np.arange(SEQ)
    freq = np.power(10000.0, (-np.arange(0, 64, 2, dtype=np.float32) / np.float32(64)).astype(np.float64)).astype(np.float32)
    ar, ac = ((p.astype(np.float32)[:, None] * freq) for p in (n // 64, n % 64))
    ang = np.concatenate([ar, ar, ac, ac], 1).astype(np.float64)
    sign = np.tile(np.repeat([-1.0, 1.0], 32), 2)
    c["cos"], c["sin"] = np.cos(ang), np.sin(ang) * sign
    inv = [np.power(500000.0, (-np.arange(0, r, 2, dtype=np.float32) / np.float32(r)).astype(np.float64)) for r in (32, 16)]
    c["invf"] = np.concatenate(inv)
    c = {k: np.ascontiguousarray(v, dtype=np.float32) for k, v in c.items()}
    c["tokid"] = (s[:, None] + P * np.arange(TT)[None]).astype(np.int32)
    return c


def kernel(**inputs):
    import concourse.bacc as bacc
    from concourse.bass_utils import run_bass_kernel_spmd

    nc = bacc.Bacc("TRN2", target_bir_lowering=False, num_devices=1)
    arrays = {n: np.ascontiguousarray(inputs[n]) for n in _INS}
    arrays |= {"const_" + n: a for n, a in constants().items()}
    aps = {n: nc.dram_tensor("in_" + n, a.shape, mybir.dt.from_np(a.dtype), kind="ExternalInput").ap()
           for n, a in arrays.items()}
    out = nc.dram_tensor("out_x", (1, SEQ, D), F32, kind="ExternalOutput").ap()
    two_blocks(nc, aps, out)
    r = run_bass_kernel_spmd(nc, [{"in_" + n: a for n, a in arrays.items()}], core_ids=[0])
    return r.results[0]["out_x"]
```
